# Optimizing a Trainium2 kernel written in Bass

```python
import math
import jax, jax.numpy as jnp
from jax import lax
import numpy as np

D_MODEL = 1024
BATCH = 1
SEQ = 512
DEPTH = 1

HEAD_DIM = 64
ATTN_SCALE = HEAD_DIM ** -0.5
NSA_HEADS = 8
NSA_KV = 2
NSA_REP = NSA_HEADS // NSA_KV
NSA_WIDTH = NSA_HEADS * HEAD_DIM
CMP_LEN = 32
CMP_STRIDE = 16
CMP_HIDDEN = 256
SEL_LEN = 64
SEL_TOPN = 8
NSA_WINDOW = 512
SWA_HEADS = 8
SWA_KV = 2
SWA_REP = SWA_HEADS // SWA_KV
SWA_WIDTH = SWA_HEADS * HEAD_DIM
SWA_WINDOW = 128
Q_BLOCK = 128
D_FF = 2816
FFN_RES = 0.5
RMS_EPS = 1e-6
NEG_INF = -1e30
SEL_BONUS = 1e4
IN_SIZES = (NSA_WIDTH, 2 * NSA_KV * HEAD_DIM, 2 * NSA_KV * HEAD_DIM, 2 * NSA_KV * HEAD_DIM,
            3 * NSA_HEADS, SWA_WIDTH, 2 * SWA_KV * HEAD_DIM, 2 * D_MODEL)
IN_WIDTH = NSA_WIDTH + 6 * NSA_KV * HEAD_DIM + 3 * NSA_HEADS + SWA_WIDTH + 2 * SWA_KV * HEAD_DIM + 2 * D_MODEL

kernel_name = "hybrid_nsa_swa_sink_macaron_adaln"

def alibi_slopes(n):
    return np.array([2.0 ** (-8.0 * (h + 1) / n) for h in range(n)], dtype=np.float32)

def rms_norm(x, g):
    xf = x.astype(jnp.float32)
    y = xf * lax.rsqrt(jnp.mean(xf * xf, axis=-1, keepdims=True) + RMS_EPS)
    return y.astype(x.dtype) * g

def modulate(h, g, shift, scale):
    return rms_norm(h, g) * (1.0 + scale[:, None, :]) + shift[:, None, :]

def swiglu(u, wg, wu, wd):
    return (jax.nn.silu(u @ wg) * (u @ wu)) @ wd

def split_cols(a, sizes):
    outs, off = [], 0
    for n in sizes:
        outs.append(a[..., off:off + n])
        off += n
    return outs

def split_kv(a, groups):
    B, S, _ = a.shape
    a = a.reshape(B, S, 2, groups, HEAD_DIM)
    return a[:, :, 0], a[:, :, 1]

def banded_attention(q, k, v, slopes, window, sinks=None):
    B, S, KH, R, dh = q.shape
    nb = S // Q_BLOCK
    pad = -(-window // Q_BLOCK) * Q_BLOCK
    span = pad + Q_BLOCK
    kp = jnp.pad(k, ((0, 0), (pad, 0), (0, 0), (0, 0)))
    vp = jnp.pad(v, ((0, 0), (pad, 0), (0, 0), (0, 0)))
    qb = jnp.moveaxis(q.reshape(B, nb, Q_BLOCK, KH, R, dh), 1, 0)
    sl = jnp.asarray(slopes)[:, :, None, None]

    def one(args):
        b, qblk = args
        start = b * Q_BLOCK
        kblk = lax.dynamic_slice_in_dim(kp, start, span, axis=1)
        vblk = lax.dynamic_slice_in_dim(vp, start, span, axis=1)
        q_pos = start + jnp.arange(Q_BLOCK)
        k_pos = start - pad + jnp.arange(span)
        dist = q_pos[:, None] - k_pos[None, :]
        valid = (dist >= 0) & (dist < window) & (k_pos[None, :] >= 0)
        s = jnp.einsum('bqkrd,bskd->bkrqs', qblk, kblk).astype(jnp.float32) * ATTN_SCALE
        s = s - sl * dist.astype(jnp.float32)
        s = jnp.where(valid, s, NEG_INF)
        if sinks is not None:
            sink = jnp.broadcast_to(sinks.astype(jnp.float32)[None, :, :, None, None], (B, KH, R, Q_BLOCK, 1))
            p = jax.nn.softmax(jnp.concatenate([s, sink], axis=-1), axis=-1)[..., :-1]
        else:
            p = jax.nn.softmax(s, axis=-1)
        return jnp.einsum('bkrqs,bskd->bqkrd', p.astype(v.dtype), vblk)

    o = lax.map(one, (jnp.arange(nb), qb))
    return jnp.moveaxis(o, 0, 1).reshape(B, S, KH, R, dh)

def nsa_compress(kraw, pos, w1, w2):
    S = kraw.shape[1]
    nc = (S - CMP_LEN) // CMP_STRIDE + 1
    idx = np.arange(nc)[:, None] * CMP_STRIDE + np.arange(CMP_LEN)[None, :]
    blocks = kraw[:, idx] + pos[None, None, :, None, :]
    h = jax.nn.gelu(jnp.einsum('bnlgd,ldh->bngh', blocks, w1))
    return jnp.einsum('bngh,hd->bngd', h, w2)

def selected_attention(q, k, v, idx, slopes):
    B, S, G, R, dh = q.shape
    n = idx.shape[-1]
    nqb = S // SEL_LEN
    qb = jnp.moveaxis(q.reshape(B, nqb, SEL_LEN, G, R, dh), 1, 0)
    ib = jnp.moveaxis(idx.reshape(B, nqb, SEL_LEN, G, n), 1, 0)
    bi = jnp.arange(B)[:, None, None, None]
    gi = jnp.arange(G)[None, None, :, None]
    offs = jnp.arange(SEL_LEN)
    sl = jnp.asarray(slopes)[None, None, :, :, None]

    def one(args):
        b, qblk, iblk = args
        t = b * SEL_LEN + jnp.arange(SEL_LEN)
        tok = (iblk[..., None] * SEL_LEN + offs).reshape(B, SEL_LEN, G, n * SEL_LEN)
        ks = k[bi, tok, gi]
        vs = v[bi, tok, gi]
        dist = (t[None, :, None, None] - tok)[:, :, :, None, :]
        s = jnp.einsum('bqgrd,bqgsd->bqgrs', qblk, ks).astype(jnp.float32) * ATTN_SCALE
        s = s - sl * dist.astype(jnp.float32)
        s = jnp.where(dist >= 0, s, NEG_INF)
        p = jax.nn.softmax(s, axis=-1)
        return jnp.einsum('bqgrs,bqgsd->bqgrd', p.astype(v.dtype), vs)

    o = lax.map(one, (jnp.arange(nqb), qb, ib))
    return jnp.moveaxis(o, 0, 1).reshape(B, S, G, R, dh)

def nsa_attention(q, kv_c, kv_s, kv_w, gates, pos_k, w1_k, w2_k, pos_v, w1_v, w2_v):
    B, S = q.shape[0], q.shape[1]
    q = q.reshape(B, S, NSA_KV, NSA_REP, HEAD_DIM)
    slopes = alibi_slopes(NSA_HEADS).reshape(NSA_KV, NSA_REP)
    kc_raw, vc_raw = split_kv(kv_c, NSA_KV)
    k_s, v_s = split_kv(kv_s, NSA_KV)
    k_w, v_w = split_kv(kv_w, NSA_KV)
    kc = nsa_compress(kc_raw, pos_k, w1_k, w2_k)
    vc = nsa_compress(vc_raw, pos_v, w1_v, w2_v)
    nc = kc.shape[1]
    t = np.arange(S)
    cmp_start = np.arange(nc) * CMP_STRIDE
    dist_c = t[:, None] - (cmp_start + CMP_LEN - 1)[None, :]
    pen_c = (slopes[:, :, None, None] * dist_c[None, None]).astype(np.float32)
    s = jnp.einsum('bsgrd,bngd->bgrsn', q, kc).astype(jnp.float32) * ATTN_SCALE - pen_c
    p_cmp = jax.nn.softmax(jnp.where(dist_c >= 0, s, NEG_INF), axis=-1)
    p_cmp = jnp.where((t >= CMP_LEN - 1)[:, None], p_cmp, 0.0)
    o_cmp = jnp.einsum('bgrsn,bngd->bsgrd', p_cmp.astype(vc.dtype), vc)
    nsel = S // SEL_LEN
    n_top = min(SEL_TOPN, nsel)
    sel_start = np.arange(nsel) * SEL_LEN
    overlap = ((cmp_start[:, None] < sel_start[None, :] + SEL_LEN)
               & (cmp_start[:, None] + CMP_LEN > sel_start[None, :])).astype(np.float32)
    imp = jnp.einsum('bgrsn,nj->bsgj', p_cmp, overlap)
    cur = t // SEL_LEN
    jj = np.arange(nsel)
    valid_sel = (sel_start[None, :] <= t[:, None])[:, None, :]
    forced = ((jj[None, :] == 0) | (jj[None, :] == cur[:, None]) | (jj[None, :] == cur[:, None] - 1))[:, None, :]
    score = jnp.where(forced, SEL_BONUS, jnp.where(valid_sel, imp, -1.0))
    _, idx = lax.top_k(score, n_top)
    o_slc = selected_attention(q, k_s, v_s, idx, slopes)
    o_win = banded_attention(q, k_w, v_w, slopes, NSA_WINDOW)
    g = jax.nn.sigmoid(gates.reshape(B, S, NSA_KV, NSA_REP, 3))
    o = g[..., 0:1] * o_cmp + g[..., 1:2] * o_slc + g[..., 2:3] * o_win
    return o.reshape(B, S, NSA_WIDTH)

def swa_sink_attention(q, kv, sinks):
    B, S = q.shape[0], q.shape[1]
    q = q.reshape(B, S, SWA_KV, SWA_REP, HEAD_DIM)
    k, v = split_kv(kv, SWA_KV)
    slopes = alibi_slopes(SWA_HEADS).reshape(SWA_KV, SWA_REP)
    o = banded_attention(q, k, v, slopes, SWA_WINDOW, sinks=sinks)
    return o.reshape(B, S, SWA_WIDTH)

def hybrid_mixer(u, w_in, cmp_pos_k, cmp_w1_k, cmp_w2_k, cmp_pos_v, cmp_w1_v, cmp_w2_v,
                 sinks, w_up_a, w_up_b, w_out):
    proj = u @ w_in
    q_n, kv_c, kv_s, kv_w, g_n, q_s, kv_b, g_m = split_cols(proj, IN_SIZES)
    y_a = nsa_attention(q_n, kv_c, kv_s, kv_w, g_n, cmp_pos_k, cmp_w1_k, cmp_w2_k,
                        cmp_pos_v, cmp_w1_v, cmp_w2_v)
    y_b = swa_sink_attention(q_s, kv_b, sinks)
    gate_a, gate_b = g_m[..., :D_MODEL], g_m[..., D_MODEL:]
    merged = jax.nn.sigmoid(gate_a) * (y_a @ w_up_a) + jax.nn.sigmoid(gate_b) * (y_b @ w_up_b)
    return merged @ w_out

def setup_inputs(seed: int = 0) -> dict:
    key = jax.random.key(seed)
    ks = jax.random.split(key, 25)
    L, D = DEPTH, D_MODEL

    def nrm(k, shape, scale):
        return jax.random.normal(k, shape, jnp.float32) * scale

    return {
        "x": nrm(ks[0], (BATCH, SEQ, D), 1.0),
        "c": nrm(ks[1], (BATCH, D), 1.0),
        "w_ada": nrm(ks[2], (L, D, 9 * D), D ** -0.5),
        "b_ada": nrm(ks[3], (L, 9 * D), 0.01),
        "g_ffn1": 1.0 + nrm(ks[4], (L, D), 0.02),
        "w1_gate": nrm(ks[5], (L, D, D_FF), D ** -0.5),
        "w1_up": nrm(ks[6], (L, D, D_FF), D ** -0.5),
        "w1_down": nrm(ks[7], (L, D_FF, D), D_FF ** -0.5),
        "g_mix": 1.0 + nrm(ks[8], (L, D), 0.02),
        "w_in": nrm(ks[9], (L, D, IN_WIDTH), D ** -0.5),
        "cmp_pos_k": nrm(ks[10], (L, CMP_LEN, HEAD_DIM), 0.1),
        "cmp_w1_k": nrm(ks[11], (L, CMP_LEN, HEAD_DIM, CMP_HIDDEN), (CMP_LEN * HEAD_DIM) ** -0.5),
        "cmp_w2_k": nrm(ks[12], (L, CMP_HIDDEN, HEAD_DIM), CMP_HIDDEN ** -0.5),
        "cmp_pos_v": nrm(ks[13], (L, CMP_LEN, HEAD_DIM), 0.1),
        "cmp_w1_v": nrm(ks[14], (L, CMP_LEN, HEAD_DIM, CMP_HIDDEN), (CMP_LEN * HEAD_DIM) ** -0.5),
        "cmp_w2_v": nrm(ks[15], (L, CMP_HIDDEN, HEAD_DIM), CMP_HIDDEN ** -0.5),
        "sinks": nrm(ks[16], (L, SWA_KV, SWA_REP), 1.0),
        "w_up_a": nrm(ks[17], (L, NSA_WIDTH, D), NSA_WIDTH ** -0.5),
        "w_up_b": nrm(ks[18], (L, SWA_WIDTH, D), SWA_WIDTH ** -0.5),
        "w_out": nrm(ks[19], (L, D, D), D ** -0.5),
        "g_ffn2": 1.0 + nrm(ks[20], (L, D), 0.02),
        "w2_gate": nrm(ks[21], (L, D, D_FF), D ** -0.5),
        "w2_up": nrm(ks[22], (L, D, D_FF), D ** -0.5),
        "w2_down": nrm(ks[23], (L, D_FF, D), D_FF ** -0.5),
        "g_final": 1.0 + nrm(ks[24], (D,), 0.02),
    }

def reference(x, c, w_ada, b_ada, g_ffn1, w1_gate, w1_up, w1_down, g_mix, w_in,
              cmp_pos_k, cmp_w1_k, cmp_w2_k, cmp_pos_v, cmp_w1_v, cmp_w2_v, sinks,
              w_up_a, w_up_b, w_out, g_ffn2, w2_gate, w2_up, w2_down, g_final):
    h = x
    for l in range(DEPTH):
        mod = jax.nn.silu(c) @ w_ada[l] + b_ada[l]
        sh1, sc1, gt1, sh2, sc2, gt2, sh3, sc3, gt3 = jnp.split(mod, 9, axis=-1)
        u = modulate(h, g_ffn1[l], sh1, sc1)
        h = h + FFN_RES * gt1[:, None, :] * swiglu(u, w1_gate[l], w1_up[l], w1_down[l])
        u = modulate(h, g_mix[l], sh2, sc2)
        y = hybrid_mixer(u, w_in[l], cmp_pos_k[l], cmp_w1_k[l], cmp_w2_k[l], cmp_pos_v[l],
                         cmp_w1_v[l], cmp_w2_v[l], sinks[l], w_up_a[l], w_up_b[l], w_out[l])
        h = h + gt2[:, None, :] * y
        u = modulate(h, g_ffn2[l], sh3, sc3)
        h = h + FFN_RES * gt3[:, None, :] * swiglu(u, w2_gate[l], w2_up[l], w2_down[l])
    return rms_norm(h, g_final)


_drawn_inputs = setup_inputs


def setup_inputs(seed=0):
    import zlib

    import numpy as np

    out = dict(_drawn_inputs(seed))
    spreads = {}
    factors = {'b_ada': 4.536,
     'g_ffn1': 6.8,
     'g_mix': 7.871,
     'cmp_pos_k': 8.0,
     'cmp_pos_v': 33.032,
     'g_ffn2': 7.691,
     'g_final': 8.091,
     'sinks': 8.0}
    for name, (base, spread) in spreads.items():
        noise = np.random.default_rng([zlib.crc32(name.encode()), seed]).standard_normal(out[name].shape)
        drawn = base * np.exp(spread * noise) if base else spread * noise
        out[name] = __import__('jax').numpy.asarray(drawn.astype(out[name].dtype))
    for name, factor in factors.items():
        out[name] = (out[name] * factor).astype(out[name].dtype)
    return out
```

```python
import math
from contextlib import ExitStack

import numpy as np

import concourse.bass as bass
from concourse import mybir

F32 = mybir.dt.float32
F32R = mybir.dt.float32r
I32 = mybir.dt.int32
ALU = mybir.AluOpType
ACT = mybir.ActivationFunctionType
AX = mybir.AxisListType

P = 128
D = 1024
DT = D // P
T = 512
QT = T // P
FF = 2816
FT = FF // P
GROUPS = FT // 2
DH = 64
HEADS = 8
KV = 2
REP = HEADS // KV
CMP_LEN, CMP_STRIDE = 32, 16
NC_BLOCKS = (T - CMP_LEN) // CMP_STRIDE + 1
NCP = NC_BLOCKS + 1
HID_C = 256
RMS_EPS = 1e-6
MASKED = -1e30
SCALE = DH ** -0.5
SLOPES = [2.0 ** (-8.0 * (h + 1) / HEADS) for h in range(HEADS)]

TILES_IN = ["qs0", "qs1", "qs2", "qs3", "kb", "vb", "qn0", "qn1", "qn2", "qn3",
            "kc", "vc", "ks", "vs", "kw", "vw", "gn"]
N_IRREG = len(TILES_IN)
N_GATES = 16
C_ID, C_MSK, C_MCA, C_MCC = 0, 128, 640, 768
C_END = C_MCC + T
M_UP, M_U, M_L, M_LP = range(4)
V_BADA, V_G, V_C, V_END = 0, 72, 104, 112
AUG0 = 64
AUG_ROWS = 35
BRANCHES = ("cmp", "win", "slc", "swa")
A_KPOS, A_CPOS, A_IND, A_SLOPE = 0, T, T + NCP, T + NCP + 4
A_END = A_SLOPE + HEADS
ROW_M = {"cmp": 96, "win": 97, "slc": 98, "swa": 96}


class Record:
    pass


def counter():
    n = [0]

    def step(by=1):
        n[0] += by
        return n[0]
    step.now = lambda: n[0]
    return step


def split_terms(hi_a, lo_a, hi_b, lo_b):
    return ((hi_a, hi_b), (hi_a, lo_b), (lo_a, hi_b))


def build(nc, a):
    with ExitStack() as ctx:
        k = Record()
        k.nc, k.a = nc, a
        base = -(-nc.sbuf_base // 64) * 64
        X = 56 * 1024

        def at(name, shape, dt, off):
            return nc.alloc_sbuf_tensor_at(name, shape, dt, offset=base + int(off))
        sems = {}

        def sem(name):
            if name not in sems:
                sems[name] = nc.alloc_semaphore(name)
            return sems[name]

        def clear_semaphores():
            nc.clear_and_free_semaphores(list(sems.values()))
            nc.all_engine_barrier()
            sems.clear()
        k.at, k.sem, k.X = at, sem, X
        k.bank = [ctx.enter_context(nc.psum_tensor(f"bank{i}", [P, 512], F32)) for i in range(8)]
        K = 1024
        k.hT = at("hT", [P, DT, T], F32, 0)
        k.uh = at("u_hi", [P, DT, T], F32R, 16 * K)
        k.ul = at("u_lo", [P, DT, T], F32R, 32 * K)
        c0 = 48 * K
        k.vec = at("vec", [P, V_END], F32, c0)
        k.mod = at("mod", [P, 72], F32, c0 + 512)
        k.gain = at("gain", [P, 3, DT], F32, c0 + 1024)
        k.gate = at("gate", [P, 3, DT], F32, c0 + 1024 + 128)
        k.csil = at("csil", [P, DT], F32, c0 + 1280)
        k.stat = at("stat", [P, 4, QT], F32, c0 + 1344)
        k.rstd = at("rstd", [P, QT], F32, c0 + 1408)
        k.ones = at("ones", [P, 1], F32, c0 + 1472)
        k.idF = at("identF", [P, P], F32, c0 + 1536)
        k.idR = at("identR", [P, P], F32R, c0 + 2048)
        k.msk = at("masks", [P, 4, P], F32R, c0 + 2560)
        k.mca = at("mask_cA", [P, QT, NCP], F32R, c0 + 4608)
        k.mcc = at("mask_cC", [P, T], F32R, c0 + 5120)
        k.hT_spill = nc.dram_tensor("h_spill", (D, T), F32, kind="Internal").ap()
        k.fac = nc.dram_tensor("factors", (4, HEADS * T), F32, kind="Internal").ap()

        ffn1 = ffn_buffers(k, "f1", a.gu1, a.dn1)
        startup_and_ffn1(k, ffn1)
        m = mixer_buffers(k)
        projections(k, m)
        merge(k, m, attention(k, m))
        clear_semaphores()
        ffn2 = ffn_buffers(k, "f2", a.gu2, a.dn2)
        ffn2_and_output(k, ffn2)


def norm_buffers(k, n, off_sq, off, banks=(4, 5)):
    s, at = Record(), k.at
    s.sq = at(f"sq{n}", [P, 4, T], F32, off_sq)
    s.xn = at(f"xn{n}", [P, 3, T], F32, off)
    s.u32 = at(f"u32_{n}", [P, 3, T], F32, off + 6144)
    s.s_h, s.s_sq, s.s_sqmm = k.sem(f"n{n}_h"), k.sem(f"n{n}_sq"), k.sem(f"n{n}_sqmm")
    s.s_chain, s.s_rstd, s.s_bc = k.sem(f"n{n}_chain"), k.sem(f"n{n}_rstd"), k.sem(f"n{n}_bc")
    s.s_xn, s.s_u32, s.s_uh = k.sem(f"n{n}_xn"), k.sem(f"n{n}_u32"), k.sem(f"n{n}_uh")
    s.s_ul = k.sem(f"n{n}_ul")
    s.ss = k.bank[banks[0]]
    s.bc = k.bank[banks[1]]
    return s


def norm_scalar_squares(k, s, act, s_ready=None, before=0):
    for t in range(DT):
        if s_ready is not None:
            act.wait_ge(s_ready, before + t + 1)
        if t >= 4:
            act.wait_ge(s.s_sqmm, t - 3)
        k.nc.scalar.activation(s.sq[:, t % 4], k.hT[:, t], ACT.Square).then_inc(s.s_sq, 1)


def norm_tensor_sums(k, s, pe):
    for t in range(DT):
        pe.wait_ge(s.s_sq, t + 1)
        for q in range(QT):
            mm = k.nc.tensor.matmul(s.ss[:, q:q + 1], s.sq[:, t % 4, q * P:(q + 1) * P], k.ones[:, :],
                                    start=(t == 0 and q == 0), stop=(t == DT - 1), skip_group_check=True)
        mm.then_inc(s.s_sqmm, 1)
    pe.wait_ge(s.s_rstd, 1)
    for q in range(QT):
        mm = k.nc.tensor.matmul(s.bc[:, q * P:(q + 1) * P], k.rstd[:, q:q + 1].to_broadcast([P, P]), k.idF[:, :],
                                start=True, stop=True)
    mm.then_inc(s.s_bc, 1)


def norm_vector_rstd(k, s, dve):
    v, i, half, y = (k.stat[:, j] for j in range(4))
    V = k.nc.vector
    n = counter()

    def then(ins):
        ins.then_inc(s.s_chain, 1)
        dve.wait_ge(s.s_chain, n())
    dve.wait_ge(s.s_sqmm, DT)
    then(V.tensor_scalar(v, s.ss[:, 0:QT], 1.0 / D, RMS_EPS, ALU.mult, ALU.add))
    then(V.tensor_scalar(i.bitcast(I32), v.bitcast(I32), 1, None, ALU.arith_shift_right))
    then(V.tensor_scalar(y.bitcast(I32), i.bitcast(I32), -1.0, float(0x5F3759DF), ALU.mult, ALU.add))
    for _ in range(4):
        then(V.tensor_tensor(half, y, y, ALU.mult))
        then(V.tensor_tensor(half, half, v, ALU.mult))
        then(V.tensor_scalar(half, half, -0.5, 1.5, ALU.mult, ALU.add))
        then(V.tensor_tensor(y, y, half, ALU.mult))
    V.tensor_copy(k.rstd[:, :], y).then_inc(s.s_rstd, 1)


def norm_vector_modulate(k, s, dve, A, B):
    V = k.nc.vector
    dve.wait_ge(s.s_bc, 1)

    def low(t):
        dve.wait_ge(s.s_uh, t + 1)
        dve.wait_ge(s.s_u32, t + 1)
        V.tensor_tensor(k.ul[:, t], s.u32[:, t % 3], k.uh[:, t].bitcast(F32), ALU.subtract).then_inc(s.s_ul, 1)
    for t in range(DT):
        if t >= 3:
            dve.wait_ge(s.s_uh, t - 2)
        V.tensor_tensor(s.xn[:, t % 3], k.hT[:, t], s.bc[:, :], ALU.mult).then_inc(s.s_xn, 1)
        if t >= 1:
            low(t - 1)
        dve.wait_ge(s.s_xn, t + 1)
        V.tensor_scalar(s.u32[:, t % 3], s.xn[:, t % 3], A[:, t:t + 1], B[:, t:t + 1], ALU.mult,
                        ALU.add).then_inc(s.s_u32, 1)
    low(DT - 1)


def norm_scalar_modulate(k, s, act, A, B):
    for t in range(DT):
        act.wait_ge(s.s_xn, t + 1)
        k.nc.scalar.activation(k.uh[:, t], s.xn[:, t % 3], ACT.Identity, bias=B[:, t:t + 1],
                               scale=A[:, t:t + 1]).then_inc(s.s_uh, 1)


def ffn_buffers(k, p, gu, dn):
    f, at, X = Record(), k.at, k.X
    K = 1024
    f.gu, f.dn = gu, dn.rearrange("(f p) n -> f p n", p=P)
    f.rgu = at(p + "_raw_gu", [P, 2, 2, DT, P], F32, X)
    f.rdn = at(p + "_raw_dn", [P, 2, D], F32, X + 16 * K)
    f.guh = at(p + "_gu_hi", [P, 2, 2, DT, P], F32R, X + 24 * K)
    f.gul = at(p + "_gu_lo", [P, 2, 2, DT, P], F32R, X + 40 * K)
    f.dnh = at(p + "_dn_hi", [P, 2, D], F32R, X + 56 * K)
    f.dnl = at(p + "_dn_lo", [P, 2, D], F32R, X + 64 * K)
    f.hidh = at(p + "_hid_hi", [P, 4, T], F32R, X + 72 * K)
    f.hidl = at(p + "_hid_lo", [P, 4, T], F32R, X + 80 * K)
    f.sil = at(p + "_sil", [P, 2, T], F32, X + 88 * K)
    f.hid = at(p + "_hid", [P, 2, T], F32, X + 92 * K)

    def pair(name):
        return [k.sem(f"{p}_{name}{s}") for s in range(2)]
    f.s_raw_gu, f.s_raw_dn, f.s_gu_hi = pair("raw_gu_"), pair("raw_dn_"), pair("gu_hi_")
    f.s_gu_lo, f.s_gate, f.s_up = pair("gu_lo_"), pair("gate_"), pair("up_")
    f.s_sil, f.s_hid, f.s_hid_hi = pair("sil_"), pair("hid_"), pair("hid_hi_")
    f.s_hid_lo = pair("hid_lo_")
    f.s_dn_hi, f.s_dn_lo = k.sem(p + "_dn_hi"), k.sem(p + "_dn_lo")
    f.s_dn_mm, f.s_bank = k.sem(p + "_dn_mm"), k.sem(p + "_dn_bank_free")
    f.gb, f.ub, f.db = k.bank[0:2], k.bank[2:4], k.bank[4:8]
    return f


def ffn_load_gu(k, f, sp, g, s):
    sp.dma_start(f.rgu[:, s], f.gu[g * 2 + s]).then_inc(f.s_raw_gu[s], 16)


def ffn_load_dn(k, f, sp, g, s):
    sp.dma_start(f.rdn[:, s], f.dn[g * 2 + s]).then_inc(f.s_raw_dn[s], 16)


def ffn_sync_gu(k, f, sp, g):
    for s in range(2):
        sp.wait_ge(f.s_gu_lo[s], g)
        ffn_load_gu(k, f, sp, g, s)


def ffn_sync_dn(k, f, sp, g):
    for s in range(2):
        sp.wait_ge(f.s_dn_lo, g * 2 - 1 + s)
        ffn_load_dn(k, f, sp, g, s)


def ffn_scalar_gu_hi(k, f, act, g, s):
    act.wait_ge(f.s_raw_gu[s], (g + 1) * 16)
    k.nc.scalar.activation(f.guh[:, s], f.rgu[:, s], ACT.Copy).then_inc(f.s_gu_hi[s], 1)


def ffn_vector_gu_lo(k, f, dve, g, s):
    dve.wait_ge(f.s_gu_hi[s], g + 1)
    k.nc.vector.tensor_tensor(f.gul[:, s], f.rgu[:, s], f.guh[:, s].bitcast(F32),
                              ALU.subtract).then_inc(f.s_gu_lo[s], 1)


def ffn_scalar_dn_hi(k, f, act, g):
    for s in range(2):
        act.wait_ge(f.s_raw_dn[s], (g + 1) * 16)
        k.nc.scalar.activation(f.dnh[:, s], f.rdn[:, s], ACT.Copy).then_inc(f.s_dn_hi, 1)


def ffn_vector_dn_lo(k, f, dve, g):
    for s in range(2):
        dve.wait_ge(f.s_dn_hi, g * 2 + 1 + s)
        k.nc.vector.tensor_tensor(f.dnl[:, s], f.rdn[:, s], f.dnh[:, s].bitcast(F32),
                                  ALU.subtract).then_inc(f.s_dn_lo, 1)


def ffn_scalar_group(k, f, act, g, q, first=False, last=False):
    A = k.nc.scalar
    for s in range(2):
        act.wait_ge(f.s_gate[s], g + 1)
        if not first:
            act.wait_ge(f.s_hid[s], g)
        A.activation(f.sil[:, s], f.gb[s][:, :], ACT.Silu).then_inc(f.s_sil[s], 1)
        if s == 0 and not first:
            ffn_scalar_dn_hi(k, f, act, g - 1)
        if not last:
            act.wait_ge(f.s_up[s], g + 1)
            ffn_scalar_gu_hi(k, f, act, g + 1, s)
        act.wait_ge(f.s_hid[s], g + 1)
        A.activation(f.hidh[:, q * 2 + s], f.hid[:, s], ACT.Copy).then_inc(f.s_hid_hi[s], 1)


def ffn_vector_hidden(k, f, dve, g, q, s, split_next):
    V = k.nc.vector
    dve.wait_ge(f.s_sil[s], g + 1)
    dve.wait_ge(f.s_up[s], g + 1)
    V.tensor_tensor(f.hid[:, s], f.sil[:, s], f.ub[s][:, :], ALU.mult).then_inc(f.s_hid[s], 1)
    if split_next:
        ffn_vector_gu_lo(k, f, dve, g + 1, s)
    dve.wait_ge(f.s_hid_hi[s], g + 1)
    V.tensor_tensor(f.hidl[:, q * 2 + s], f.hid[:, s], f.hidh[:, q * 2 + s].bitcast(F32),
                    ALU.subtract).then_inc(f.s_hid_lo[s], 1)


def ffn_vector_down(k, f, dve, g, gate, tiles=range(DT)):
    for m in tiles:
        dve.wait_ge(f.s_dn_mm, g * 8 + m + 1)
        k.nc.vector.scalar_tensor_tensor(k.hT[:, m], f.db[m % 4][:, :], gate[:, m:m + 1], k.hT[:, m],
                                         ALU.mult, ALU.add).then_inc(f.s_bank, 1)


def ffn_tensor_gate_up(k, f, pe, g, s, first, s_u=None):
    for half, (bank, s_read, s_done) in enumerate(((f.gb[s], f.s_sil[s], f.s_gate[s]),
                                                   (f.ub[s], f.s_hid[s], f.s_up[s]))):
        if half == 0:
            pe.wait_ge(f.s_gu_lo[s], g + 1)
        if not first:
            pe.wait_ge(s_read, g)
        for kt in range(DT):
            if s_u is not None and half == 0:
                pe.wait_ge(s_u, kt + 1)
            for j, (w, x) in enumerate(split_terms(f.guh[:, s, half, kt], f.gul[:, s, half, kt],
                                                   k.uh[:, kt], k.ul[:, kt])):
                mm = k.nc.tensor.matmul(bank[:, :], w, x, start=(kt == 0 and j == 0),
                                        stop=(kt == DT - 1 and j == 2))
        mm.then_inc(s_done, 1)


def ffn_tensor_down(k, f, pe, g, q):
    pe.wait_ge(f.s_dn_lo, g * 2 + 2)
    for s in range(2):
        pe.wait_ge(f.s_hid_lo[s], g + 1)
    for m in range(DT):
        pe.wait_ge(f.s_bank, g * 8 + m + 1)
        for s in range(2):
            w = slice(m * P, (m + 1) * P)
            for j, (x, y) in enumerate(split_terms(f.dnh[:, s, w], f.dnl[:, s, w],
                                                   f.hidh[:, q * 2 + s], f.hidl[:, q * 2 + s])):
                mm = k.nc.tensor.matmul(f.db[m % 4][:, :], x, y, start=(s == 0 and j == 0),
                                        stop=(s == 1 and j == 2))
        mm.then_inc(f.s_dn_mm, 1)


def startup_and_ffn1(k, f):
    nc, a, X, K = k.nc, k.a, k.X, 1024
    n = norm_buffers(k, 1, X + 88 * K, X + 61 * K)
    acc2 = k.at("ada_acc2", [P, 6 * D], F32, X + 96 * K)
    ring = k.at("ada_ring", [P, 4, 1536], F32, X + 120 * K)
    accg = k.at("ada_acc_gt1", [P, D], F32, X + 144 * K)
    acc1 = k.at("ada_acc1", [P, 2, D], F32, X + 80 * K)
    stage = k.at("const_stage", [P, C_END], F32, X + 56 * K)
    w_ada = a.w_ada.rearrange("(k p) n -> k p n", p=P)
    S = k.sem
    s_vec, s_const, s_acc = S("vec_in"), S("const_in"), S("ada_acc")
    s_raw = [S(f"ada_raw{j}") for j in range(4)]
    s_used = [S(f"ada_used{j}") for j in range(4)]
    s_csil, s_fill, s_ones, s_idf = S("csil"), S("ada_zero"), S("ones"), S("identF_ready")
    s_mm1, s_mmg, s_mm2 = S("ada_mm1"), S("ada_mmg"), S("ada_mm2")
    s_mod, s_mod2 = S("mod1"), S("mod2_read")
    s_const_ready = S("const_ready")
    pieces = [(kt, c) for kt in range(DT) for c in (0, 1)] + [(kt, 2) for kt in range(DT)]

    with nc.Block() as block:
        @block.sync
        def _(sp):
            sp.dma_start(k.vec[:, :], a.vec).then_inc(s_vec, 16)
            for i, (kt, c) in enumerate(pieces):
                if i == 16:
                    for s in range(2):
                        ffn_load_gu(k, f, sp, 0, s)
                j = i % 4
                if i >= 4:
                    sp.wait_ge(s_used[j], i // 4)
                sp.dma_start(ring[:, j, 0:D], w_ada[kt, :, c * D:(c + 1) * D]).then_inc(s_raw[j], 16)
            for s in range(2):
                ffn_load_dn(k, f, sp, 0, s)

            ffn_sync_gu(k, f, sp, 1)

            def group(g):
                ffn_sync_gu(k, f, sp, g + 1)
                for j in range(4):
                    sp.wait_ge(s_used[j], g + 5)
                    sp.dma_start(ring[:, j], w_ada[g - 1, :, 3 * D + j * 1536:3 * D + (j + 1) * 1536])\
                        .then_inc(s_raw[j], 16)
                ffn_sync_dn(k, f, sp, g)
            with sp.Fori(0, 4) as it:
                group(it * 2 + 1)
                group(it * 2 + 2)
            ffn_sync_gu(k, f, sp, 10)
            ffn_sync_dn(k, f, sp, 9)
            ffn_sync_dn(k, f, sp, 10)

        @block.gpsimd
        def _(pool):
            nc.gpsimd.memset(k.ones[:, :], 1.0).then_inc(s_ones, 1)
            nc.gpsimd.memset(acc2[:, :], 0.0).then_inc(s_fill, 1)

        @block.scalar
        def _(act):
            act.dma_start(stage[:, :], a.const).then_inc(s_const, 16)
            act.dma_start(k.hT[:, :, :], a.xT.rearrange("(t p) n -> p t n", p=P)).then_inc(n.s_h, 16)
            act.wait_ge(s_vec, 16)
            nc.scalar.activation(k.csil[:, :], k.vec[:, V_C:V_END], ACT.Silu).then_inc(s_csil, 1)
            act.wait_ge(n.s_h, 16)
            norm_scalar_squares(k, n, act)
            act.wait_ge(s_const, 16)
            nc.scalar.activation(k.idR[:, :], stage[:, C_ID:C_ID + P], ACT.Copy)
            nc.scalar.activation(k.msk[:, :, :], stage[:, C_MSK:C_MCA].rearrange("p (m c) -> p m c", c=P), ACT.Copy)
            nc.scalar.activation(k.mca[:, :, :], stage[:, C_MCA:C_MCC].rearrange("p (m c) -> p m c", c=NCP), ACT.Copy)
            nc.scalar.activation(k.mcc[:, :], stage[:, C_MCC:C_END], ACT.Copy).then_inc(s_const_ready, 1)
            act.wait_ge(s_mod, 2)
            norm_scalar_modulate(k, n, act, k.gain[:, 0], k.mod[:, 0:8])
            for s in range(2):
                ffn_scalar_gu_hi(k, f, act, 0, s)
            ffn_scalar_group(k, f, act, 0, 0, first=True)
            with act.Fori(0, 4) as it:
                ffn_scalar_group(k, f, act, it * 2 + 1, 1)
                ffn_scalar_group(k, f, act, it * 2 + 2, 0)
            ffn_scalar_group(k, f, act, 9, 1)
            ffn_scalar_group(k, f, act, 10, 0, last=True)
            act.wait_ge(f.s_dn_mm, 80)
            ffn_scalar_dn_hi(k, f, act, 10)

        @block.vector
        def _(dve):
            V = nc.vector
            dve.wait_ge(s_const, 16)
            V.tensor_copy(k.idF[:, :], stage[:, C_ID:C_ID + P]).then_inc(s_idf, 1)

            def piece(i, kt, c):
                j, acc = i % 4, (accg[:, :] if c == 2 else acc1[:, c])
                dve.wait_ge(s_raw[j], 16 * (i // 4 + 1))
                col = k.csil[:, kt:kt + 1]
                if kt == 0:
                    V.tensor_scalar(acc, ring[:, j, 0:D], col, None, ALU.mult).then_inc(s_used[j], 1)
                else:
                    before = i - (2 if c < 2 else 1)
                    dve.wait_ge(s_used[before % 4], before // 4 + 1)
                    V.scalar_tensor_tensor(acc, ring[:, j, 0:D], col, acc, ALU.mult, ALU.add)\
                        .then_inc(s_used[j], 1)
            dve.wait_ge(s_csil, 1)
            for i in range(16):
                piece(i, *pieces[i])
                if i == 7:
                    norm_vector_rstd(k, n, dve)
            dve.wait_ge(s_mm1, 1)
            V.tensor_tensor(k.mod[:, 0:16], k.bank[6][:, 0:16], k.vec[:, V_BADA:V_BADA + 16], ALU.add)\
                .then_inc(s_mod, 1)
            dve.wait_ge(s_mod, 1)
            V.scalar_tensor_tensor(k.gain[:, 0], k.mod[:, 8:16], 1.0, k.vec[:, V_G:V_G + 8], ALU.add, ALU.mult)\
                .then_inc(s_mod, 1)
            dve.wait_ge(s_mod, 2)
            norm_vector_modulate(k, n, dve, k.gain[:, 0], k.mod[:, 0:8])
            for s in range(2):
                ffn_vector_gu_lo(k, f, dve, 0, s)
            for i in range(16, 24):
                piece(i, *pieces[i])
            for s in range(2):
                ffn_vector_hidden(k, f, dve, 0, 0, s, split_next=True)
            dve.wait_ge(s_mmg, 1)
            V.tensor_tensor(k.mod[:, 16:24], k.bank[7][:, 0:8], k.vec[:, 16:24], ALU.add).then_inc(s_mod, 1)
            dve.wait_ge(s_mod, 3)
            V.tensor_scalar(k.gate[:, 0], k.mod[:, 16:24], 0.5, None, ALU.mult).then_inc(f.s_bank, 4)
            dve.wait_ge(f.s_bank, 4)
            dve.wait_ge(s_fill, 1)

            def group(g, q, ada):
                ffn_vector_dn_lo(k, f, dve, g - 1)
                for s in range(2):
                    ffn_vector_hidden(k, f, dve, g, q, s, split_next=(s == 0))
                    if ada:
                        for j in (2 * s, 2 * s + 1):
                            part = acc2[:, j * 1536:(j + 1) * 1536]
                            dve.wait_ge(s_raw[j], (g + 6) * 16)
                            dve.wait_ge(s_used[j], g + 5)
                            V.scalar_tensor_tensor(part, ring[:, j], k.csil[:, bass.ds(g - 1, 1)], part,
                                                   ALU.mult, ALU.add).then_inc(s_used[j], 1)
                ffn_vector_down(k, f, dve, g - 1, k.gate[:, 0], range(4))
                ffn_vector_gu_lo(k, f, dve, g + 1, 1)
                ffn_vector_down(k, f, dve, g - 1, k.gate[:, 0], range(4, DT))
            with dve.Fori(0, 4) as it:
                group(it * 2 + 1, 1, True)
                group(it * 2 + 2, 0, True)
            group(9, 1, False)
            ffn_vector_dn_lo(k, f, dve, 9)
            ffn_vector_hidden(k, f, dve, 10, 0, 0, False)
            ffn_vector_hidden(k, f, dve, 10, 0, 1, False)
            dve.wait_ge(s_mm2, 1)
            V.tensor_tensor(k.mod[:, 24:72], k.bank[4][:, 0:48], k.vec[:, 24:72], ALU.add).then_inc(s_mod2, 1)
            dve.wait_ge(s_mod2, 1)
            V.scalar_tensor_tensor(k.gain[:, 1], k.mod[:, 32:40], 1.0, k.vec[:, V_G + 8:V_G + 16], ALU.add, ALU.mult)
            V.scalar_tensor_tensor(k.gain[:, 2], k.mod[:, 56:64], 1.0, k.vec[:, V_G + 16:V_G + 24], ALU.add, ALU.mult)
            V.tensor_copy(k.gate[:, 1], k.mod[:, 40:48])
            V.tensor_scalar(k.gate[:, 2], k.mod[:, 64:72], 0.5, None, ALU.mult)
            ffn_vector_down(k, f, dve, 9, k.gate[:, 0])
            ffn_vector_dn_lo(k, f, dve, 10)
            ffn_vector_down(k, f, dve, 10, k.gate[:, 0])

        @block.tensor
        def _(pe):
            pe.wait_ge(s_ones, 1)
            pe.wait_ge(s_idf, 1)
            norm_tensor_sums(k, n, pe)
            pe.wait_ge(s_used[2], 4)
            pe.wait_ge(s_used[3], 4)
            for m in range(16):
                mm = nc.tensor.matmul(k.bank[6][:, m:m + 1], acc1[:, m // 8, (m % 8) * P:(m % 8 + 1) * P], k.ones[:, :],
                                      start=True, stop=True)
            mm.then_inc(s_mm1, 1)
            for s in range(2):
                ffn_tensor_gate_up(k, f, pe, 0, s, True, s_u=n.s_ul if s == 0 else None)
            pe.wait_ge(s_used[3], 6)
            for m in range(8):
                mm = nc.tensor.matmul(k.bank[7][:, m:m + 1], accg[:, m * P:(m + 1) * P], k.ones[:, :],
                                      start=True, stop=True)
            mm.then_inc(s_mmg, 1)

            def group(g, q):
                for s in range(2):
                    ffn_tensor_gate_up(k, f, pe, g, s, False)
                ffn_tensor_down(k, f, pe, g - 1, 1 - q)
            with pe.Fori(0, 4) as it:
                group(it * 2 + 1, 1)
                group(it * 2 + 2, 0)
            group(9, 1)
            for s in range(2):
                ffn_tensor_gate_up(k, f, pe, 10, s, False)
            for j in range(4):
                pe.wait_ge(s_used[j], 14)
            pe.wait_ge(f.s_bank, 4 + 72)
            for m in range(48):
                mm = nc.tensor.matmul(k.bank[4][:, m:m + 1], acc2[:, m * P:(m + 1) * P], k.ones[:, :],
                                      start=True, stop=True)
            mm.then_inc(s_mm2, 1)
            pe.wait_ge(s_mod2, 1)
            ffn_tensor_down(k, f, pe, 9, 1)
            ffn_tensor_down(k, f, pe, 10, 0)


def mixer_buffers(k):
    m, at, X, K = Record(), k.at, k.X, 1024
    m.gates = at("gates", [P, N_GATES, T], F32, X)
    m.qn = at("q_nsa", [P, HEADS, T], F32R, X + 32 * K)
    m.qn2 = at("q_nsa_pair", [P, HEADS, T], F32R, X + 48 * K)
    m.qs = at("q_swa", [P, HEADS, T], F32R, 16 * K)
    m.qs2 = at("q_swa_pair", [P, HEADS, T], F32R, 32 * K)
    m.kk = at("k_rows", [P, 3, KV, T], F32R, X + 64 * K)
    m.kk2 = at("k_pair", [P, 3, KV, T], F32R, X + 76 * K)
    m.vh = at("v_hi", [P, 3, KV, QT, DH + 2], F32R, X + 88 * K)
    m.vl = at("v_lo", [P, 3, KV, QT, DH + 2], F32R, X + 88 * K + 6400)
    m.vT = at("v_T", [P, 2, T], F32, X + 101 * K)
    m.qsf = at("q_swa_f32", [P, 4, T], F32, X + 105 * K)
    c = X + 115 * K
    m.kc = at("kc_rows", [P, KV, NCP], F32R, c)
    m.kc2 = at("kc_pair", [P, KV, NCP], F32R, c + 256)
    m.vch = at("vc_hi", [P, KV, DH + 2], F32R, c + 512)
    m.vcl = at("vc_lo", [P, KV, DH + 2], F32R, c + 1088)
    m.cpos = at("cmp_pos", [P, 2, 16], F32, c + 1664)
    m.gs = at("nsa_gates", [3 * HEADS, T], F32, X + 118 * K)
    m.wh = at("w_hi", [P, 2, D], F32R, X + 120 * K)
    m.wl = at("w_lo", [P, 2, D], F32R, X + 128 * K)
    m.raw = at("w_raw", [P, 3, D], F32, X + 136 * K)
    m.aug = at("aug", [P, A_END], F32, X + 148 * K)
    NB = 16 * KV * NC_BLOCKS
    m.blk = at("blocks", [P, 2, NB], F32, X)
    m.blkh = at("blocks_hi", [P, 2, NB], F32R, X + 8 * K)
    m.blkl = at("blocks_lo", [P, 2, NB], F32R, X + 16 * K)
    g = X + 24 * K
    m.cw2 = at("cmp_w2", [P, 2, 2, DH], F32, g)
    m.cw2h = at("cmp_w2_hi", [P, 2, 2, DH], F32R, g + 1024)
    m.cw2l = at("cmp_w2_lo", [P, 2, 2, DH], F32R, g + 2048)
    m.ge = at("gelu_tmp", [P, 4, 2, KV * NC_BLOCKS], F32, g + 3072)
    m.geh = at("gelu_hi", [P, 2, KV * NC_BLOCKS], F32R, g + 5120)
    m.gel = at("gelu_lo", [P, 2, KV * NC_BLOCKS], F32R, g + 5632)
    return m


def stream_items():
    names = list(TILES_IN)
    at = names.index("vs") + 1
    items = [("in", n) for n in names[:at]] + [("ck", c) for c in range(4)]
    items += [("in", n) for n in names[at:]] + [("cv", c) for c in range(4)]
    return items


def projections(k, m):
    nc, a, X, K = k.nc, k.a, k.X, 1024
    n2 = norm_buffers(k, 2, X, X + 8 * K)
    S = k.sem
    items = stream_items()
    N = len(items)
    kinds = [i[0] if i[0] != "in" else i[1][:2] for i in items]
    win_index = {name: i for i, name in enumerate(TILES_IN)}
    s_raw = [S(f"w_raw{j}") for j in range(3)]
    s_hi, s_lo, s_item = S("w_hi"), S("w_lo"), S("w_item")
    s_act, s_dve = S("evac_act"), S("evac_dve")
    s_cw2 = S("cw2_in")
    s_spill, s_aux, s_fill, s_kv0 = S("h_spilled"), S("aux_in"), S("kv_cleared"), S("rows_set")
    s_vt, s_vta, s_vtd = S("v_transposed"), S("v_hi_done"), S("v_lo_done")
    s_blkh, s_blkl = S("blocks_hi_done"), S("blocks_lo_done")
    s_w2h, s_w2l = S("cw2_hi"), S("cw2_lo")
    s_x, s_th, s_g, s_gh, s_gl = S("gelu_x"), S("gelu_tanh"), S("gelu_g"), S("gelu_hi_done"), S("gelu_lo_done")
    s_c2, s_c2a, s_c2d = S("cmp_out"), S("cmp_hi_done"), S("cmp_lo_done")
    ACT_KINDS = {"qs", "kb", "vb", "qn", "ks", "vs", "kw", "vw", "gn"}
    DVE_KINDS = {"kb", "qn", "kc", "vc", "ks", "kw"}
    act_after = [sum(x in ACT_KINDS for x in kinds[:i + 1]) for i in range(N)]
    dve_after = [sum(x in DVE_KINDS for x in kinds[:i + 1]) for i in range(N)]
    proj_items = [i for i in range(N) if items[i][0] == "in"]
    bank_of = {i: n % 2 for n, i in enumerate(proj_items)}
    bank_before = {i: (proj_items[n - 2] if n >= 2 else None) for n, i in enumerate(proj_items)}
    v_items = [i for i in range(N) if kinds[i] in ("vb", "vs", "vw")]
    v_branch = {"vb": 2, "vs": 1, "vw": 0}
    k_branch = {"kb": 2, "ks": 1, "kw": 0}
    cmp_end = {i: (0 if kinds[i] == "ck" else 1) for i in range(N) if items[i] in (("ck", 3), ("cv", 3))}

    def source(i):
        kind, x = items[i]
        return a.win[win_index[x]] if kind == "in" else a.cw1[x + (4 if kind == "cv" else 0)]

    with nc.Block() as block:
        @block.sync
        def _(sp):
            sp.dma_start(m.aug[AUG0:AUG0 + AUG_ROWS, :], a.aug).then_inc(s_aux, 16)
            sp.dma_start(m.cpos[:, :, :], a.cpos).then_inc(s_aux, 16)
            for i in range(N):
                if i >= 3:
                    sp.wait_ge(s_lo, i - 2)
                sp.dma_start(m.raw[:, i % 3], source(i).rearrange("p k c -> p (k c)")).then_inc(s_raw[i % 3], 16)
                if i == 2:
                    sp.dma_start(k.hT_spill.rearrange("(t p) n -> p t n", p=P), k.hT[:, :, :]).then_inc(s_spill, 16)
                if i == 4:
                    sp.wait_ge(n2.s_ul, DT)
                    sp.dma_start(m.cw2[:, :, :, :], a.cw2).then_inc(s_cw2, 16)
            for j in range(N_GATES):
                sp.wait_ge(s_lo, N + j - 2)
                sp.dma_start(m.raw[:, (N + j) % 3], a.win[N_IRREG + j].rearrange("p k c -> p (k c)"))\
                    .then_inc(s_raw[(N + j) % 3], 16)
            sp.wait_ge(s_spill, 16)

        @block.gpsimd
        def _(pool):
            G = nc.gpsimd
            G.memset(m.vh[:, :, :, :, :].bitcast(F32), 0.0).then_inc(s_fill, 1)
            G.memset(m.vl[:, :, :, :, :].bitcast(F32), 0.0)
            G.memset(m.vch[:, :, :].bitcast(F32), 0.0).then_inc(s_fill, 1)
            G.memset(m.vcl[:, :, :].bitcast(F32), 0.0)
            G.memset(m.kc[:, :, :].bitcast(F32), 0.0)
            G.memset(m.kc2[:, :, :].bitcast(F32), 0.0).then_inc(s_fill, 1)
            pool.wait_ge(s_fill, 2)
            G.memset(m.vh[:, :, :, :, DH:DH + 1].bitcast(F32), 1.0)
            G.memset(m.vch[:, :, DH:DH + 1].bitcast(F32), 1.0).then_inc(s_fill, 1)

        @block.scalar
        def _(act):
            A = nc.scalar

            def w_hi(i):
                act.wait_ge(s_raw[i % 3], 16 * (i // 3 + 1))
                if i >= 2:
                    act.wait_ge(s_item, i - 1)
                A.activation(m.wh[:, i % 2], m.raw[:, i % 3], ACT.Copy).then_inc(s_hi, 1)

            norm_scalar_squares(k, n2, act)
            w_hi(0)
            w_hi(1)
            norm_scalar_modulate(k, n2, act, k.gain[:, 1], k.mod[:, 24:32])
            act.wait_ge(s_aux, 32)
            rows = slice(AUG0, AUG0 + AUG_ROWS)
            A.activation(m.qn[rows, :, :], m.aug[rows, A_SLOPE:A_SLOPE + HEADS].unsqueeze(2)
                         .to_broadcast([AUG_ROWS, HEADS, T]), ACT.Copy)
            for b, br in ((0, 1), (1, 2), (2, 3)):
                for g in range(KV):
                    A.activation(m.kk[rows, b, g], m.aug[rows, A_KPOS:A_KPOS + T], ACT.Identity,
                                 bias=m.aug[rows, A_IND + br:A_IND + br + 1])
            act.wait_ge(s_fill, 4)
            for g in range(KV):
                ins = A.activation(m.kc[rows, g], m.aug[rows, A_CPOS:A_CPOS + NCP], ACT.Identity,
                                   bias=m.aug[rows, A_IND:A_IND + 1])
            ins.then_inc(s_kv0, 1)
            for i in range(N):
                kind, bank = kinds[i], k.bank[bank_of.get(i, 0)]
                if i >= 1 and i + 1 < N + 1:
                    w_hi(i + 1)
                if kind in ACT_KINDS:
                    act.wait_ge(s_item, i + 1)
                if kind == "qs":
                    A.activation(m.qsf[:, int(items[i][1][2])], bank[:, :], ACT.Copy, scale=SCALE).then_inc(s_act, 1)
                elif kind in ("kb", "ks", "kw"):
                    b = k_branch[kind]
                    for g in range(KV):
                        src = bank[g * DH:(g + 1) * DH, :]
                        A.activation(m.kk[0:DH, b, g], src, ACT.Copy)
                        ins = A.activation(m.kk2[0:DH, b, g], src, ACT.Copy)
                    ins.then_inc(s_act, 1)
                elif kind == "qn":
                    for r in range(2):
                        h, src = int(items[i][1][2]) * 2 + r, bank[r * DH:(r + 1) * DH, :]
                        A.activation(m.qn[0:DH, h], src, ACT.Copy, scale=SCALE)
                        ins = A.activation(m.qn2[DH:P, h], src, ACT.Copy, scale=SCALE)
                    ins.then_inc(s_act, 1)
                elif kind in ("vb", "vs", "vw"):
                    j = v_items.index(i)
                    if j >= 2:
                        act.wait_ge(s_vt, j - 1)
                    A.activation(m.vT[:, j % 2], bank[:, :], ACT.Copy).then_inc(s_act, 1)
                elif kind == "gn":
                    A.activation(m.gs[:, :], bank[0:3 * HEADS, :], ACT.Sigmoid).then_inc(s_act, 1)
                if i - 1 in v_items:
                    j = v_items.index(i - 1)
                    b = v_branch[kinds[i - 1]]
                    act.wait_ge(s_vt, j + 1)
                    if j == 0:
                        act.wait_ge(s_fill, 4)
                    for g in range(KV):
                        ins = A.activation(m.vh[:, b, g, :, 0:DH],
                                           k.bank[3][:, :].rearrange("p (t g d) -> p t g d", t=QT, g=KV)[:, :, g],
                                           ACT.Copy)
                    ins.then_inc(s_vta, 1)
                if i - 1 >= 0 and kinds[i - 1] in ("kc", "vc"):
                    c = 0 if kinds[i - 1] == "kc" else 1
                    act.wait_ge(s_dve, dve_after[i - 1])
                    A.activation(m.blkh[:, c], m.blk[:, c], ACT.Copy).then_inc(s_blkh, 1)
                    if c == 0:
                        act.wait_ge(s_cw2, 16)
                        A.activation(m.cw2h[:, :, :, :], m.cw2[:, :, :, :], ACT.Copy).then_inc(s_w2h, 1)
                if i in cmp_end:
                    c = cmp_end[i]
                    act.wait_ge(s_x, 4 * c + 4)
                    A.activation(m.ge[:, 2], m.ge[:, 1], ACT.Tanh, scale=math.sqrt(2 / math.pi)).then_inc(s_th, 1)
                    act.wait_ge(s_g, c + 1)
                    A.activation(m.geh[:, :], m.ge[:, 3], ACT.Copy, scale=0.5).then_inc(s_gh, 1)
                    act.wait_ge(s_c2, c + 1)
                    if c == 0:
                        src = k.bank[2][0:DH, 0:KV * NC_BLOCKS].rearrange("p (g n) -> p g n", g=KV)
                        A.activation(m.kc[0:DH, :, 0:NC_BLOCKS], src, ACT.Copy)
                        A.activation(m.kc2[0:DH, :, 0:NC_BLOCKS], src, ACT.Copy).then_inc(s_c2a, 1)
                    else:
                        A.activation(m.vch[0:NC_BLOCKS, :, 0:DH],
                                     k.bank[2][0:NC_BLOCKS, 0:P].rearrange("p (g d) -> p g d", g=KV),
                                     ACT.Copy).then_inc(s_c2a, 1)
            for j in range(N_GATES):
                if j + 1 < N_GATES:
                    w_hi(N + j + 1)
                act.wait_ge(s_item, N + j + 1)
                A.activation(m.gates[:, j], k.bank[j % 2][:, :], ACT.Sigmoid).then_inc(s_act, 1)

        @block.vector
        def _(dve):
            V = nc.vector

            def w_lo(i):
                dve.wait_ge(s_hi, i + 1)
                V.tensor_tensor(m.wl[:, i % 2], m.raw[:, i % 3], m.wh[:, i % 2].bitcast(F32),
                                ALU.subtract).then_inc(s_lo, 1)
            norm_vector_rstd(k, n2, dve)
            w_lo(0)
            norm_vector_modulate(k, n2, dve, k.gain[:, 1], k.mod[:, 24:32])
            w_lo(1)
            for i in range(N):
                kind, bank = kinds[i], k.bank[bank_of.get(i, 0)]
                if i >= 1:
                    w_lo(i + 1)
                if kind in ("kb", "ks", "kw"):
                    dve.wait_ge(s_act, act_after[i])
                    b = k_branch[kind]
                    for g in range(KV):
                        ins = V.tensor_tensor(m.kk2[DH:P, b, g], bank[g * DH:(g + 1) * DH, :],
                                              m.kk[0:DH, b, g].bitcast(F32), ALU.subtract)
                    ins.then_inc(s_dve, 1)
                elif kind == "qn":
                    dve.wait_ge(s_act, act_after[i])
                    for r in range(2):
                        h = int(items[i][1][2]) * 2 + r
                        ins = V.scalar_tensor_tensor(m.qn2[0:DH, h], bank[r * DH:(r + 1) * DH, :], SCALE,
                                                     m.qn[0:DH, h].bitcast(F32), ALU.mult, ALU.subtract)
                    ins.then_inc(s_dve, 1)
                elif kind in ("kc", "vc"):
                    c = 0 if kind == "kc" else 1
                    dve.wait_ge(s_item, i + 1)
                    if c == 0:
                        dve.wait_ge(s_aux, 32)
                    for g in range(KV):
                        for par in range(2):
                            half = slice(par * DH, (par + 1) * DH)
                            src = bank[g * DH:(g + 1) * DH, par:par + 1]
                            tok = bass.AP(tensor=src.tensor, offset=src.offset,
                                          ap=[list(src.ap[0]), [2, 16], [CMP_STRIDE, NC_BLOCKS]])
                            dst = m.blk[half, c].rearrange("p (j g n) -> p j g n", j=16, g=KV)[:, :, g]
                            ins = V.tensor_tensor(dst, tok, m.cpos[half, c].unsqueeze(2)
                                                  .to_broadcast([DH, 16, NC_BLOCKS]), ALU.add)
                    ins.then_inc(s_dve, 1)
                if i - 1 in v_items:
                    j = v_items.index(i - 1)
                    b = v_branch[kinds[i - 1]]
                    dve.wait_ge(s_vta, j + 1)
                    for g in range(KV):
                        ins = V.tensor_tensor(m.vl[:, b, g, :, 0:DH],
                                              k.bank[3][:, :].rearrange("p (t g d) -> p t g d", t=QT, g=KV)[:, :, g],
                                              m.vh[:, b, g, :, 0:DH].bitcast(F32), ALU.subtract)
                    ins.then_inc(s_vtd, 1)
                if i - 1 >= 0 and kinds[i - 1] in ("kc", "vc"):
                    c = 0 if kinds[i - 1] == "kc" else 1
                    dve.wait_ge(s_blkh, c + 1)
                    V.tensor_tensor(m.blkl[:, c], m.blk[:, c], m.blkh[:, c].bitcast(F32),
                                    ALU.subtract).then_inc(s_blkl, 1)
                    if c == 0:
                        dve.wait_ge(s_w2h, 1)
                        V.tensor_tensor(m.cw2l[:, :, :, :], m.cw2[:, :, :, :], m.cw2h[:, :, :, :].bitcast(F32),
                                        ALU.subtract).then_inc(s_w2l, 1)
                if i in cmp_end:
                    c = cmp_end[i]
                    dve.wait_ge(s_item, i + 1)
                    x, t, th, g_ = (m.ge[:, j] for j in range(4))
                    for hid in range(2):
                        ins = V.tensor_copy(x[:, hid], k.bank[4 + 2 * c + hid][:, 0:KV * NC_BLOCKS])
                    ins.then_inc(s_x, 1)
                    dve.wait_ge(s_x, 4 * c + 1)
                    V.tensor_tensor(t, x, x, ALU.mult).then_inc(s_x, 1)
                    dve.wait_ge(s_x, 4 * c + 2)
                    V.tensor_scalar(t, t, 0.044715, 1.0, ALU.mult, ALU.add).then_inc(s_x, 1)
                    dve.wait_ge(s_x, 4 * c + 3)
                    V.tensor_tensor(t, t, x, ALU.mult).then_inc(s_x, 1)
                    dve.wait_ge(s_th, c + 1)
                    V.scalar_tensor_tensor(g_, th, 1.0, x, ALU.add, ALU.mult).then_inc(s_g, 1)
                    dve.wait_ge(s_gh, c + 1)
                    V.scalar_tensor_tensor(m.gel[:, :], g_, 0.5, m.geh[:, :].bitcast(F32), ALU.mult,
                                           ALU.subtract).then_inc(s_gl, 1)
                    dve.wait_ge(s_c2a, c + 1)
                    if c == 0:
                        src = k.bank[2][0:DH, 0:KV * NC_BLOCKS].rearrange("p (g n) -> p g n", g=KV)
                        V.tensor_tensor(m.kc2[DH:P, :, 0:NC_BLOCKS], src, m.kc[0:DH, :, 0:NC_BLOCKS].bitcast(F32),
                                        ALU.subtract).then_inc(s_c2d, 1)
                    else:
                        V.tensor_tensor(m.vcl[0:NC_BLOCKS, :, 0:DH],
                                        k.bank[2][0:NC_BLOCKS, 0:P].rearrange("p (g d) -> p g d", g=KV),
                                        m.vch[0:NC_BLOCKS, :, 0:DH].bitcast(F32), ALU.subtract).then_inc(s_c2d, 1)
            for j in range(N_GATES):
                if j + 1 < N_GATES:
                    w_lo(N + j + 1)

        @block.tensor
        def _(pe):
            norm_tensor_sums(k, n2, pe)

            def product(slot, bank, s_u=None):
                w = [m.wh[:, slot].rearrange("p (k c) -> p k c", c=P), m.wl[:, slot].rearrange("p (k c) -> p k c", c=P)]
                for kt in range(DT):
                    if s_u is not None:
                        pe.wait_ge(s_u, kt + 1)
                    for j, (x, y) in enumerate(split_terms(w[0][:, kt], w[1][:, kt], k.uh[:, kt], k.ul[:, kt])):
                        mm = nc.tensor.matmul(bank[:, :], x, y, start=(kt == 0 and j == 0),
                                              stop=(kt == DT - 1 and j == 2))
                mm.then_inc(s_item, 1)
            for i in range(N):
                pe.wait_ge(s_lo, i + 1)
                if items[i][0] == "in":
                    before = bank_before[i]
                    if before is not None:
                        if kinds[before] in DVE_KINDS:
                            pe.wait_ge(s_dve, dve_after[before])
                        else:
                            pe.wait_ge(s_act, act_after[before])
                    product(i % 2, k.bank[bank_of[i]], n2.s_ul if i == 0 else None)
                else:
                    c, chunk = (0 if items[i][0] == "ck" else 1), items[i][1]
                    if chunk == 0:
                        pe.wait_ge(s_blkl, c + 1)
                    w = [x[:, i % 2].rearrange("p (j h) -> p j h", j=4) for x in (m.wh, m.wl)]
                    b = [x[:, c].rearrange("p (j n) -> p j n", j=16) for x in (m.blkh, m.blkl)]
                    for hid in range(2):
                        cols = slice(hid * P, (hid + 1) * P)
                        for j in range(4):
                            for q, (x, y) in enumerate(split_terms(w[0][:, j, cols], w[1][:, j, cols],
                                                                   b[0][:, chunk * 4 + j], b[1][:, chunk * 4 + j])):
                                mm = nc.tensor.matmul(k.bank[4 + 2 * c + hid][:, 0:KV * NC_BLOCKS], x, y,
                                                      start=(chunk == 0 and j == 0 and q == 0),
                                                      stop=(chunk == 3 and j == 3 and q == 2))
                    mm.then_inc(s_item, 1)
                if i - 1 in v_items:
                    j = v_items.index(i - 1)
                    pe.wait_ge(s_act, act_after[i - 1])
                    if j >= 1:
                        pe.wait_ge(s_vtd, j)
                    for t in range(QT):
                        mm = nc.tensor.transpose(k.bank[3][:, t * P:(t + 1) * P], m.vT[:, j % 2, t * P:(t + 1) * P],
                                                 k.idF[:, :])
                    mm.then_inc(s_vt, 1)
                if i in cmp_end:
                    c = cmp_end[i]
                    pe.wait_ge(s_gl, c + 1)
                    pe.wait_ge(s_w2l, 1)
                    if c == 0:
                        for hid in range(2):
                            for q, (x, y) in enumerate(split_terms(m.cw2h[:, 0, hid], m.cw2l[:, 0, hid],
                                                                   m.geh[:, hid], m.gel[:, hid])):
                                mm = nc.tensor.matmul(k.bank[2][0:DH, 0:KV * NC_BLOCKS], x, y,
                                                      start=(hid == 0 and q == 0), stop=(hid == 1 and q == 2))
                    else:
                        pe.wait_ge(s_c2d, 1)
                        for g in range(KV):
                            nn = slice(g * NC_BLOCKS, (g + 1) * NC_BLOCKS)
                            for hid in range(2):
                                for q, (x, y) in enumerate(split_terms(m.geh[:, hid, nn], m.gel[:, hid, nn],
                                                                       m.cw2h[:, 1, hid], m.cw2l[:, 1, hid])):
                                    mm = nc.tensor.matmul(k.bank[2][0:NC_BLOCKS, g * DH:(g + 1) * DH], x, y,
                                                          start=(hid == 0 and q == 0), stop=(hid == 1 and q == 2))
                    mm.then_inc(s_c2, 1)
            pe.wait_ge(s_act, act_after[N - 1])
            pe.wait_ge(s_dve, dve_after[N - 1])
            with pe.Fori(0, N_GATES // 2) as it:
                for s in range(2):
                    pe.wait_ge(s_lo, it * 2 + (N + s + 1))
                    pe.wait_ge(s_act, it * 2 + (act_after[N - 1] + s - 1))
                    product((N + s) % 2, k.bank[s])


def attention_buffers(k, m):
    s, at, X, K = Record(), k.at, k.X, 1024
    s.p32 = at("exp_f32", [P, 3, T], F32, X + 120 * K)
    s.ph = at("exp_hi", [P, 3, T], F32R, X + 126 * K)
    s.pl = at("exp_lo", [P, 3, T], F32R, X + 132 * K)
    s.num = [at("numerator0", [P, 4, T], F32, X + 138 * K), at("numerator1", [P, 4, T], F32, 0)]
    s.ya = at("y_a", [P, 4, T], F32, 8 * K)
    s.yb = s.num[1]
    s.yah = at("y_a_hi", [P, 4, T], F32R, X + 32 * K)
    s.yal = at("y_a_lo", [P, 4, T], F32R, X + 40 * K)
    s.ybh = at("y_b_hi", [P, 4, T], F32R, X + 48 * K)
    s.ybl = at("y_b_lo", [P, 4, T], F32R, X + 56 * K)
    s.fb = at("factor_bc", [P, 4, T], F32, X + 105 * K)
    s.R = [at(f"minus_max_rows{j}", [HEADS, T], F32R, X + (101 + 2 * j) * K) for j in range(2)]
    s.se = at("sink_exp", [HEADS, T], F32, X + 113 * K)
    c = X + 146 * K
    s.nm = at("minus_max", [P, 2, HEADS, QT], F32, c)
    s.sk = at("minus_sink", [P, HEADS, QT], F32, c + 256)
    s.sinks = at("sinks_bc", [P, HEADS], F32, c + 384)
    s.sinkc = at("sinks_col", [HEADS, 1], F32, c + 416)
    s.gsp = at("gates_spread", [P, 3, 32], F32, c + 448)
    s.den = at("den_spread", [P, 4, 32], F32, c + 832)
    s.sden = at("sink_den_spread", [P, 32], F32, c + 1344)
    s.fac = at("factor_spread", [P, 2, 32], F32, c + 1472)
    s.dr = [at("den_row0", [P, T], F32, X + 118 * K), at("den_row1", [P, T], F32, X + 148 * K)]
    s.s_setup, s.s_gsp, s.s_qrows = k.sem("at_setup"), k.sem("at_gsp"), k.sem("at_qrows")
    s.s_qsh, s.s_qsl, s.s_a = k.sem("at_qsh"), k.sem("at_qsl"), k.sem("at_a")
    s.s_red, s.s_nm, s.s_tr = k.sem("at_red"), k.sem("at_nm"), k.sem("at_tr")
    s.s_R, s.s_st, s.s_ph = k.sem("at_R"), k.sem("at_st"), k.sem("at_ph")
    s.s_pl, s.s_pv, s.s_num = k.sem("at_pl"), k.sem("at_pv"), k.sem("at_num")
    s.s_dr, s.s_sets, s.s_sead = k.sem("at_dr"), k.sem("at_sets"), k.sem("at_sead")
    s.s_mul, s.s_seex, s.s_sed = k.sem("at_mul"), k.sem("at_seex"), k.sem("at_sed")
    s.s_d1, s.s_d2, s.s_yh = k.sem("at_d1"), k.sem("at_d2"), k.sem("at_yh")
    s.s_yl = k.sem("at_yl")
    s.s_row = [k.sem(f"at_row{b}") for b in range(4)]
    s.s_drd = [k.sem(f"at_den{j}") for j in range(2)]
    s.s_fout = [k.sem(f"at_fout{b}") for b in range(4)]
    s.s_fin = [k.sem(f"at_fin{b}") for b in range(4)]
    return s


def attention_units(b):
    out = []
    for h in range(HEADS):
        if b == 0:
            out.append((h, 0, 0, T, True, True))
        else:
            for kb in range(QT):
                n = T - kb * P if b < 3 else min(2 * P, T - kb * P)
                out.append((h, kb, kb * P, n, kb == 0, kb == QT - 1))
    return out


def maximum_groups(b):
    if b == 0:
        return [[(h, q, 0, NCP, (h % 4) * P + q * NCP) for h in range(g * 4, g * 4 + 4) for q in range(QT)]
                for g in range(2)]
    if b == 3:
        return [x for h in range(HEADS) for x in ([(h, 1, 0, 2 * P, 0), (h, 2, P, 2 * P, 2 * P)],
                                                  [(h, 3, 2 * P, 2 * P, 0), (h, 0, 0, P, 2 * P)])]
    return [x for h in range(HEADS) for x in ([(h, 0, 0, P, 0), (h, 2, 0, 3 * P, P)], [(h, 1, 0, 2 * P, 0)],
                                              [(h, 3, 0, 4 * P, 0)])]


def attention_order():
    out, groups = [], {b: [("max", b, g) for g in range(len(maximum_groups(b)))] for b in range(4)}

    def take(b, n):
        for _ in range(min(n, len(groups[b]))):
            out.append(groups[b].pop(0))
    take(0, 2)
    out.append(("rows", 0))
    take(1, 6)
    for b in range(4):
        for u in range(len(attention_units(b))):
            if b < 3:
                take(b + 1, 2 if b == 0 else 1)
            if b in (1, 2) and not groups[b + 1] and ("rows", b + 1) not in out:
                out.append(("rows", b + 1))
            out.append(("unit", b, u))
            if b == 0:
                out.append(("swaq", u))
            if b > 0 and u == 4:
                out.append(("div", b - 1))
            if b > 0 and u >= 12 and u % 2 == 0 and u < 20:
                out.append(("mul", b - 1, (u - 12) // 2))
            if b == 3 and u >= 22 and u % 2 == 0 and u < 30:
                out.append(("yhi", (u - 22) // 2))
        if b == 0:
            take(1, 99)
            out.append(("rows", 1))
            take(2, 6)
    return out


def attention(k, m):
    nc, a = k.nc, k.a
    s = attention_buffers(k, m)
    order = attention_order()
    unit_at = [(b, u) for kind, b, u in (x for x in order if x[0] == "unit")]
    index = {x: i for i, x in enumerate(unit_at)}
    info = [(b,) + attention_units(b)[u] for b, u in unit_at]
    group_index = {x[1:]: i for i, x in enumerate(x for x in order if x[0] == "max")}
    LAG = 2
    q_of = lambda b: (m.qn, m.qn2) if b < 3 else (m.qs, m.qs2)

    def keys(b, h):
        g = h // REP
        return (m.kc[:, g], m.kc2[:, g]) if b == 0 else (m.kk[:, b - 1, g], m.kk2[:, b - 1, g])

    def values(b, h, kb):
        g = h // REP
        if b == 0:
            return m.vch[0:NC_BLOCKS, g, 0:DH + 1], m.vcl[0:NC_BLOCKS, g, 0:DH + 1]
        return m.vh[:, b - 1, g, kb, 0:DH + 1], m.vl[:, b - 1, g, kb, 0:DH + 1]

    def head_no(i):
        return info[i][0] * HEADS + info[i][1]

    with nc.Block() as block:
        @block.sync
        def _(sp):
            sp.dma_start(s.sinks[:, :], a.sinks.unsqueeze(0).to_broadcast([P, HEADS])).then_inc(s.s_setup, 16)
            sp.dma_start(s.sk[:, :, :].rearrange("p h q -> p (h q)"), a.slope_cols).then_inc(s.s_setup, 16)
            sp.dma_start(s.sinkc[:, :], a.sinks.rearrange("(h o) -> h o", o=1)).then_inc(s.s_setup, 16)
            sp.dma_start(s.se[:, :], a.slope_rows).then_inc(s.s_setup, 16)
            for b, rows in enumerate((0, 2, 1)):
                sp.dma_start(s.gsp[:, b], m.gs[rows * HEADS:(rows + 1) * HEADS, :]).then_inc(s.s_gsp, 16)
            sp.dma_start(m.qs[DH:96].bitcast(F32), m.qn[DH:96].bitcast(F32)).then_inc(s.s_qrows, 16)

            def denominator_out(i):
                if i >= 0 and info[i][6]:
                    c, h = head_no(i), info[i][1]
                    sp.wait_ge(s.s_dr, c + 1)
                    sp.dma_start(s.den[h * 16:(h + 1) * 16, info[i][0]], s.dr[c % 2][DH:DH + 1, :])\
                        .then_inc(s.s_drd[c % 2], 16)
            for x in order:
                if x[0] == "rows":
                    b = x[1]
                    row = ROW_M[BRANCHES[b]]
                    sp.wait_ge(s.s_R, b + 1)
                    sp.dma_start(q_of(b)[0][row:row + 1].bitcast(F32), s.R[b % 2][:, :].bitcast(F32))\
                        .then_inc(s.s_row[b], 16)
                    if b == 3:
                        sp.wait_ge(s.s_seex, 1)
                        sp.dma_start(s.sden[:, :], s.se[:, :]).then_inc(s.s_sed, 16)
                elif x[0] == "unit":
                    denominator_out(index[x[1:]] - LAG)
                elif x[0] == "div":
                    factors_out(k, s, sp, x[1])
            for i in range(len(info) - LAG, len(info)):
                denominator_out(i)

        @block.scalar
        def _(act):
            A = nc.scalar

            def exps(i):
                b, h, kb, q0, n, first, last = info[i]
                rows = NC_BLOCKS if b == 0 else P
                act.wait_ge(s.s_st, i + 1)
                if i >= 3:
                    act.wait_ge(s.s_pv, i - 2)
                src = k.bank[2 + i % 3][0:rows, 0:n]
                A.activation(s.p32[0:rows, i % 3, 0:n], src, ACT.Exp)
                A.activation(s.ph[0:rows, i % 3, 0:n], src, ACT.Exp).then_inc(s.s_ph, 1)

            def numerator(i):
                b, h, kb, q0, n, first, last = info[i]
                if last:
                    c = b * HEADS + h
                    act.wait_ge(s.s_pv, i + 1)
                    if b >= 2 and h == 0:
                        act.wait_ge(s.s_d2, 4 * (b - 1))
                    half = slice((h % 2) * DH, (h % 2 + 1) * DH)
                    A.activation(s.num[b % 2][half, h // 2], k.bank[5 + c % 2][0:DH, :], ACT.Copy).then_inc(s.s_num, 1)
            for x in order:
                if x[0] == "unit":
                    i = index[x[1:]]
                    exps(i)
                    if i >= LAG:
                        numerator(i - LAG)
                elif x[0] == "rows":
                    b = x[1]
                    act.wait_ge(s.s_tr, b + 1)
                    A.activation(s.R[b % 2][:, :], k.bank[7][0:HEADS, :], ACT.Copy).then_inc(s.s_R, 1)
                    if b == 3:
                        act.wait_ge(s.s_sead, 1)
                        A.activation(s.se[:, :], s.se[:, :], ACT.Exp, bias=s.sinkc[:, :]).then_inc(s.s_seex, 1)
                elif x[0] == "swaq":
                    h = x[1]
                    src = m.qsf[(h % 2) * DH:(h % 2 + 1) * DH, h // 2]
                    A.activation(m.qs[0:DH, h], src, ACT.Copy)
                    A.activation(m.qs2[DH:P, h], src, ACT.Copy).then_inc(s.s_qsh, 1)
                elif x[0] == "yhi":
                    p = x[1]
                    act.wait_ge(s.s_d2, 8 + p + 1)
                    A.activation(s.yah[:, p], s.ya[:, p], ACT.Copy).then_inc(s.s_yh, 1)
            for i in range(len(info) - LAG, len(info)):
                numerator(i)

        @block.vector
        def _(dve):
            V = nc.vector

            def denominator(i):
                b, h, kb, q0, n, first, last = info[i]
                if last:
                    c = b * HEADS + h
                    if c == 0:
                        dve.wait_ge(s.s_gsp, 48)
                    dve.wait_ge(s.s_pv, i + 1)
                    if c >= 2:
                        dve.wait_ge(s.s_drd[c % 2], 16 * (c // 2))
                    V.tensor_copy(s.dr[c % 2][DH:DH + 1, :], k.bank[5 + c % 2][DH:DH + 1, :]).then_inc(s.s_dr, 1)
            dve.wait_ge(s.s_setup, 64)
            V.tensor_tensor(s.sk[:, :, :], s.sk[:, :, :], s.sinks[:, :].unsqueeze(2).to_broadcast([P, HEADS, QT]),
                            ALU.add).then_inc(s.s_sets, 1)
            dve.wait_ge(s.s_sets, 1)
            V.tensor_scalar(s.sk[:, :, :], s.sk[:, :, :], -1.0, None, ALU.mult).then_inc(s.s_sets, 1)
            for x in order:
                if x[0] == "max":
                    _, b, g = x
                    gi = group_index[(b, g)]
                    parts = maximum_groups(b)[g]
                    bank = k.bank[gi % 2]
                    nm = s.nm[:, b % 2]
                    dve.wait_ge(s.s_a, gi + 1)
                    if b == 0:
                        ins = V.tensor_reduce(nm[:, g * 4:g * 4 + 4, :].rearrange("p h q -> p (h q)"),
                                              bank[:, :].rearrange("p (r n) -> p r n", n=NCP), AX.X, ALU.max, negate=True)
                    else:
                        for h, q, _, n, col in parts:
                            ins = V.tensor_reduce(nm[:, h, q:q + 1], bank[:, col:col + n], AX.X, ALU.max, negate=True)
                    ins.then_inc(s.s_red, 1)
                    if g == len(maximum_groups(b)) - 1:
                        dve.wait_ge(s.s_red, gi + 1)
                        if b < 3:
                            V.tensor_scalar(nm, nm, 1e20, None, ALU.min).then_inc(s.s_nm, 1)
                        else:
                            dve.wait_ge(s.s_sets, 2)
                            V.tensor_tensor(nm, nm, s.sk[:, :, :], ALU.min).then_inc(s.s_nm, 1)
                elif x[0] == "rows" and x[1] == 3:
                    dve.wait_ge(s.s_R, 4)
                    V.tensor_tensor(s.se[:, :], s.se[:, :], s.R[1][:, :].bitcast(F32), ALU.add).then_inc(s.s_sead, 1)
                elif x[0] == "unit":
                    i = index[x[1:]]
                    b, h, kb, q0, n, first, last = info[i]
                    rows = NC_BLOCKS if b == 0 else P
                    dve.wait_ge(s.s_ph, i + 1)
                    V.tensor_tensor(s.pl[0:rows, i % 3, 0:n], s.p32[0:rows, i % 3, 0:n],
                                    s.ph[0:rows, i % 3, 0:n].bitcast(F32), ALU.subtract).then_inc(s.s_pl, 1)
                    if i >= LAG:
                        denominator(i - LAG)
                elif x[0] == "swaq":
                    h = x[1]
                    dve.wait_ge(s.s_qsh, h + 1)
                    hi = m.qs2[DH:P, h] if h % 2 else m.qs[0:DH, h]
                    V.tensor_tensor(m.qs2[0:DH, h], m.qsf[(h % 2) * DH:(h % 2 + 1) * DH, h // 2], hi.bitcast(F32),
                                    ALU.subtract).then_inc(s.s_qsl, 1)
                elif x[0] == "yhi":
                    p = x[1]
                    dve.wait_ge(s.s_yh, p + 1)
                    V.tensor_tensor(s.yal[:, p], s.ya[:, p], s.yah[:, p].bitcast(F32), ALU.subtract).then_inc(s.s_yl, 1)
                elif x[0] == "div":
                    factors(k, s, dve, x[1])
                elif x[0] == "mul":
                    weigh(k, s, dve, x[1], x[2])
            for i in range(len(info) - LAG, len(info)):
                denominator(i)

        @block.tensor
        def _(pe):
            def scores(i):
                b, h, kb, q0, n, first, last = info[i]
                rows, last_row = (NC_BLOCKS if b == 0 else P), ROW_M[BRANCHES[b]] + 1
                kr, kp = keys(b, h)
                ks = slice(kb * P, kb * P + rows)
                q1, q2 = q_of(b)
                out = k.bank[2 + i % 3][0:rows, 0:n]
                if h == 0 and first:
                    pe.wait_ge(s.s_row[b], 16)
                    if b == 3:
                        pe.wait_ge(s.s_qsl, HEADS)
                if i >= 3:
                    pe.wait_ge(s.s_ph, i - 2)
                mm = nc.tensor.matmul
                width = T if b == 0 else P if b < 3 or n == P else 2 * P
                mask = k.mcc[0:rows, :] if b == 0 else \
                    k.msk[:, M_L:M_L + width // P].rearrange("p m c -> p (m c)")
                mm(out[:, 0:width], k.idR[0:rows, 0:rows], mask, start=True, stop=False, skip_group_check=True)
                mm(out, kr[0:last_row, ks], q1[0:last_row, h, q0:q0 + n], start=False, stop=False,
                   skip_group_check=True)
                mm(out, kp[:, ks], q2[:, h, q0:q0 + n], start=False, stop=True, skip_group_check=True)\
                    .then_inc(s.s_st, 1)

            def product(i):
                b, h, kb, q0, n, first, last = info[i]
                c = b * HEADS + h
                rows = NC_BLOCKS if b == 0 else P
                vh, vl = values(b, h, kb)
                out = k.bank[5 + c % 2][0:DH + 1, q0:q0 + n]
                pe.wait_ge(s.s_pl, i + 1)
                if first and c >= 2:
                    pe.wait_ge(s.s_num, c - 1)
                    pe.wait_ge(s.s_dr, c - 1)
                ph, pl = s.ph[0:rows, i % 3, 0:n], s.pl[0:rows, i % 3, 0:n]
                for j, (x, y) in enumerate(((vh, ph), (vh, pl), (vl, ph))):
                    mm = nc.tensor.matmul(out, x, y, start=(first and j == 0), stop=(last and j == 2),
                                          skip_group_check=True)
                mm.then_inc(s.s_pv, 1)

            for x in order:
                if x[0] == "max":
                    _, b, g = x
                    gi = group_index[(b, g)]
                    bank, q1 = k.bank[gi % 2], q_of(b)[0]
                    if gi >= 2:
                        pe.wait_ge(s.s_red, gi - 1)
                    if b == 3 and g == 0:
                        pe.wait_ge(s.s_qrows, 16)
                    if b == 3 and g % 2 == 0:
                        pe.wait_ge(s.s_qsh, g // 2 + 1)
                    parts = maximum_groups(b)[g]
                    for j, (h, q, k0, n, col) in enumerate(parts):
                        kr = keys(b, h)[0]
                        mm = nc.tensor.matmul(bank[:, col:col + n], q1[0:DH + 1, h, q * P:(q + 1) * P],
                                              kr[0:DH + 1, k0:k0 + n], start=(j == 0), stop=False,
                                              skip_group_check=True)
                        if b == 0 and q == QT - 1:
                            mm = nc.tensor.matmul(bank[:, (h % 4) * P:(h % 4 + 1) * P], k.idR[:, :],
                                                  k.mca[:, :, :].rearrange("p q n -> p (q n)"), start=False,
                                                  stop=True, skip_group_check=True)
                        elif b > 0:
                            width = 2 * P if b == 3 and n == 2 * P else P
                            mask = k.msk[:, 2 - width // P:2].rearrange("p m c -> p (m c)")
                            mm = nc.tensor.matmul(bank[:, col + n - width:col + n], k.idR[:, :], mask, start=False,
                                                  stop=True, skip_group_check=True)
                    mm.then_inc(s.s_a, 1)
                elif x[0] == "rows":
                    b = x[1]
                    pe.wait_ge(s.s_nm, b + 1)
                    if b >= 1:
                        pe.wait_ge(s.s_R, b)
                    for q in range(QT):
                        mm = nc.tensor.transpose(k.bank[7][0:HEADS, q * P:(q + 1) * P], s.nm[:, b % 2, :, q], k.idF[:, :])
                    mm.then_inc(s.s_tr, 1)
                elif x[0] == "unit":
                    i = index[x[1:]]
                    scores(i)
                    if i >= LAG:
                        product(i - LAG)
            for i in range(len(info) - LAG, len(info)):
                product(i)
    return s


def factors(k, s, dve, b):
    V = k.nc.vector
    den, fac = s.den[:, b], s.fac[:, b % 2]
    n = counter()
    n(3 * b)

    def then(ins):
        ins.then_inc(s.s_d1, 1)
        return n()
    for j in range(2):
        dve.wait_ge(s.s_drd[j], 16 * 4 * (b + 1))
    if b == 0:
        dve.wait_ge(s.s_gsp, 48)
    if b == 3:
        dve.wait_ge(s.s_sed, 16)
        dve.wait_ge(s.s_d1, then(V.tensor_tensor(den, den, s.sden[:, :], ALU.add)))
    else:
        dve.wait_ge(s.s_d1, then(V.tensor_scalar(den, den, 1e-30, None, ALU.max)))
    dve.wait_ge(s.s_d1, then(V.reciprocal(fac, den)))
    if b < 3:
        V.tensor_tensor(fac, fac, s.gsp[:, b], ALU.mult).then_inc(s.s_d1, 1)


def factors_out(k, s, sp, b):
    sp.wait_ge(s.s_d1, 3 * b + (3 if b < 3 else 2))
    sp.dma_start(k.fac[b].rearrange("(p c) -> p c", c=32), s.fac[:, b % 2]).then_inc(s.s_fout[b], 16)
    sp.wait_ge(s.s_fout[b], 16)
    if b == 0:
        sp.wait_ge(s.s_qsl, HEADS)
    else:
        sp.wait_ge(s.s_d2, 4 * b)
    rows = k.fac[b].rearrange("(h r t) -> r h t", r=2, t=T)
    for r in range(2):
        sp.dma_start(s.fb[r * DH:(r + 1) * DH, :, :], rows[r].unsqueeze(0).to_broadcast([DH, HEADS // 2, T])).then_inc(s.s_fin[b], 16)


def weigh(k, s, dve, b, p):
    V = k.nc.vector
    num = s.num[b % 2][:, p]
    if p == 0:
        dve.wait_ge(s.s_fin[b], 32)
    dve.wait_ge(s.s_num, b * HEADS + 2 * p + 2)
    if b == 0:
        V.tensor_tensor(s.ya[:, p], num, s.fb[:, p], ALU.mult).then_inc(s.s_d2, 1)
    elif b == 3:
        V.tensor_tensor(num, num, s.fb[:, p], ALU.mult).then_inc(s.s_d2, 1)
    else:
        V.tensor_tensor(num, num, s.fb[:, p], ALU.mult).then_inc(s.s_mul, 1)
        dve.wait_ge(s.s_mul, (b - 1) * 4 + p + 1)
        V.tensor_tensor(s.ya[:, p], s.ya[:, p], num, ALU.add).then_inc(s.s_d2, 1)


def merge(k, m, s):
    nc, a, X, K = k.nc, k.a, k.X, 1024
    S = k.sem
    raw = k.at("merge_raw", [P, 3, D], F32, X + 64 * K)
    wh = k.at("merge_w_hi", [P, 2, D], F32R, X + 76 * K)
    wl = k.at("merge_w_lo", [P, 2, D], F32R, X + 84 * K)
    ta = k.at("gated_a", [P, 2, T], F32, X + 92 * K)
    tb = k.at("gated_b", [P, 2, T], F32, X + 96 * K)
    mg = k.at("merged_f32", [P, 2, T], F32, X + 100 * K)
    mh, ml = k.uh, k.ul
    s_raw = [S(f"mg_raw{j}") for j in range(3)]
    s_hi, s_lo, s_item, s_h = S("mg_w_hi"), S("mg_w_lo"), S("mg_item"), S("mg_h")
    s_ta, s_tb, s_mg, s_mh, s_ml, s_add = S("mg_ta"), S("mg_tb"), S("mg_sum"), S("mg_hi"), S("mg_lo"), S("mg_add")
    items = [("a", n) for n in range(4)]
    for n in range(DT):
        items.append(("b", n))
        if n + 4 < DT:
            items.append(("a", n + 4))
    items += [("o", n) for n in range(DT)]
    N = len(items)
    where = {x: i for i, x in enumerate(items)}
    width = [D if x[0] == "o" else D // 2 for x in items]

    def source(i):
        kind, n = items[i]
        return a.wout[n].rearrange("p k c -> p (k c)") if kind == "o" else \
            a.wup[n, :, "ab".index(kind)].rearrange("p k c -> p (k c)")
    with nc.Block() as block:
        @block.sync
        def _(sp):
            for i in range(3):
                sp.dma_start(raw[:, i, 0:width[i]], source(i)).then_inc(s_raw[i], 16)
            factors_out(k, s, sp, 3)
            for i in range(3, N):
                sp.wait_ge(s_lo, i - 2)
                if i == where[("b", 4)]:
                    sp.wait_ge(s.s_yl, 8)
                    sp.dma_start(k.hT[:, :, :], k.hT_spill.rearrange("(t p) n -> p t n", p=P)).then_inc(s_h, 16)
                sp.dma_start(raw[:, i % 3, 0:width[i]], source(i)).then_inc(s_raw[i % 3], 16)

        @block.scalar
        def _(act):
            A = nc.scalar

            def w_hi(i):
                act.wait_ge(s_raw[i % 3], 16 * (i // 3 + 1))
                if i >= 2:
                    act.wait_ge(s_item, i - 1)
                A.activation(wh[:, i % 2, 0:width[i]], raw[:, i % 3, 0:width[i]], ACT.Copy).then_inc(s_hi, 1)
            w_hi(0)
            for i in range(N):
                if i + 1 < N:
                    w_hi(i + 1)
                if i == 3:
                    for p in range(4):
                        act.wait_ge(s.s_d2, 12 + p + 1)
                        A.activation(s.ybh[:, p], s.yb[:, p], ACT.Copy).then_inc(s.s_yh, 1)
                kind, n = items[i]
                if kind == "b":
                    act.wait_ge(s_mg, n + 1)
                    A.activation(mh[:, n], mg[:, n % 2], ACT.Copy).then_inc(s_mh, 1)

        @block.vector
        def _(dve):
            V = nc.vector

            def w_lo(i):
                dve.wait_ge(s_hi, i + 1)
                w = width[i]
                V.tensor_tensor(wl[:, i % 2, 0:w], raw[:, i % 3, 0:w], wh[:, i % 2, 0:w].bitcast(F32),
                                ALU.subtract).then_inc(s_lo, 1)

            w_lo(0)
            factors(k, s, dve, 3)
            for i in range(N):
                if i + 1 < N:
                    w_lo(i + 1)
                if i == 3:
                    for p in range(4):
                        weigh(k, s, dve, 3, p)
                        dve.wait_ge(s.s_yh, 4 + p + 1)
                        V.tensor_tensor(s.ybl[:, p], s.yb[:, p], s.ybh[:, p].bitcast(F32), ALU.subtract)\
                            .then_inc(s.s_yl, 1)
                kind, n = items[i]
                if kind == "b":
                    dve.wait_ge(s_item, where[("a", n)] + 1)
                    V.tensor_tensor(ta[:, n % 2], m.gates[:, n], k.bank[n % 4][:, :], ALU.mult).then_inc(s_ta, 1)
                    dve.wait_ge(s_item, i + 1)
                    V.tensor_tensor(tb[:, n % 2], m.gates[:, DT + n], k.bank[4 + n % 2][:, :], ALU.mult).then_inc(s_tb, 1)
                    dve.wait_ge(s_ta, n + 1)
                    dve.wait_ge(s_tb, n + 1)
                    V.tensor_tensor(mg[:, n % 2], ta[:, n % 2], tb[:, n % 2], ALU.add).then_inc(s_mg, 1)
                    dve.wait_ge(s_mh, n + 1)
                    V.tensor_tensor(ml[:, n], mg[:, n % 2], mh[:, n].bitcast(F32), ALU.subtract).then_inc(s_ml, 1)
                elif kind == "o":
                    if n == 0:
                        dve.wait_ge(s_h, 16)
                    dve.wait_ge(s_item, i + 1)
                    V.scalar_tensor_tensor(k.hT[:, n], k.bank[6 + n % 2][:, :], k.gate[:, 1, n:n + 1], k.hT[:, n],
                                           ALU.mult, ALU.add).then_inc(s_add, 1)

        @block.tensor
        def _(pe):
            for i in range(N):
                kind, n = items[i]
                pe.wait_ge(s_lo, i + 1)
                w = [x[:, i % 2, 0:width[i]].rearrange("p (k c) -> p k c", c=P) for x in (wh, wl)]
                if kind == "o":
                    bank, xs = k.bank[6 + n % 2], (mh, ml)
                    if n >= 2:
                        pe.wait_ge(s_add, n - 1)
                elif kind == "a":
                    bank, xs = k.bank[n % 4], (s.yah, s.yal)
                    if n >= 4:
                        pe.wait_ge(s_ta, n - 3)
                else:
                    bank, xs = k.bank[4 + n % 2], (s.ybh, s.ybl)
                    if n >= 2:
                        pe.wait_ge(s_tb, n - 1)
                depth = width[i] // P
                for kt in range(depth):
                    if kind == "a" and n == 0:
                        pe.wait_ge(s.s_yl, kt + 1)
                    if kind == "b" and n == 0:
                        pe.wait_ge(s.s_yl, 4 + kt + 1)
                    if kind == "o" and n == 0:
                        pe.wait_ge(s_ml, kt + 1)
                    for j, (x, y) in enumerate(split_terms(w[0][:, kt], w[1][:, kt], xs[0][:, kt], xs[1][:, kt])):
                        mm = nc.tensor.matmul(bank[:, :], x, y, start=(kt == 0 and j == 0),
                                              stop=(kt == depth - 1 and j == 2))
                mm.then_inc(s_item, 1)


def ffn2_and_output(k, f):
    nc, a, X, K = k.nc, k.a, k.X, 1024
    n = norm_buffers(k, 3, X + 88 * K, X + 61 * K)
    e = norm_buffers(k, 4, X + 24 * K, X + 40 * K, banks=(0, 1))
    o = k.at("out_tiles", [P, DT, T], F32, X + 104 * K)
    s_y, s_out = k.sem("out_ready"), k.sem("out_stored")
    yT = a.out.rearrange("(t p) n -> t p n", p=P)
    last_add = 4 + 8 * (GROUPS - 1)
    with nc.Block() as block:
        @block.sync
        def _(sp):
            for s in range(2):
                ffn_load_gu(k, f, sp, 0, s)
            for s in range(2):
                ffn_load_dn(k, f, sp, 0, s)
            ffn_sync_gu(k, f, sp, 1)
            with sp.Fori(1, GROUPS - 1) as g:
                ffn_sync_gu(k, f, sp, g + 1)
                ffn_sync_dn(k, f, sp, g)
            ffn_sync_dn(k, f, sp, GROUPS - 1)
            for t in range(DT):
                sp.wait_ge(s_y, t + 1)
                sp.dma_start(yT[t], o[:, t]).then_inc(s_out, 16)
            sp.wait_ge(s_out, 16 * DT)

        @block.scalar
        def _(act):
            norm_scalar_squares(k, n, act)
            norm_scalar_modulate(k, n, act, k.gain[:, 2], k.mod[:, 48:56])
            for s in range(2):
                ffn_scalar_gu_hi(k, f, act, 0, s)
            ffn_scalar_group(k, f, act, 0, 0, first=True)
            with act.Fori(0, 4) as it:
                ffn_scalar_group(k, f, act, it * 2 + 1, 1)
                ffn_scalar_group(k, f, act, it * 2 + 2, 0)
            ffn_scalar_group(k, f, act, 9, 1)
            ffn_scalar_group(k, f, act, 10, 0, last=True)
            act.wait_ge(f.s_dn_mm, 80)
            ffn_scalar_dn_hi(k, f, act, 10)
            norm_scalar_squares(k, e, act, f.s_bank, last_add)

        @block.vector
        def _(dve):
            norm_vector_rstd(k, n, dve)
            norm_vector_modulate(k, n, dve, k.gain[:, 2], k.mod[:, 48:56])
            nc.vector.tensor_copy(k.stat[:, 0], k.stat[:, 1]).then_inc(f.s_bank, 4)
            for s in range(2):
                ffn_vector_gu_lo(k, f, dve, 0, s)
            for s in range(2):
                ffn_vector_hidden(k, f, dve, 0, 0, s, split_next=True)

            def group(g, q):
                ffn_vector_dn_lo(k, f, dve, g - 1)
                for s in range(2):
                    ffn_vector_hidden(k, f, dve, g, q, s, split_next=(s == 0))
                ffn_vector_down(k, f, dve, g - 1, k.gate[:, 2], range(4))
                ffn_vector_gu_lo(k, f, dve, g + 1, 1)
                ffn_vector_down(k, f, dve, g - 1, k.gate[:, 2], range(4, DT))
            with dve.Fori(0, 4) as it:
                group(it * 2 + 1, 1)
                group(it * 2 + 2, 0)
            group(9, 1)
            ffn_vector_dn_lo(k, f, dve, 9)
            for s in range(2):
                ffn_vector_hidden(k, f, dve, 10, 0, s, split_next=False)
            ffn_vector_down(k, f, dve, 9, k.gate[:, 2])
            ffn_vector_dn_lo(k, f, dve, 10)
            ffn_vector_down(k, f, dve, 10, k.gate[:, 2])
            norm_vector_rstd(k, e, dve)
            dve.wait_ge(e.s_bc, 1)
            for t in range(DT):
                nc.vector.scalar_tensor_tensor(o[:, t], k.hT[:, t], k.vec[:, V_G + 24 + t:V_G + 25 + t], e.bc[:, :],
                                               ALU.mult, ALU.mult).then_inc(s_y, 1)

        @block.tensor
        def _(pe):
            norm_tensor_sums(k, n, pe)
            for s in range(2):
                ffn_tensor_gate_up(k, f, pe, 0, s, True, s_u=n.s_ul if s == 0 else None)

            def group(g, q):
                for s in range(2):
                    ffn_tensor_gate_up(k, f, pe, g, s, False)
                ffn_tensor_down(k, f, pe, g - 1, 1 - q)
            with pe.Fori(0, 4) as it:
                group(it * 2 + 1, 1)
                group(it * 2 + 2, 0)
            group(9, 1)
            group(10, 0)
            ffn_tensor_down(k, f, pe, 10, 0)
            norm_tensor_sums(k, e, pe)


def _constants():
    const = np.zeros((P, C_END), np.float32)
    const[:, C_ID:C_ID + P] = np.eye(P, dtype=np.float32)
    i, j = np.arange(P)[:, None], np.arange(P)[None, :]
    for n, hidden in ((M_UP, j <= i), (M_U, j > i), (M_L, i > j), (M_LP, i <= j)):
        const[:, C_MSK + n * P:C_MSK + (n + 1) * P] = np.where(hidden, np.float32(MASKED), np.float32(0))
    t = np.arange(T)
    end = np.arange(NCP) * CMP_STRIDE + CMP_LEN - 1
    end[NC_BLOCKS:] = 2 * T
    hidden = (end[None, :] > t[:, None]).reshape(QT, P, NCP).transpose(1, 0, 2).reshape(P, QT * NCP)
    const[:, C_MCA:C_MCC] = np.where(hidden, np.float32(MASKED), np.float32(0))
    const[:NC_BLOCKS, C_MCC:] = np.where(end[:NC_BLOCKS, None] > t[None, :], np.float32(MASKED), np.float32(0))
    aug = np.zeros((AUG_ROWS, A_END), np.float32)
    aug[0, A_KPOS:A_KPOS + T] = t
    aug[0, A_CPOS:A_CPOS + NC_BLOCKS] = end[:NC_BLOCKS]
    for n, br in enumerate(BRANCHES):
        aug[ROW_M[br] - AUG0, A_IND + n] = 1.0
    aug[0, A_SLOPE:A_SLOPE + HEADS] = SLOPES
    rows = np.asarray(SLOPES, np.float32)[:, None] * t[None, :].astype(np.float32)
    cols = rows.reshape(HEADS, QT, P).transpose(2, 0, 1).reshape(P, HEADS * QT)
    return const, aug, rows, np.ascontiguousarray(cols)


def _tiles(w, per=P):
    kk, n = w.shape
    return np.ascontiguousarray(w.reshape(kk // P, P, n // per, per).transpose(2, 1, 0, 3))


def kernel(**inputs):
    import concourse.bacc as bacc
    from concourse.bass_utils import run_bass_kernel_spmd as run

    x = {n: np.asarray(v) for n, v in inputs.items()}
    cols = lambda v: v.reshape(-1, P).T
    w_in = x["w_in"][0]
    at = {"qn": 0, "kc": 512, "vc": 640, "ks": 768, "vs": 896, "kw": 1024, "vw": 1152, "gn": 1280, "qs": 1304,
          "kb": 1816, "vb": 1944, "gm": 2072}
    order = []
    for name in TILES_IN:
        if name == "gn":
            order.append(np.concatenate([at["gn"] + np.arange(24).reshape(HEADS, 3).T.reshape(-1),
                                         np.arange(P - 24)]))
        else:
            order.append(at[name[:2]] + P * int(name[2:] or 0) + np.arange(P))
    order += [at["gm"] + P * n + np.arange(P) for n in range(N_GATES)]
    chunk = lambda w: w[0].reshape(4, 4, 2 * DH, HID_C).transpose(0, 2, 1, 3)
    const, aug, rows, tcols = _constants()
    gu = lambda g, u: np.ascontiguousarray(np.stack([_tiles(x[g][0]), _tiles(x[u][0])], axis=2))
    arrays = dict(
        xT=x["x"][0].T,
        vec=np.concatenate([cols(x["b_ada"][0]), cols(x["g_ffn1"][0]), cols(x["g_mix"][0]), cols(x["g_ffn2"][0]),
                            cols(x["g_final"]), cols(x["c"][0])], axis=1),
        w_ada=x["w_ada"][0], gu1=gu("w1_gate", "w1_up"), dn1=x["w1_down"][0],
        gu2=gu("w2_gate", "w2_up"), dn2=x["w2_down"][0],
        win=_tiles(w_in[:, np.concatenate(order)]),
        cw1=np.concatenate([chunk(x["cmp_w1_k"]), chunk(x["cmp_w1_v"])]),
        cw2=np.stack([x[n][0].reshape(2, P, DH).transpose(1, 0, 2) for n in ("cmp_w2_k", "cmp_w2_v")], axis=1),
        cpos=np.stack([x[n][0].reshape(16, 2 * DH).T for n in ("cmp_pos_k", "cmp_pos_v")], axis=1),
        wup=np.stack([_tiles(x["w_up_a"][0]), _tiles(x["w_up_b"][0])], axis=2),
        wout=_tiles(x["w_out"][0]),
        sinks=x["sinks"].reshape(HEADS), const=const, aug=aug, slope_rows=rows, slope_cols=tcols)
    arrays = {n: np.ascontiguousarray(v) for n, v in arrays.items()}
    nc = bacc.Bacc("TRN2", target_bir_lowering=False, num_devices=1)
    a = Record()
    (a.xT, a.vec, a.w_ada, a.gu1, a.dn1, a.gu2, a.dn2, a.win, a.cw1, a.cw2, a.cpos, a.wup, a.wout, a.sinks, a.const, a.aug, a.slope_rows, a.slope_cols) = (
        nc.dram_tensor(f"in_{n}", v.shape, mybir.dt.from_np(v.dtype), kind="ExternalInput").ap()
        for n, v in arrays.items())
    a.out = nc.dram_tensor("out_T", (D, T), F32, kind="ExternalOutput").ap()
    build(nc, a)
    r = run(nc, [{f"in_{n}": v for n, v in arrays.items()}], core_ids=[0])
    return np.ascontiguousarray(r.results[0]["out_T"].T)[None]
```

```python
import math
from contextlib import ExitStack

import numpy as np

import concourse.bass as bass
from concourse import mybir

F32 = mybir.dt.float32
F32R = mybir.dt.float32r
I32 = mybir.dt.int32
ALU = mybir.AluOpType
ACT = mybir.ActivationFunctionType
AX = mybir.AxisListType

P = 128
D = 1024
DT = D // P
T = 512
QT = T // P
FF = 2816
FT = FF // P
GROUPS = FT // 2
DH = 64
HEADS = 8
KV = 2
REP = HEADS // KV
CMP_LEN, CMP_STRIDE = 32, 16
NC_BLOCKS = (T - CMP_LEN) // CMP_STRIDE + 1
NCP = NC_BLOCKS + 1
HID_C = 256
RMS_EPS = 1e-6
MASKED = -1e30
SCALE = DH ** -0.5
SLOPES = [2.0 ** (-8.0 * (h + 1) / HEADS) for h in range(HEADS)]

TILES_IN = ["kc", "vc", "qn0", "qn1", "qn2", "qn3", "ks", "vs", "kw", "vw",
            "gn", "vb", "kb", "qs0", "qs1", "qs2", "qs3"]
FIRST_STEPS = [(s, kt) for half in range(2) for s in range(2) for kt in range(4 * half, 4 * half + 4)]
N_IRREG = len(TILES_IN)
N_GATES = 16
C_ID, C_MSK, C_MCA, C_MCC = 0, 128, 640, 768
C_END = C_MCC + T
M_UP, M_U, M_L, M_LP = range(4)
V_BADA, V_G, V_C, V_END = 0, 72, 104, 112
AUG0 = 64
AUG_ROWS = 35
BRANCHES = ("cmp", "win", "slc", "swa")
A_KPOS, A_CPOS, A_IND, A_SLOPE = 0, T, T + NCP, T + NCP + 4
A_END = A_SLOPE + HEADS
ROW_M = {"cmp": 96, "win": 97, "slc": 98, "swa": 96}


class Record:
    pass


def counter():
    n = [0]

    def step(by=1):
        n[0] += by
        return n[0]
    step.now = lambda: n[0]
    return step


def split_terms(hi_a, lo_a, hi_b, lo_b):
    return ((hi_a, hi_b), (hi_a, lo_b), (lo_a, hi_b))


def build(nc, a):
    with ExitStack() as ctx:
        k = Record()
        k.nc, k.a = nc, a
        base = -(-nc.sbuf_base // 64) * 64
        X = 56 * 1024

        def at(name, shape, dt, off):
            return nc.alloc_sbuf_tensor_at(name, shape, dt, offset=base + int(off))
        sems = {}

        def sem(name):
            if name not in sems:
                sems[name] = nc.alloc_semaphore(name)
            return sems[name]

        def clear_semaphores(keep):
            done = [name for name in sems if not name.startswith(keep)]
            nc.clear_and_free_semaphores([sems.pop(name) for name in done])
            nc.all_engine_barrier()
        k.at, k.sem, k.X = at, sem, X
        k.bank = [ctx.enter_context(nc.psum_tensor(f"bank{i}", [P, 512], F32)) for i in range(8)]
        K = 1024
        k.hT = at("hT", [P, DT, T], F32, 0)
        k.uh = at("u_hi", [P, DT, T], F32R, 16 * K)
        k.ul = at("u_lo", [P, DT, T], F32R, 32 * K)
        c0 = 48 * K
        k.vec = at("vec", [P, V_END], F32, c0)
        k.mod = at("mod", [P, 72], F32, c0 + 512)
        k.gain = at("gain", [P, 3, DT], F32, c0 + 1024)
        k.gate = at("gate", [P, 3, DT], F32, c0 + 1024 + 128)
        k.csil = at("csil", [P, DT], F32, c0 + 1280)
        k.stat = at("stat", [P, 4, QT], F32, c0 + 1344)
        k.rstd = at("rstd", [P, QT], F32, c0 + 1408)
        k.ones = at("ones", [P, 1], F32, c0 + 1472)
        k.onesR = at("ones_r", [P, 2], F32R, c0 + 1504)
        k.warm = at("table_warmer", [P, 1], F32, c0 + 1440)
        k.idF = at("identF", [P, P], F32, c0 + 1536)
        k.idR = at("identR", [P, P], F32R, c0 + 2048)
        k.msk = at("masks", [P, 4, P], F32R, c0 + 2560)
        k.mca = at("mask_cA", [P, QT, NCP], F32R, c0 + 4608)
        k.mcc = at("mask_cC", [P, T], F32R, c0 + 5120)
        k.hT_spill = nc.dram_tensor("h_spill", (D, T), F32, kind="Internal").ap()
        k.fac = nc.dram_tensor("factors", (4, HEADS * T), F32, kind="Internal").ap()

        ffn1, m = ffn_buffers(k, "f1", a.gu1, a.dn1), mixer_buffers(k)
        norm2 = norm_buffers(k, 2, X, X + 8 * K, X, banks=(2, 3))
        startup_and_ffn1(k, ffn1, m, norm2)
        clear_semaphores(keep=("w_", "aux", "n2_"))
        s = attention_buffers(k, m)
        projections(k, m, norm2, s)
        ffn2 = ffn_buffers(k, "f2", a.gu2, a.dn2)
        norm3 = norm_buffers(k, 3, X + 106 * K, X + 104 * K, X + 61 * K)
        g = merge_buffers(k)
        attention(k, m, s, g)
        merge(k, m, g, s, ffn2, norm3)
        ffn2_and_output(k, ffn2, norm3)


def norm_buffers(k, n, off_sq, off_sum, off, banks=(4, 5)):
    s, at = Record(), k.at
    s.sq = at(f"sq{n}", [P, 4, T], F32, off_sq)
    s.sum = at(f"sq_sum{n}", [P, T], F32, off_sum)
    s.xn = at(f"xn{n}", [P, 3, T], F32, off)
    s.u32 = at(f"u32_{n}", [P, 3, T], F32, off + 6144)
    s.s_h, s.s_sq, s.s_sum = k.sem(f"n{n}_h"), k.sem(f"n{n}_sq"), k.sem(f"n{n}_sum")
    s.s_sqmm, s.s_chain, s.s_rstd = k.sem(f"n{n}_sqmm"), k.sem(f"n{n}_chain"), k.sem(f"n{n}_rstd")
    s.s_bc, s.s_xn, s.s_u32, s.s_ul = k.sem(f"n{n}_bc"), k.sem(f"n{n}_xn"), k.sem(f"n{n}_u32"), k.sem(f"n{n}_ul")
    s.ss = k.bank[banks[0]]
    s.bc = k.bank[banks[1]]
    return s


def norm_scalar_squares(k, s, act, s_ready=None, before=0, tiles=range(DT)):
    for t in tiles:
        if s_ready is not None:
            act.wait_ge(s_ready, before + t + 1)
        if t >= 4:
            act.wait_ge(s.s_sum, max(1, t - 4))
        k.nc.scalar.activation(s.sq[:, t % 4], k.hT[:, t], ACT.Square).then_inc(s.s_sq, 1)


def norm_vector_sum(k, s, dve, t):
    dve.wait_ge(s.s_sq, t + 1)
    if t > 1:
        dve.wait_ge(s.s_sum, t - 1)
    k.nc.vector.tensor_tensor(s.sum[:, :], s.sq[:, 0] if t == 1 else s.sum[:, :], s.sq[:, t % 4],
                              ALU.add).then_inc(s.s_sum, 1)


def norm_tensor_sums(k, s, pe):
    pe.wait_ge(s.s_sum, DT - 1)
    for q in range(QT):
        mm = k.nc.tensor.matmul(s.ss[:, q:q + 1], s.sum[:, q * P:(q + 1) * P], k.ones[:, :], start=True, stop=True)
    mm.then_inc(s.s_sqmm, 1)


def norm_tensor_broadcast(k, s, pe):
    pe.wait_ge(s.s_rstd, 1)
    for q in range(QT):
        mm = k.nc.tensor.matmul(s.bc[:, q * P:(q + 1) * P], k.rstd[:, q:q + 1].to_broadcast([P, P]), k.idF[:, :],
                                start=True, stop=True)
    mm.then_inc(s.s_bc, 1)


def norm_vector_rstd(k, s, dve):
    v, i, half, y = (k.stat[:, j] for j in range(4))
    V = k.nc.vector
    n = counter()

    def then(ins):
        ins.then_inc(s.s_chain, 1)
        dve.wait_ge(s.s_chain, n())
    dve.wait_ge(s.s_sqmm, 1)
    then(V.tensor_scalar(v, s.ss[:, 0:QT], 1.0 / D, RMS_EPS, ALU.mult, ALU.add))
    then(V.tensor_scalar(i.bitcast(I32), v.bitcast(I32), 1, None, ALU.arith_shift_right))
    then(V.tensor_scalar(y.bitcast(I32), i.bitcast(I32), -1.0, float(0x5F3759DF), ALU.mult, ALU.add))
    then(V.tensor_scalar(v, v, -0.5, None, ALU.mult))
    for step in range(3):
        then(V.tensor_tensor(half, v, y, ALU.mult))
        then(V.tensor_tensor(half, half, y, ALU.mult))
        if step < 2:
            then(V.scalar_tensor_tensor(y, half, 1.5, y, ALU.add, ALU.mult))
    V.scalar_tensor_tensor(k.rstd[:, :], half, 1.5, y, ALU.add, ALU.mult).then_inc(s.s_rstd, 1)


def norm_vector_modulate(k, s, dve, tiles=range(DT)):
    V = k.nc.vector
    dve.wait_ge(s.s_bc, 1)

    def low(t):
        dve.wait_ge(s.s_u32, t + 1)
        V.tensor_tensor(k.ul[:, t], s.u32[:, t % 3], k.uh[:, t].bitcast(F32), ALU.subtract).then_inc(s.s_ul, 1)
    for t in tiles:
        if t >= 3:
            dve.wait_ge(s.s_u32, t - 2)
        V.tensor_tensor(s.xn[:, t % 3], k.hT[:, t], s.bc[:, :], ALU.mult).then_inc(s.s_xn, 1)
        if t > tiles[0]:
            low(t - 1)
    low(tiles[-1])


def norm_scalar_modulate(k, s, act, A, B, tiles=range(DT)):
    for t in tiles:
        act.wait_ge(s.s_xn, t + 1)
        k.nc.scalar.activation(k.uh[:, t], s.xn[:, t % 3], ACT.Identity, bias=B[:, t:t + 1], scale=A[:, t:t + 1])
        if t >= 3:
            act.wait_ge(s.s_ul, t - 2)
        k.nc.scalar.activation(s.u32[:, t % 3], s.xn[:, t % 3], ACT.Identity, bias=B[:, t:t + 1],
                               scale=A[:, t:t + 1]).then_inc(s.s_u32, 1)


def ffn_buffers(k, p, gu, dn):
    f, at, X = Record(), k.at, k.X
    K = 1024
    f.gu, f.dn = gu, dn.rearrange("(f p) n -> f p n", p=P)
    f.rgu = at(p + "_raw_gu", [P, 2, 2, DT, P], F32, X)
    f.rdn = at(p + "_raw_dn", [P, 2, D], F32, X + 16 * K)
    f.guh = at(p + "_gu_hi", [P, 2, 2, DT, P], F32R, X + 24 * K)
    f.gul = at(p + "_gu_lo", [P, 2, 2, DT, P], F32R, X + 40 * K)
    f.dnh = at(p + "_dn_hi", [P, 2, D], F32R, X + 56 * K)
    f.dnl = at(p + "_dn_lo", [P, 2, D], F32R, X + 64 * K)
    f.hidh = at(p + "_hid_hi", [P, 4, T], F32R, X + 72 * K)
    f.hidl = at(p + "_hid_lo", [P, 4, T], F32R, X + 80 * K)
    f.sil = at(p + "_sil", [P, 2, T], F32, X + 88 * K)
    f.hid = at(p + "_hid", [P, 2, T], F32, X + 92 * K)

    def pair(name):
        return [k.sem(f"{p}_{name}{s}") for s in range(2)]
    f.s_raw_gu, f.s_raw_dn, f.s_gu_hi = pair("raw_gu_"), pair("raw_dn_"), pair("gu_hi_")
    f.s_gu_lo, f.s_gate, f.s_up = pair("gu_lo_"), pair("gate_"), pair("up_")
    f.s_sil, f.s_hid, f.s_hid_hi = pair("sil_"), pair("hid_"), pair("hid_hi_")
    f.s_hid_lo = pair("hid_lo_")
    f.s_dn_hi, f.s_dn_lo = k.sem(p + "_dn_hi"), k.sem(p + "_dn_lo")
    f.s_dn_mm, f.s_bank = k.sem(p + "_dn_mm"), k.sem(p + "_dn_bank_free")
    f.gb, f.ub, f.db = k.bank[0:2], k.bank[2:4], k.bank[4:8]
    return f


def ffn_load_gu(k, f, sp, g, s):
    sp.dma_start(f.rgu[:, s], f.gu[g * 2 + s]).then_inc(f.s_raw_gu[s], 16)


def ffn_load_dn(k, f, sp, g, s):
    sp.dma_start(f.rdn[:, s], f.dn[g * 2 + s]).then_inc(f.s_raw_dn[s], 16)


def ffn_sync_gu(k, f, sp, g):
    for s in range(2):
        sp.wait_ge(f.s_gu_lo[s], g)
        ffn_load_gu(k, f, sp, g, s)


def ffn_sync_dn(k, f, sp, g):
    for s in range(2):
        sp.wait_ge(f.s_dn_lo, g * 2 - 1 + s)
        ffn_load_dn(k, f, sp, g, s)


def load_table(k, act, function):
    k.nc.scalar.activation(k.warm[:, :], k.csil[:, 0:1], function)


def ffn_scalar_gu_hi(k, f, act, g, s):
    act.wait_ge(f.s_raw_gu[s], (g + 1) * 16)
    k.nc.scalar.activation(f.guh[:, s], f.rgu[:, s], ACT.Copy).then_inc(f.s_gu_hi[s], 1)


def ffn_vector_gu_lo(k, f, dve, g, s):
    dve.wait_ge(f.s_gu_hi[s], g + 1)
    k.nc.vector.tensor_tensor(f.gul[:, s], f.rgu[:, s], f.guh[:, s].bitcast(F32),
                              ALU.subtract).then_inc(f.s_gu_lo[s], 1)


def ffn_down_parts(k, f, last):
    if not last:
        return f.dnh, f.dnl
    return [x[:, 0].rearrange("p h k c -> p (h k c)").rearrange("p (s d) -> p s d", s=2) for x in (f.guh, f.gul)]


def ffn_scalar_dn_hi(k, f, act, g, last=False):
    hi, _ = ffn_down_parts(k, f, last)
    for s in range(2):
        act.wait_ge(f.s_raw_dn[s], (g + 1) * 16)
        k.nc.scalar.activation(hi[:, s], f.rdn[:, s], ACT.Copy).then_inc(f.s_dn_hi, 1)


def ffn_vector_dn_lo(k, f, dve, g, last=False):
    hi, lo = ffn_down_parts(k, f, last)
    for s in range(2):
        dve.wait_ge(f.s_dn_hi, g * 2 + 1 + s)
        k.nc.vector.tensor_tensor(lo[:, s], f.rdn[:, s], hi[:, s].bitcast(F32),
                                  ALU.subtract).then_inc(f.s_dn_lo, 1)


def ffn_scalar_group(k, f, act, g, q, first=False, last=False):
    A = k.nc.scalar
    for s in range(2):
        act.wait_ge(f.s_gate[s], g + 1)
        if not first:
            act.wait_ge(f.s_hid[s], g)
        A.activation(f.sil[:, s], f.gb[s][:, :], ACT.Silu).then_inc(f.s_sil[s], 1)
        if s == 0 and not first:
            ffn_scalar_dn_hi(k, f, act, g - 1)
        if not last:
            act.wait_ge(f.s_up[s], g + 1)
            ffn_scalar_gu_hi(k, f, act, g + 1, s)
        act.wait_ge(f.s_hid[s], g + 1)
        A.activation(f.hidh[:, q * 2 + s], f.hid[:, s], ACT.Copy).then_inc(f.s_hid_hi[s], 1)


def ffn_vector_hidden(k, f, dve, g, q, s, split_next):
    V = k.nc.vector
    dve.wait_ge(f.s_sil[s], g + 1)
    dve.wait_ge(f.s_up[s], g + 1)
    V.tensor_tensor(f.hid[:, s], f.sil[:, s], f.ub[s][:, :], ALU.mult).then_inc(f.s_hid[s], 1)
    if split_next:
        ffn_vector_gu_lo(k, f, dve, g + 1, s)
    dve.wait_ge(f.s_hid_hi[s], g + 1)
    V.tensor_tensor(f.hidl[:, q * 2 + s], f.hid[:, s], f.hidh[:, q * 2 + s].bitcast(F32),
                    ALU.subtract).then_inc(f.s_hid_lo[s], 1)


def ffn_vector_down(k, f, dve, g, gate, tiles=range(DT), norm=None):
    for m in tiles:
        dve.wait_ge(f.s_dn_mm, g * 8 + m + 1)
        k.nc.vector.scalar_tensor_tensor(k.hT[:, m], f.db[m % 4][:, :], gate[:, m:m + 1], k.hT[:, m],
                                         ALU.mult, ALU.add).then_inc(f.s_bank, 1)
        if norm is not None and m >= 2:
            norm_vector_sum(k, norm, dve, m - 1)
            if m == DT - 1:
                norm_vector_sum(k, norm, dve, m)


def ffn_tensor_first(k, f, pe, s_u, steps):
    for s, kt in steps:
        pe.wait_ge(s_u, kt + 1)
        if kt == 0:
            pe.wait_ge(f.s_gu_lo[s], 1)
        for part, (bank, s_done) in enumerate(((f.gb[s], f.s_gate[s]), (f.ub[s], f.s_up[s]))):
            for j, (w, x) in enumerate(split_terms(f.guh[:, s, part, kt], f.gul[:, s, part, kt],
                                                   k.uh[:, kt], k.ul[:, kt])):
                mm = k.nc.tensor.matmul(bank[:, :], w, x, start=(kt == 0 and j == 0),
                                        stop=(kt == DT - 1 and j == 2))
            if kt == DT - 1:
                mm.then_inc(s_done, 1)


def ffn_tensor_gate_up(k, f, pe, g, s, between=None):
    for half, (bank, s_read, s_done) in enumerate(((f.gb[s], f.s_sil[s], f.s_gate[s]),
                                                   (f.ub[s], f.s_hid[s], f.s_up[s]))):
        if half == 0:
            pe.wait_ge(f.s_gu_lo[s], g + 1)
        pe.wait_ge(s_read, g)
        for kt in range(DT):
            for j, (w, x) in enumerate(split_terms(f.guh[:, s, half, kt], f.gul[:, s, half, kt],
                                                   k.uh[:, kt], k.ul[:, kt])):
                mm = k.nc.tensor.matmul(bank[:, :], w, x, start=(kt == 0 and j == 0),
                                        stop=(kt == DT - 1 and j == 2))
            if kt == DT - 1:
                mm.then_inc(s_done, 1)
            if between is not None:
                between(half * DT + kt)


def ffn_tensor_down(k, f, pe, g, q, last=False):
    hi, lo = ffn_down_parts(k, f, last)
    pe.wait_ge(f.s_dn_lo, g * 2 + 2)
    for s in range(2):
        pe.wait_ge(f.s_hid_lo[s], g + 1)
    for m in range(DT):
        pe.wait_ge(f.s_bank, g * 8 + m + 1)
        for s in range(2):
            w = slice(m * P, (m + 1) * P)
            for j, (x, y) in enumerate(split_terms(hi[:, s, w], lo[:, s, w],
                                                   f.hidh[:, q * 2 + s], f.hidl[:, q * 2 + s])):
                mm = k.nc.tensor.matmul(f.db[m % 4][:, :], x, y, start=(s == 0 and j == 0),
                                        stop=(s == 1 and j == 2))
        mm.then_inc(f.s_dn_mm, 1)


def startup_and_ffn1(k, f, m, n2):
    nc, a, X, K = k.nc, k.a, k.X, 1024
    n = norm_buffers(k, 1, X + 88 * K, X + 74 * K, X + 61 * K)
    acc2 = k.at("ada_acc2", [P, 6 * D], F32, X + 96 * K)
    ring = k.at("ada_ring", [P, 4, 1536], F32, X + 120 * K)
    acc2h = k.at("ada_acc2_hi", [P, 6 * D], F32R, X + 120 * K)
    acc2l = k.at("ada_acc2_lo", [P, 6 * D], F32R, X + 96 * K)
    accg = k.at("ada_acc_gt1", [P, D], F32, X + 144 * K)
    acc1 = k.at("ada_acc1", [P, 2, D], F32, X + 80 * K)
    stage = k.at("const_stage", [P, C_END - C_MSK], F32, X + 56 * K)
    w_ada = a.w_ada.rearrange("(k p) n -> k p n", p=P)
    S = k.sem
    s_x = [S(f"x_in{half}") for half in range(2)]
    s_vec, s_const, s_idf = S("vec_in"), S("const_in"), S("identF_in")
    s_raw = [S(f"ada_raw{j}") for j in range(4)]
    s_used = [S(f"ada_used{j}") for j in range(4)]
    s_csil, s_fill, s_ones, s_const_ready = S("csil"), S("ada_zero"), S("ones"), S("const_ready")
    s_mm1, s_mmg, s_mm2, s_mod, s_mod2 = S("ada_mm1"), S("ada_mmg"), S("ada_mm2"), S("mod1"), S("mod2_read")
    s_acch, s_accl = S("ada_acc2_hi_done"), S("ada_acc2_lo_done")
    pieces = [(kt, half) for half in (0, 1) for kt in range(DT)] + [(kt, 2) for kt in range(DT)]
    HD = D // 2
    DIRECT = 3

    def half_of(x, half):
        return x.rearrange("p (c n) -> p c n", n=D)[:, :, half * HD:(half + 1) * HD]

    with nc.Block() as block:
        @block.sync
        def _(sp):
            sp.dma_start(k.vec[:, :], a.vec).then_inc(s_vec, 16)
            xT = a.xT.rearrange("(t p) n -> p t n", p=P)
            for i, (kt, c) in enumerate(pieces):
                if i in (2, 4):
                    half = i // 2 - 1
                    sp.dma_start(k.hT[:, 4 * half:4 * half + 4], xT[:, 4 * half:4 * half + 4]).then_inc(s_x[half], 16)
                if i == 8:
                    for s in range(2):
                        ffn_load_gu(k, f, sp, 0, s)
                j = i % 4
                if i >= 4:
                    sp.wait_ge(s_used[j], i // 4)
                if c == 2:
                    sp.dma_start(ring[:, j, 0:D], w_ada[kt, :, c * D:(c + 1) * D]).then_inc(s_raw[j], 16)
                else:
                    sp.dma_start(ring[:, j, 0:D].rearrange("p (c n) -> p c n", c=2),
                                 half_of(w_ada[kt, :, 0:2 * D], c)).then_inc(s_raw[j], 16)
                if i == 15:
                    ffn_sync_gu(k, f, sp, 1)
            for s in range(2):
                ffn_load_dn(k, f, sp, 0, s)

            def group(g):
                ffn_sync_gu(k, f, sp, g + 1)
                for j in range(4):
                    sp.wait_ge(s_used[j], g + 5)
                    sp.dma_start(ring[:, j], w_ada[g - 1, :, 3 * D + j * 1536:3 * D + (j + 1) * 1536])\
                        .then_inc(s_raw[j], 16)
                ffn_sync_dn(k, f, sp, g)
            with sp.Fori(0, 4) as it:
                group(it * 2 + 1)
                group(it * 2 + 2)
            ffn_sync_gu(k, f, sp, 10)
            ffn_sync_dn(k, f, sp, 9)
            ffn_sync_dn(k, f, sp, 10)
            sp.wait_ge(s_mm2, 1)
            sp.dma_start(m.aug[AUG0:AUG0 + AUG_ROWS, :], a.aug).then_inc(m.s_aux, 16)
            sp.dma_start(m.cpos[:, :, :], a.cpos).then_inc(m.s_aux, 16)
            for i in range(3):
                projection_load(k, m, sp, i)

        @block.gpsimd
        def _(pool):
            nc.gpsimd.memset(k.ones[:, :], 1.0).then_inc(s_ones, 1)
            nc.gpsimd.memset(k.onesR[:, :].bitcast(F32), 1.0).then_inc(s_ones, 1)
            nc.gpsimd.memset(acc2[:, :], 0.0).then_inc(s_fill, 1)

        @block.scalar
        def _(act):
            act.dma_start(k.idF[:, :], a.const[:, C_ID:C_ID + P]).then_inc(s_idf, 16)
            act.wait_ge(s_vec, 16)
            nc.scalar.activation(k.csil[:, :], k.vec[:, V_C:V_END], ACT.Silu).then_inc(s_csil, 1)
            for half in range(2):
                act.wait_ge(s_x[half], 16)
                norm_scalar_squares(k, n, act, tiles=range(4 * half, 4 * half + 4))
            for s in range(2):
                ffn_scalar_gu_hi(k, f, act, 0, s)
            act.dma_start(stage[:, :], a.const[:, C_MSK:C_END]).then_inc(s_const, 16)
            act.wait_ge(s_mod, 2)
            A, B = k.gain[:, 0], k.mod[:, 0:8]
            norm_scalar_modulate(k, n, act, A, B, range(0, 4))
            act.wait_ge(s_const, 16)
            nc.scalar.activation(k.idR[:, :], k.idF[:, :], ACT.Copy)
            nc.scalar.activation(k.msk[:, :, :], stage[:, 0:4 * P].rearrange("p (m c) -> p m c", c=P), ACT.Copy)
            nc.scalar.activation(k.mca[:, :, :], stage[:, C_MCA - C_MSK:C_MCC - C_MSK]
                                 .rearrange("p (m c) -> p m c", c=NCP), ACT.Copy)
            nc.scalar.activation(k.mcc[:, :], stage[:, C_MCC - C_MSK:], ACT.Copy).then_inc(s_const_ready, 1)
            act.wait_ge(s_mod, 4)
            norm_scalar_modulate(k, n, act, A, B, range(4, DT))
            load_table(k, act, ACT.Silu)
            ffn_scalar_group(k, f, act, 0, 0, first=True)
            with act.Fori(0, 4) as it:
                ffn_scalar_group(k, f, act, it * 2 + 1, 1)
                ffn_scalar_group(k, f, act, it * 2 + 2, 0)
            for j in range(4):
                act.wait_ge(s_used[j], 14)
            for half in range(2):
                part = slice(half * 3 * D, (half + 1) * 3 * D)
                nc.scalar.activation(acc2h[:, part], acc2[:, part], ACT.Copy).then_inc(s_acch, 1)
            ffn_scalar_group(k, f, act, 9, 1)
            ffn_scalar_group(k, f, act, 10, 0, last=True)
            ffn_scalar_dn_hi(k, f, act, 10, last=True)
            for i in range(2):
                projection_w_hi(k, m, act, i)
            norm_scalar_squares(k, n2, act, f.s_bank, 4 + 8 * (GROUPS - 1))
            projection_w_hi(k, m, act, 2)

        @block.vector
        def _(dve):
            V = nc.vector

            def piece(i):
                kt, c = pieces[i]
                j = i % 4
                acc = accg[:, :] if c == 2 else half_of(acc1[:, :, :].rearrange("p c n -> p (c n)"), c)
                src = ring[:, j, 0:D] if c == 2 else ring[:, j, 0:D].rearrange("p (c n) -> p c n", c=2)
                dve.wait_ge(s_raw[j], 16 * (i // 4 + 1))
                col = k.csil[:, kt:kt + 1]
                if i in (0, 8 + DIRECT, 16):
                    V.tensor_scalar(acc, src, col, None, ALU.mult).then_inc(s_used[j], 1)
                else:
                    dve.wait_ge(s_used[(i - 1) % 4], (i - 1) // 4 + 1)
                    V.scalar_tensor_tensor(acc, src, col, acc, ALU.mult, ALU.add).then_inc(s_used[j], 1)

            def vectors(half):
                sh, sc = (slice(c * 8 + half * 4, c * 8 + half * 4 + 4) for c in (0, 1))
                dve.wait_ge(s_mm1, half + 1)
                both = lambda x: x.rearrange("p (c n) -> p c n", c=2)[:, :, half * 4:half * 4 + 4]
                V.tensor_tensor(both(k.mod[:, 0:16]), both(k.bank[6 + half][:, 0:16]),
                                both(k.vec[:, V_BADA:V_BADA + 16]), ALU.add).then_inc(s_mod, 1)
                dve.wait_ge(s_mod, half * 2 + 1)
                V.scalar_tensor_tensor(k.gain[:, 0, half * 4:half * 4 + 4], k.mod[:, sc], 1.0,
                                       k.vec[:, V_G + half * 4:V_G + half * 4 + 4], ALU.add, ALU.mult).then_inc(s_mod, 1)
            dve.wait_ge(s_csil, 1)
            for i in range(8):
                piece(i)
                for t in {3: (1, 2), 4: (3,), 5: (4, 5), 6: (6, 7)}.get(i, ()):
                    norm_vector_sum(k, n, dve, t)
            norm_vector_rstd(k, n, dve)
            vectors(0)
            ffn_vector_gu_lo(k, f, dve, 0, 0)
            norm_vector_modulate(k, n, dve, range(0, 2))
            norm_vector_modulate(k, n, dve, range(2, 4))
            ffn_vector_gu_lo(k, f, dve, 0, 1)
            for i in range(8 + DIRECT, 16):
                piece(i)
            vectors(1)
            norm_vector_modulate(k, n, dve, range(4, DT))
            for i in range(16, 20):
                piece(i)
            for s in range(2):
                ffn_vector_hidden(k, f, dve, 0, 0, s, split_next=True)
            for i in range(20, 24):
                piece(i)
            dve.wait_ge(s_mmg, 1)
            V.tensor_tensor(k.mod[:, 16:24], k.bank[6][:, 0:8], k.vec[:, 16:24], ALU.add).then_inc(s_mod, 1)
            dve.wait_ge(s_mod, 5)
            V.tensor_scalar(k.gate[:, 0], k.mod[:, 16:24], 0.5, None, ALU.mult).then_inc(f.s_bank, 4)
            dve.wait_ge(f.s_bank, 4)
            dve.wait_ge(s_fill, 1)

            def group(g, q, ada):
                def part(j):
                    if ada:
                        acc = acc2[:, j * 1536:(j + 1) * 1536]
                        dve.wait_ge(s_raw[j], (g + 6) * 16)
                        dve.wait_ge(s_used[j], g + 5)
                        V.scalar_tensor_tensor(acc, ring[:, j], k.csil[:, bass.ds(g - 1, 1)], acc,
                                               ALU.mult, ALU.add).then_inc(s_used[j], 1)
                ffn_vector_dn_lo(k, f, dve, g - 1)
                ffn_vector_hidden(k, f, dve, g, q, 0, split_next=True)
                for j in range(3):
                    part(j)
                ffn_vector_hidden(k, f, dve, g, q, 1, split_next=False)
                ffn_vector_down(k, f, dve, g - 1, k.gate[:, 0], range(4))
                part(3)
                ffn_vector_down(k, f, dve, g - 1, k.gate[:, 0], range(4, DT))
                ffn_vector_gu_lo(k, f, dve, g + 1, 1)
            with dve.Fori(0, 4) as it:
                group(it * 2 + 1, 1, True)
                group(it * 2 + 2, 0, True)
            for half in range(2):
                part = slice(half * 3 * D, (half + 1) * 3 * D)
                dve.wait_ge(s_acch, half + 1)
                V.tensor_tensor(acc2l[:, part], acc2[:, part], acc2h[:, part].bitcast(F32), ALU.subtract)\
                    .then_inc(s_accl, 1)
            group(9, 1, False)
            ffn_vector_dn_lo(k, f, dve, 9)
            ffn_vector_hidden(k, f, dve, 10, 0, 0, False)
            dve.wait_ge(s_mm2, 1)
            V.tensor_tensor(k.mod[:, 24:72], k.bank[4][:, 0:96].rearrange("p (m r) -> p m r", r=2)[:, :, 0],
                            k.vec[:, 24:72], ALU.add).then_inc(s_mod2, 1)
            dve.wait_ge(s_mod2, 1)
            V.scalar_tensor_tensor(k.gain[:, 1], k.mod[:, 32:40], 1.0, k.vec[:, V_G + 8:V_G + 16], ALU.add, ALU.mult)
            V.scalar_tensor_tensor(k.gain[:, 2], k.mod[:, 56:64], 1.0, k.vec[:, V_G + 16:V_G + 24], ALU.add, ALU.mult)
            V.tensor_copy(k.gate[:, 1], k.mod[:, 40:48])
            V.tensor_scalar(k.gate[:, 2], k.mod[:, 64:72], 0.5, None, ALU.mult)
            ffn_vector_hidden(k, f, dve, 10, 0, 1, False)
            ffn_vector_down(k, f, dve, 9, k.gate[:, 0], range(4))
            ffn_vector_dn_lo(k, f, dve, 10, last=True)
            projection_w_lo(k, m, dve, 0)
            ffn_vector_down(k, f, dve, 9, k.gate[:, 0], range(4, DT))
            projection_w_lo(k, m, dve, 1)
            ffn_vector_down(k, f, dve, 10, k.gate[:, 0], norm=n2)
            norm_vector_rstd(k, n2, dve)
            projection_w_lo(k, m, dve, 2)

        @block.tensor
        def _(pe):
            pe.wait_ge(s_ones, 2)
            pe.wait_ge(s_idf, 16)
            norm_tensor_sums(k, n, pe)

            def vectors(half):
                for j in range(4):
                    pe.wait_ge(s_used[j], 2 * half + 2)
                for c in range(2):
                    for t in range(half * 4, half * 4 + 4):
                        mm = nc.tensor.matmul(k.bank[6 + half][:, c * 8 + t:c * 8 + t + 1],
                                              acc1[:, c, t * P:(t + 1) * P], k.ones[:, :],
                                              start=(half == 0 and c == 0 and t == 0), stop=True, skip_group_check=True)
                mm.then_inc(s_mm1, 1)
            vectors(0)
            norm_tensor_broadcast(k, n, pe)
            for i in range(8, 8 + DIRECT):
                j, kt = i % 4, pieces[i][0]
                pe.wait_ge(s_raw[j], 16 * (i // 4 + 1))
                for c in range(2):
                    for t in range(4):
                        mm = nc.tensor.matmul(k.bank[7][:, c * 8 + 4 + t:c * 8 + 5 + t],
                                              ring[:, j, c * HD + t * P:c * HD + (t + 1) * P], k.csil[:, kt:kt + 1],
                                              start=(i == 8 and c == 0 and t == 0), stop=False, skip_group_check=True)
                mm.then_inc(s_used[j], 1)
            ffn_tensor_first(k, f, pe, n.s_ul, FIRST_STEPS[:6])
            vectors(1)
            ffn_tensor_first(k, f, pe, n.s_ul, FIRST_STEPS[6:])

            def group(g, q, gate=False):
                ffn_tensor_gate_up(k, f, pe, g, 0)
                if gate:
                    pe.wait_ge(s_used[3], 6)
                    for c in range(8):
                        mm = nc.tensor.matmul(k.bank[6][:, c:c + 1], accg[:, c * P:(c + 1) * P], k.ones[:, :],
                                              start=True, stop=True)
                    mm.then_inc(s_mmg, 1)
                ffn_tensor_gate_up(k, f, pe, g, 1)
                ffn_tensor_down(k, f, pe, g - 1, 1 - q)
            group(1, 1, gate=True)
            group(2, 0)
            with pe.Fori(1, 4) as it:
                group(it * 2 + 1, 1)
                group(it * 2 + 2, 0)
            group(9, 1)

            def vectors2(n):
                if n < 2 or n >= 14:
                    return
                if n == 2:
                    pe.wait_ge(s_accl, 2)
                    pe.wait_ge(f.s_bank, 4 + 72)
                for c in range(4 * (n - 2), 4 * (n - 2) + 4):
                    out = k.bank[4][:, 2 * c:2 * c + 2]
                    nc.tensor.matmul(out, acc2h[:, c * P:(c + 1) * P], k.onesR[:, :], start=True, stop=False)
                    mm = nc.tensor.matmul(out, acc2l[:, c * P:(c + 1) * P], k.onesR[:, :], start=False, stop=True)
                if n == 13:
                    mm.then_inc(s_mm2, 1)
            ffn_tensor_gate_up(k, f, pe, 10, 0, between=vectors2)
            ffn_tensor_gate_up(k, f, pe, 10, 1)
            pe.wait_ge(s_mod2, 1)
            ffn_tensor_down(k, f, pe, 9, 1)
            ffn_tensor_down(k, f, pe, 10, 0, last=True)
            norm_tensor_sums(k, n2, pe)
            norm_tensor_broadcast(k, n2, pe)


def mixer_buffers(k):
    m, at, X, K = Record(), k.at, k.X, 1024
    m.gates = at("gates", [P, N_GATES, T], F32, X)
    m.qn = at("q_nsa", [P, HEADS, T], F32R, X + 32 * K)
    m.qn2 = at("q_nsa_pair", [P, HEADS, T], F32R, X + 48 * K)
    m.qs = at("q_swa", [P, HEADS, T], F32R, 16 * K)
    m.qs2 = at("q_swa_pair", [P, HEADS, T], F32R, 32 * K)
    m.kk = at("k_rows", [P, 3, KV, T], F32R, X + 64 * K)
    m.kk2 = at("k_pair", [P, 3, KV, T], F32R, X + 76 * K)
    m.vh = at("v_hi", [P, 3, KV, QT, DH + 2], F32R, X + 88 * K)
    m.vl = at("v_lo", [P, 3, KV, QT, DH + 2], F32R, X + 88 * K + 6400)
    m.vT = at("v_T", [P, 2, T], F32, X + 101 * K)
    m.qsf = at("q_swa_f32", [P, 4, T], F32, X + 105 * K)
    c = X + 115 * K
    m.kc = at("kc_rows", [P, KV, NCP], F32R, c)
    m.kc2 = at("kc_pair", [P, KV, NCP], F32R, c + 256)
    m.vch = at("vc_hi", [P, KV, DH + 2], F32R, c + 512)
    m.vcl = at("vc_lo", [P, KV, DH + 2], F32R, c + 1088)
    m.cpos = at("cmp_pos", [P, 2, 16], F32, c + 1664)
    m.gs = at("nsa_gates", [3 * HEADS, T], F32, X + 118 * K)
    m.wh = [at(f"w_hi{j}", [P, D], F32R, X + o * K) for j, o in enumerate((120, 124, 16))]
    m.wl = [at(f"w_lo{j}", [P, D], F32R, X + o * K) for j, o in enumerate((128, 132, 20))]
    m.raw = at("w_raw", [P, 3, D], F32, X + 136 * K)
    m.aug = at("aug", [P, A_END], F32, X + 148 * K)
    NB = 16 * KV * NC_BLOCKS
    m.blk = at("blocks", [P, 2, NB], F32, X)
    m.blkh = at("blocks_hi", [P, 2, NB], F32R, X + 8 * K)
    m.blkl = at("blocks_lo", [P, 2, NB], F32R, X)
    g = X + 24 * K
    NG = KV * NC_BLOCKS
    m.cw2 = at("cmp_w2", [P, 2, 2, DH], F32, g)
    m.cw2h = at("cmp_w2_hi", [P, 2, 2, DH], F32R, g + 1024)
    m.cw2l = at("cmp_w2_lo", [P, 2, 2, DH], F32R, g + 2048)
    m.ge = at("gelu_tmp", [P, 4, 2, NG], F32, g + 3072)
    m.geh = at("gelu_hi", [P, 2, NG], F32R, g + 5120)
    m.gel = at("gelu_lo", [P, 2, NG], F32R, g + 5632)
    m.hid = at("cmp_hidden", [NG, HID_C], F32, g + 6144)
    m.items = stream_items()
    m.s_raw = [k.sem(f"w_raw{j}") for j in range(3)]
    m.s_hi, m.s_lo, m.s_item, m.s_aux = k.sem("w_hi"), k.sem("w_lo"), k.sem("w_item"), k.sem("aux_in")
    return m


def stream_items():
    chunks = [("ck", c) for c in range(4)] + [("cv", c) for c in range(4)]
    items = []
    for n, name in enumerate(TILES_IN):
        items.append(("in", name))
        if 2 <= n < 10:
            items.append(chunks[n - 2])
    return items


def projection_slot(m, i):
    n = len(m.items)
    slot_of = lambda j: j % 3 if j < n else (j - n + 1) % 2
    slot = slot_of(i)
    before = [j for j in range(i) if slot_of(j) == slot]
    return slot, (before[-1] if before else None)


def projection_load(k, m, sp, i):
    kind, x = m.items[i]
    source = k.a.win[TILES_IN.index(x)] if kind == "in" else k.a.cw1[x + (4 if kind == "cv" else 0)]
    sp.dma_start(m.raw[:, i % 3], source.rearrange("p k c -> p (k c)")).then_inc(m.s_raw[i % 3], 16)


def projection_w_hi(k, m, act, i):
    slot, before = projection_slot(m, i)
    act.wait_ge(m.s_raw[i % 3], 16 * (i // 3 + 1))
    if before is not None:
        act.wait_ge(m.s_item, before + 1)
    k.nc.scalar.activation(m.wh[slot][:, :], m.raw[:, i % 3], ACT.Copy).then_inc(m.s_hi, 1)


def projection_w_lo(k, m, dve, i):
    slot, _ = projection_slot(m, i)
    dve.wait_ge(m.s_hi, i + 1)
    k.nc.vector.tensor_tensor(m.wl[slot][:, :], m.raw[:, i % 3], m.wh[slot][:, :].bitcast(F32),
                              ALU.subtract).then_inc(m.s_lo, 1)


def projections(k, m, n2, s):
    nc, a, X, K = k.nc, k.a, k.X, 1024
    S = k.sem
    items = m.items
    N = len(items)
    kinds = [i[0] if i[0] != "in" else i[1][:2] for i in items]
    s_raw, s_lo, s_item, s_aux = m.s_raw, m.s_lo, m.s_item, m.s_aux
    s_act, s_dve = S("evac_act"), S("evac_dve")
    s_cw2 = S("cw2_in")
    s_spill, s_fill, s_kv0 = S("h_spilled"), S("kv_cleared"), S("rows_set")
    s_vt, s_vta, s_vtd = S("v_transposed"), S("v_hi_done"), S("v_lo_done")
    s_blkh, s_blkl = S("blocks_hi_done"), S("blocks_lo_done")
    s_w2h, s_w2l = S("cw2_hi"), S("cw2_lo")
    s_hid, s_hidt = S("cmp_hidden"), S("cmp_hidden_T")
    s_x, s_th, s_g, s_gh, s_gl = S("gelu_x"), S("gelu_tanh"), S("gelu_g"), S("gelu_hi_done"), S("gelu_lo_done")
    s_c2, s_c2a, s_c2d = S("cmp_out"), S("cmp_hi_done"), S("cmp_lo_done")
    ACT_KINDS = {"qs", "kb", "vb", "qn", "ks", "vs", "kw", "vw", "gn"}
    DVE_KINDS = {"kb", "qn", "kc", "vc", "ks", "kw"}
    act_after = [sum(x in ACT_KINDS for x in kinds[:i + 1]) for i in range(N)]
    dve_after = [sum(x in DVE_KINDS for x in kinds[:i + 1]) for i in range(N)]
    proj_items = [i for i in range(N) if items[i][0] == "in"]
    ring = (0, 1, 6, 7)
    bank_of = {i: ring[n % 4] for n, i in enumerate(proj_items)}
    bank_before = {i: (proj_items[n - 4] if n >= 4 else None) for n, i in enumerate(proj_items)}
    v_items = [i for i in range(N) if kinds[i] in ("vb", "vs", "vw")]
    v_branch = {"vb": 2, "vs": 1, "vw": 0}
    k_branch = {"kb": 2, "ks": 1, "kw": 0}
    cmp_end = {i: (0 if kinds[i] == "ck" else 1) for i in range(N) if items[i] in (("ck", 3), ("cv", 3))}

    def stages_beside_block(i):
        out = []
        if i >= 1 and kinds[i - 1] in ("kc", "vc"):
            out.append(("blocks", 0 if kinds[i - 1] == "kc" else 1))
        for stage, lag in (("turn", 1), ("second", 3)):
            if i >= lag and i - lag in cmp_end:
                out.append((stage, cmp_end[i - lag]))
        return out

    with nc.Block() as block:
        @block.sync
        def _(sp):
            sp.dma_start(k.hT_spill.rearrange("(t p) n -> p t n", p=P), k.hT[:, :, :]).then_inc(s_spill, 16)
            sp.dma_start(m.cw2[:, :, :, :], a.cw2).then_inc(s_cw2, 16)
            for i in range(3, N):
                sp.wait_ge(s_lo, i - 2)
                projection_load(k, m, sp, i)
            for j in range(N_GATES):
                sp.wait_ge(s_lo, N + j - 2)
                sp.dma_start(m.raw[:, (N + j) % 3], a.win[N_IRREG + j].rearrange("p k c -> p (k c)"))\
                    .then_inc(s_raw[(N + j) % 3], 16)
                for x in s.with_gates.get(j - 3, []):
                    if x[0] == "rows":
                        rows_out(k, m, s, sp, x[1])
            sp.wait_ge(s_spill, 16)

        @block.gpsimd
        def _(pool):
            G = nc.gpsimd
            G.memset(m.vh[:, :, :, :, :].bitcast(F32), 0.0).then_inc(s_fill, 1)
            G.memset(m.vl[:, :, :, :, :].bitcast(F32), 0.0)
            G.memset(m.vch[:, :, :].bitcast(F32), 0.0).then_inc(s_fill, 1)
            G.memset(m.vcl[:, :, :].bitcast(F32), 0.0)
            G.memset(m.kc[:, :, :].bitcast(F32), 0.0)
            G.memset(m.kc2[:, :, :].bitcast(F32), 0.0).then_inc(s_fill, 1)
            pool.wait_ge(s_fill, 2)
            G.memset(m.vh[:, :, :, :, DH:DH + 1].bitcast(F32), 1.0)
            G.memset(m.vch[:, :, DH:DH + 1].bitcast(F32), 1.0).then_inc(s_fill, 1)

        @block.scalar
        def _(act):
            A = nc.scalar
            rows = slice(AUG0, AUG0 + AUG_ROWS)

            def extra_rows(j):
                if j < HEADS:
                    A.activation(m.qn[rows, j], m.aug[rows, A_SLOPE + j:A_SLOPE + j + 1].to_broadcast([AUG_ROWS, T]),
                                 ACT.Copy)
                elif j < HEADS + 6:
                    b, g = (j - HEADS) // KV, (j - HEADS) % KV
                    A.activation(m.kk[rows, b, g], m.aug[rows, A_KPOS:A_KPOS + T], ACT.Identity,
                                 bias=m.aug[rows, A_IND + b + 1:A_IND + b + 2])
                else:
                    g = j - HEADS - 6
                    A.activation(m.kc[rows, g], m.aug[rows, A_CPOS:A_CPOS + NCP], ACT.Identity,
                                 bias=m.aug[rows, A_IND:A_IND + 1])

            norm_scalar_modulate(k, n2, act, k.gain[:, 1], k.mod[:, 24:32])
            act.wait_ge(s_aux, 32)
            act.wait_ge(s_fill, 4)
            for i in range(N):
                kind, bank = kinds[i], k.bank[bank_of.get(i, 0)]
                if i >= 1:
                    projection_w_hi(k, m, act, i + 2)
                if 2 <= i < 2 + N_GATES:
                    extra_rows(i - 2)
                if kind in ACT_KINDS:
                    act.wait_ge(s_item, i + 1)
                if kind == "qs":
                    A.activation(m.qsf[:, int(items[i][1][2])], bank[:, :], ACT.Copy, scale=SCALE).then_inc(s_act, 1)
                elif kind in ("kb", "ks", "kw"):
                    b = k_branch[kind]
                    for g in range(KV):
                        src = bank[g * DH:(g + 1) * DH, :]
                        A.activation(m.kk[0:DH, b, g], src, ACT.Copy)
                        ins = A.activation(m.kk2[0:DH, b, g], src, ACT.Copy)
                    ins.then_inc(s_act, 1)
                elif kind == "qn":
                    for r in range(2):
                        h, src = int(items[i][1][2]) * 2 + r, bank[r * DH:(r + 1) * DH, :]
                        A.activation(m.qn[0:DH, h], src, ACT.Copy, scale=SCALE)
                        ins = A.activation(m.qn2[DH:P, h], src, ACT.Copy, scale=SCALE)
                    ins.then_inc(s_act, 1)
                elif kind in ("vb", "vs", "vw"):
                    j = v_items.index(i)
                    if j >= 2:
                        act.wait_ge(s_vt, j - 1)
                    A.activation(m.vT[:, j % 2], bank[:, :], ACT.Copy).then_inc(s_act, 1)
                elif kind == "gn":
                    A.activation(m.gs[:, :], bank[0:3 * HEADS, :], ACT.Sigmoid).then_inc(s_act, 1)
                if i - 1 in v_items:
                    j = v_items.index(i - 1)
                    b = v_branch[kinds[i - 1]]
                    act.wait_ge(s_vt, j + 1)
                    for g in range(KV):
                        ins = A.activation(m.vh[:, b, g, :, 0:DH],
                                           k.bank[3][:, :].rearrange("p (t g d) -> p t g d", t=QT, g=KV)[:, :, g],
                                           ACT.Copy)
                    ins.then_inc(s_vta, 1)
                if i in cmp_end:
                    c = cmp_end[i]
                    act.wait_ge(s_item, i + 1)
                    if c == 1:
                        act.wait_ge(s_hidt, 1)
                    A.activation(m.hid[:, :], k.bank[4][0:KV * NC_BLOCKS, 0:HID_C], ACT.Copy).then_inc(s_hid, 1)
                for stage, c in stages_beside_block(i):
                    if stage == "blocks":
                        act.wait_ge(s_dve, dve_after[i - 1])
                        A.activation(m.blkh[:, c], m.blk[:, c], ACT.Copy).then_inc(s_blkh, 1)
                        if c == 0:
                            act.wait_ge(s_cw2, 16)
                            A.activation(m.cw2h[:, :, :, :], m.cw2[:, :, :, :], ACT.Copy).then_inc(s_w2h, 1)
                    elif stage == "turn":
                        act.wait_ge(s_x, 4 * c + 4)
                        A.activation(m.ge[:, 2], m.ge[:, 1], ACT.Tanh, scale=math.sqrt(2 / math.pi)).then_inc(s_th, 1)
                        act.wait_ge(s_g, c + 1)
                        A.activation(m.geh[:, :], m.ge[:, 3], ACT.Copy, scale=0.5).then_inc(s_gh, 1)
                    elif c == 0:
                        act.wait_ge(s_c2, 1)
                        src = k.bank[2][0:DH, 0:KV * NC_BLOCKS].rearrange("p (g n) -> p g n", g=KV)
                        A.activation(m.kc[0:DH, :, 0:NC_BLOCKS], src, ACT.Copy)
                        A.activation(m.kc2[0:DH, :, 0:NC_BLOCKS], src, ACT.Copy).then_inc(s_c2a, 1)
                    else:
                        act.wait_ge(s_c2, 2)
                        A.activation(m.vch[0:NC_BLOCKS, :, 0:DH],
                                     k.bank[2][0:NC_BLOCKS, 0:P].rearrange("p (g d) -> p g d", g=KV),
                                     ACT.Copy).then_inc(s_c2a, 1)
            for j in range(N_GATES):
                for x in s.with_gates.get(j, []):
                    if x[0] == "rows":
                        rows_scalar(k, s, act, x[1])
                if j + 2 < N_GATES:
                    projection_w_hi(k, m, act, N + j + 2)
                act.wait_ge(s_item, N + j + 1)
                A.activation(m.gates[:, j], k.bank[6 + j % 2][:, :], ACT.Sigmoid).then_inc(s_act, 1)

        @block.vector
        def _(dve):
            V = nc.vector
            norm_vector_modulate(k, n2, dve)
            for i in range(N):
                kind, bank = kinds[i], k.bank[bank_of.get(i, 0)]
                if i >= 1:
                    projection_w_lo(k, m, dve, i + 2)
                if kind in ("kb", "ks", "kw"):
                    dve.wait_ge(s_act, act_after[i])
                    b = k_branch[kind]
                    for g in range(KV):
                        ins = V.tensor_tensor(m.kk2[DH:P, b, g], bank[g * DH:(g + 1) * DH, :],
                                              m.kk[0:DH, b, g].bitcast(F32), ALU.subtract)
                    ins.then_inc(s_dve, 1)
                elif kind == "qn":
                    dve.wait_ge(s_act, act_after[i])
                    for r in range(2):
                        h = int(items[i][1][2]) * 2 + r
                        ins = V.scalar_tensor_tensor(m.qn2[0:DH, h], bank[r * DH:(r + 1) * DH, :], SCALE,
                                                     m.qn[0:DH, h].bitcast(F32), ALU.mult, ALU.subtract)
                    ins.then_inc(s_dve, 1)
                elif kind in ("kc", "vc"):
                    c = 0 if kind == "kc" else 1
                    dve.wait_ge(s_item, i + 1)
                    if c == 0:
                        dve.wait_ge(s_aux, 32)
                    for g in range(KV):
                        for par in range(2):
                            half = slice(par * DH, (par + 1) * DH)
                            src = bank[g * DH:(g + 1) * DH, par:par + 1]
                            tok = bass.AP(tensor=src.tensor, offset=src.offset,
                                          ap=[list(src.ap[0]), [2, 16], [CMP_STRIDE, NC_BLOCKS]])
                            dst = m.blk[half, c].rearrange("p (j g n) -> p j g n", j=16, g=KV)[:, :, g]
                            ins = V.tensor_tensor(dst, tok, m.cpos[half, c].unsqueeze(2)
                                                  .to_broadcast([DH, 16, NC_BLOCKS]), ALU.add)
                    ins.then_inc(s_dve, 1)
                if i - 1 in v_items:
                    j = v_items.index(i - 1)
                    b = v_branch[kinds[i - 1]]
                    dve.wait_ge(s_vta, j + 1)
                    for g in range(KV):
                        ins = V.tensor_tensor(m.vl[:, b, g, :, 0:DH],
                                              k.bank[3][:, :].rearrange("p (t g d) -> p t g d", t=QT, g=KV)[:, :, g],
                                              m.vh[:, b, g, :, 0:DH].bitcast(F32), ALU.subtract)
                    ins.then_inc(s_vtd, 1)
                for stage, c in stages_beside_block(i):
                    if stage == "blocks":
                        dve.wait_ge(s_blkh, c + 1)
                        V.tensor_tensor(m.blkl[:, c], m.blk[:, c], m.blkh[:, c].bitcast(F32),
                                        ALU.subtract).then_inc(s_blkl, 1)
                        if c == 0:
                            dve.wait_ge(s_w2h, 1)
                            V.tensor_tensor(m.cw2l[:, :, :, :], m.cw2[:, :, :, :], m.cw2h[:, :, :, :].bitcast(F32),
                                            ALU.subtract).then_inc(s_w2l, 1)
                    elif stage == "turn":
                        dve.wait_ge(s_hidt, c + 1)
                        x, t, th, g_ = (m.ge[:, j] for j in range(4))
                        V.tensor_copy(x, k.bank[5][:, 0:2 * KV * NC_BLOCKS].rearrange("p (s n) -> p s n", s=2))\
                            .then_inc(s_x, 1)
                        dve.wait_ge(s_x, 4 * c + 1)
                        V.tensor_tensor(t, x, x, ALU.mult).then_inc(s_x, 1)
                        dve.wait_ge(s_x, 4 * c + 2)
                        V.tensor_scalar(t, t, 0.044715, 1.0, ALU.mult, ALU.add).then_inc(s_x, 1)
                        dve.wait_ge(s_x, 4 * c + 3)
                        V.tensor_tensor(t, t, x, ALU.mult).then_inc(s_x, 1)
                        dve.wait_ge(s_th, c + 1)
                        V.scalar_tensor_tensor(g_, th, 1.0, x, ALU.add, ALU.mult).then_inc(s_g, 1)
                        dve.wait_ge(s_gh, c + 1)
                        V.scalar_tensor_tensor(m.gel[:, :], g_, 0.5, m.geh[:, :].bitcast(F32), ALU.mult,
                                               ALU.subtract).then_inc(s_gl, 1)
                    elif c == 0:
                        dve.wait_ge(s_c2a, 1)
                        src = k.bank[2][0:DH, 0:KV * NC_BLOCKS].rearrange("p (g n) -> p g n", g=KV)
                        V.tensor_tensor(m.kc2[DH:P, :, 0:NC_BLOCKS], src, m.kc[0:DH, :, 0:NC_BLOCKS].bitcast(F32),
                                        ALU.subtract).then_inc(s_c2d, 1)
                    else:
                        dve.wait_ge(s_c2a, 2)
                        V.tensor_tensor(m.vcl[0:NC_BLOCKS, :, 0:DH],
                                        k.bank[2][0:NC_BLOCKS, 0:P].rearrange("p (g d) -> p g d", g=KV),
                                        m.vch[0:NC_BLOCKS, :, 0:DH].bitcast(F32), ALU.subtract).then_inc(s_c2d, 1)
            for j in range(N_GATES):
                for x in s.with_gates.get(j, []):
                    if x[0] == "max":
                        max_vector(k, s, dve, *x[1:])
                if j + 2 < N_GATES:
                    projection_w_lo(k, m, dve, N + j + 2)

        @block.tensor
        def _(pe):
            def weights(slot):
                return [x[slot][:, :].rearrange("p (k c) -> p k c", c=P) for x in (m.wh, m.wl)]

            def product(slot, bank, tiles=range(DT)):
                w = weights(slot)
                for kt in tiles:
                    for j, (x, y) in enumerate(split_terms(w[0][:, kt], w[1][:, kt], k.uh[:, kt], k.ul[:, kt])):
                        mm = nc.tensor.matmul(bank[:, :], x, y, start=(kt == 0 and j == 0),
                                              stop=(kt == DT - 1 and j == 2))
                return mm
            pe.wait_ge(s_lo, 2)
            for kt in range(DT - 1):
                pe.wait_ge(n2.s_ul, kt + 1)
                for i in range(2):
                    product(i, k.bank[i], (kt,))
            pe.wait_ge(n2.s_ul, DT)
            for i in range(2):
                product(i, k.bank[i], (DT - 1,)).then_inc(s_item, 1)
            for i in range(2, N):
                pe.wait_ge(s_lo, i + 1)
                if items[i][0] == "in":
                    before = bank_before[i]
                    if before is None:
                        pass
                    elif kinds[before] in DVE_KINDS:
                        pe.wait_ge(s_dve, dve_after[before])
                    else:
                        pe.wait_ge(s_act, act_after[before])
                    product(i % 3, k.bank[bank_of[i]]).then_inc(s_item, 1)
                else:
                    c, chunk = (0 if items[i][0] == "ck" else 1), items[i][1]
                    if chunk == 0:
                        pe.wait_ge(s_blkl, c + 1)
                        if c == 1:
                            pe.wait_ge(s_hid, 1)
                    w = [x[i % 3][:, :].rearrange("p (j h) -> p j h", j=4) for x in (m.wh, m.wl)]
                    b = [x[:, c].rearrange("p (j n) -> p j n", j=16) for x in (m.blkh, m.blkl)]
                    for j in range(4):
                        for q, (x, y) in enumerate(split_terms(b[0][:, chunk * 4 + j], b[1][:, chunk * 4 + j],
                                                               w[0][:, j], w[1][:, j])):
                            mm = nc.tensor.matmul(k.bank[4][0:KV * NC_BLOCKS, 0:HID_C], x, y,
                                                  start=(chunk == 0 and j == 0 and q == 0),
                                                  stop=(chunk == 3 and j == 3 and q == 2))
                    mm.then_inc(s_item, 1)
                if i - 1 in v_items:
                    j = v_items.index(i - 1)
                    pe.wait_ge(s_act, act_after[i - 1])
                    if j >= 1:
                        pe.wait_ge(s_vtd, j)
                    for t in range(QT):
                        mm = nc.tensor.transpose(k.bank[3][:, t * P:(t + 1) * P], m.vT[:, j % 2, t * P:(t + 1) * P],
                                                 k.idF[:, :])
                    mm.then_inc(s_vt, 1)
                for stage, c in stages_beside_block(i):
                    NG = KV * NC_BLOCKS
                    if stage == "turn":
                        pe.wait_ge(s_hid, c + 1)
                        if c == 1:
                            pe.wait_ge(s_x, 1)
                        for hid in range(2):
                            mm = nc.tensor.transpose(k.bank[5][:, hid * NG:(hid + 1) * NG],
                                                     m.hid[:, hid * P:(hid + 1) * P], k.idF[0:NG, 0:NG])
                        mm.then_inc(s_hidt, 1)
                    elif stage == "second":
                        pe.wait_ge(s_gl, c + 1)
                        pe.wait_ge(s_w2l, 1)
                        if c == 0:
                            for hid in range(2):
                                for q, (x, y) in enumerate(split_terms(m.cw2h[:, 0, hid], m.cw2l[:, 0, hid],
                                                                       m.geh[:, hid], m.gel[:, hid])):
                                    mm = nc.tensor.matmul(k.bank[2][0:DH, 0:NG], x, y,
                                                          start=(hid == 0 and q == 0), stop=(hid == 1 and q == 2))
                        else:
                            pe.wait_ge(s_c2d, 1)
                            for g in range(KV):
                                nn = slice(g * NC_BLOCKS, (g + 1) * NC_BLOCKS)
                                for hid in range(2):
                                    for q, (x, y) in enumerate(split_terms(m.geh[:, hid, nn], m.gel[:, hid, nn],
                                                                           m.cw2h[:, 1, hid], m.cw2l[:, 1, hid])):
                                        mm = nc.tensor.matmul(k.bank[2][0:NC_BLOCKS, g * DH:(g + 1) * DH], x, y,
                                                              start=(hid == 0 and q == 0), stop=(hid == 1 and q == 2))
                        mm.then_inc(s_c2, 1)
            for j in range(len(s.with_gates)):
                steps = list(s.with_gates[j])
                pe.wait_ge(s_lo, N + j + 1)
                if j >= 2:
                    pe.wait_ge(s_act, act_after[N - 1] + j - 1)
                else:
                    pe.wait_ge(s_act, act_after[[i for i in proj_items if bank_of[i] == 6 + j % 2][-1]])
                for kt in range(DT):
                    if j == 0 and kt == 1:
                        pe.wait_ge(s_act, act_after[N - 1])
                        pe.wait_ge(s_dve, dve_after[N - 1])
                        pe.wait_ge(s_c2d, 2)
                    mm = product((j + 1) % 2, k.bank[6 + j % 2], (kt,))
                    if kt == DT - 1:
                        mm.then_inc(s_item, 1)
                    if kt % 2 and steps:
                        x = steps.pop(0)
                        if x[0] == "max":
                            max_tensor(k, m, s, pe, *x[1:])
                        else:
                            rows_tensor(k, s, pe, x[1])
            with pe.Fori(len(s.with_gates) // 2, N_GATES // 2) as it:
                for slot in range(2):
                    pe.wait_ge(s_lo, it * 2 + (N + slot + 1))
                    pe.wait_ge(s_act, it * 2 + (act_after[N - 1] + slot - 1))
                    product(1 - slot, k.bank[6 + slot]).then_inc(s_item, 1)


LAG = 3
RING = 4


def attention_buffers(k, m):
    s, at, X, K = Record(), k.at, k.X, 1024
    s.p32 = at("exp_f32", [P, RING, T], F32, X + 120 * K)
    s.pl = at("exp_lo", [P, RING, T], F32R, X + 120 * K)
    s.ph = at("exp_hi", [P, RING, T], F32R, X + 128 * K)
    s.num = [at("numerator0", [P, 4, T], F32, X + 138 * K), at("numerator1", [P, 4, T], F32, 0)]
    s.ya = at("y_a", [P, 4, T], F32, 8 * K)
    s.yb = s.num[1]
    s.yah = at("y_a_hi", [P, 4, T], F32R, X + 32 * K)
    s.yal = at("y_a_lo", [P, 4, T], F32R, X + 40 * K)
    s.ybh = at("y_b_hi", [P, 4, T], F32R, X + 48 * K)
    s.ybl = at("y_b_lo", [P, 4, T], F32R, X + 56 * K)
    s.fb = at("factor_bc", [P, 4, T], F32, X + 105 * K)
    s.R = [at(f"minus_max_rows{j}", [HEADS, T], F32R, X + (101 + 2 * j) * K) for j in range(2)]
    s.se = at("sink_exp", [HEADS, T], F32, X + 113 * K)
    c = X + 146 * K
    s.nm = at("minus_max", [P, 2, HEADS, QT], F32, X + 150 * K + 512)
    s.sk = at("minus_sink", [P, HEADS, QT], F32, c + 256)
    s.sinks = at("sinks_bc", [P, HEADS], F32, c + 384)
    s.sinkc = at("sinks_col", [HEADS, 1], F32, c + 416)
    s.gsp = at("gates_spread", [P, 3, 32], F32, c + 448)
    s.den = at("den_spread", [P, 4, 32], F32, c + 832)
    s.sden = at("sink_den_spread", [P, 32], F32, c + 1344)
    s.fac = at("factor_spread", [P, 2, 32], F32, c + 1472)
    s.dr = [at("den_row0", [P, T], F32, X + 118 * K), at("den_row1", [P, T], F32, X + 148 * K)]
    s.s_setup, s.s_gsp, s.s_qrows = k.sem("at_setup"), k.sem("at_gsp"), k.sem("at_qrows")
    s.s_qsh, s.s_qsl, s.s_a = k.sem("at_qsh"), k.sem("at_qsl"), k.sem("at_a")
    s.s_red, s.s_nm, s.s_tr = k.sem("at_red"), k.sem("at_nm"), k.sem("at_tr")
    s.s_R, s.s_st, s.s_ph = k.sem("at_R"), k.sem("at_st"), k.sem("at_ph")
    s.s_pl, s.s_pv, s.s_num = k.sem("at_pl"), k.sem("at_pv"), k.sem("at_num")
    s.s_dr, s.s_sets, s.s_sead = k.sem("at_dr"), k.sem("at_sets"), k.sem("at_sead")
    s.s_mul, s.s_seex, s.s_sed = k.sem("at_mul"), k.sem("at_seex"), k.sem("at_sed")
    s.s_d1, s.s_d2, s.s_yh = k.sem("at_d1"), k.sem("at_d2"), k.sem("at_yh")
    s.s_yl = k.sem("at_yl")
    s.s_row = [k.sem(f"at_row{b}") for b in range(4)]
    s.s_drd = [k.sem(f"at_den{j}") for j in range(2)]
    s.s_fout = [k.sem(f"at_fout{b}") for b in range(4)]
    s.s_fin = [k.sem(f"at_fin{b}") for b in range(4)]
    s.with_gates, s.order = attention_order()
    steps = [x for j in range(N_GATES) for x in s.with_gates.get(j, [])] + s.order
    s.group_index = {x[1:]: i for i, x in enumerate(x for x in steps if x[0] == "max")}
    s.rows_bank = lambda b: k.bank[5 if b < 2 else 7]
    return s


def attention_units(b):
    out = []
    for h in range(HEADS):
        if b == 0:
            out.append((h, 0, 0, T, True, True))
        else:
            for kb in range(QT):
                n = T - kb * P if b < 3 else min(2 * P, T - kb * P)
                out.append((h, kb, kb * P, n, kb == 0, kb == QT - 1))
    return out


def maximum_groups(b):
    if b == 0:
        return [[(h, q, 0, NCP, (h % 4) * P + q * NCP) for h in range(g * 4, g * 4 + 4) for q in range(QT)]
                for g in range(2)]
    if b == 3:
        return [x for h in range(HEADS) for x in ([(h, 1, 0, 2 * P, 0), (h, 2, P, 2 * P, 2 * P)],
                                                  [(h, 3, 2 * P, 2 * P, 0), (h, 0, 0, P, 2 * P)])]
    return [x for h in range(HEADS) for x in ([(h, 0, 0, P, 0), (h, 2, 0, 3 * P, P)], [(h, 1, 0, 2 * P, 0)],
                                              [(h, 3, 0, 4 * P, 0)])]


def attention_order():
    groups = {b: [("max", b, g) for g in range(len(maximum_groups(b)))] for b in range(4)}
    first = groups[0] + groups[1]
    with_gates = {j: first[3 * j:3 * j + 3] for j in range(9)}
    with_gates[1] = with_gates[1] + [("rows", 0)]
    with_gates[9] = [("rows", 1)]
    out = []
    for b in range(4):
        for u in range(len(attention_units(b))):
            if b == 0:
                out += groups[2][:2]
                del groups[2][:2]
            elif b < 3 and u % 2 == 0:
                source = groups[2] or groups[3]
                out += source[:1]
                del source[:1]
            if (b, u) in ((1, 19), (2, 19)):
                out.append(("rows", b + 1))
            out.append(("unit", b, u))
            if b == 0 and u % 2:
                out.append(("swaq", u // 2))
            if b == 1 and u < 8 and u % 2 == 0:
                out.append(("swaq", 4 + u // 2))
            if (b, u) == (1, 0):
                out.append(("sinks",))
            if b > 0 and u == (8 if b == 1 else 4):
                out.append(("div", b - 1))
            if b > 0 and u >= 16 and u % 2 == 0 and u < 24:
                out.append(("mul", b - 1, (u - 16) // 2))
            if b == 3 and u == 10:
                out.append(("merge", 0))
            if b == 3 and u >= 24 and u % 2 == 0:
                out.append(("yhi", (u - 24) // 2))
    return with_gates, out


def queries_of(m, b):
    return (m.qn, m.qn2) if b < 3 else (m.qs, m.qs2)


def keys_of(m, b, h):
    g = h // REP
    return (m.kc[:, g], m.kc2[:, g]) if b == 0 else (m.kk[:, b - 1, g], m.kk2[:, b - 1, g])


def max_tensor(k, m, s, pe, b, g):
    nc, gi = k.nc, s.group_index[(b, g)]
    bank, q1 = k.bank[gi % 2], queries_of(m, b)[0]
    if gi >= 2:
        pe.wait_ge(s.s_red, gi - 1)
    if b == 3 and g == 0:
        pe.wait_ge(s.s_qrows, 16)
    if b == 3 and g % 2 == 0:
        pe.wait_ge(s.s_qsh, g // 2 + 1)
    for j, (h, q, k0, n, col) in enumerate(maximum_groups(b)[g]):
        kr = keys_of(m, b, h)[0]
        mm = nc.tensor.matmul(bank[:, col:col + n], q1[0:DH + 1, h, q * P:(q + 1) * P], kr[0:DH + 1, k0:k0 + n],
                              start=(j == 0), stop=False, skip_group_check=True)
        if b == 0 and q == QT - 1:
            mm = nc.tensor.matmul(bank[:, (h % 4) * P:(h % 4 + 1) * P], k.idR[:, :],
                                  k.mca[:, :, :].rearrange("p q n -> p (q n)"), start=False, stop=True,
                                  skip_group_check=True)
        elif b > 0:
            width = 2 * P if b == 3 and n == 2 * P else P
            mask = k.msk[:, 2 - width // P:2].rearrange("p m c -> p (m c)")
            mm = nc.tensor.matmul(bank[:, col + n - width:col + n], k.idR[:, :], mask, start=False, stop=True,
                                  skip_group_check=True)
    mm.then_inc(s.s_a, 1)


def max_vector(k, s, dve, b, g):
    V, gi = k.nc.vector, s.group_index[(b, g)]
    bank, nm = k.bank[gi % 2], s.nm[:, b % 2]
    dve.wait_ge(s.s_a, gi + 1)
    if b == 0:
        ins = V.tensor_reduce(nm[:, g * 4:g * 4 + 4, :].rearrange("p h q -> p (h q)"),
                              bank[:, :].rearrange("p (r n) -> p r n", n=NCP), AX.X, ALU.max, negate=True)
    else:
        for h, q, _, n, col in maximum_groups(b)[g]:
            ins = V.tensor_reduce(nm[:, h, q:q + 1], bank[:, col:col + n], AX.X, ALU.max, negate=True)
    ins.then_inc(s.s_red, 1)
    if g == len(maximum_groups(b)) - 1:
        dve.wait_ge(s.s_red, gi + 1)
        if b < 3:
            V.tensor_scalar(nm, nm, 1e20, None, ALU.min).then_inc(s.s_nm, 1)
        else:
            dve.wait_ge(s.s_sets, 2)
            V.tensor_tensor(nm, nm, s.sk[:, :, :], ALU.min).then_inc(s.s_nm, 1)


def rows_tensor(k, s, pe, b):
    pe.wait_ge(s.s_nm, b + 1)
    if b >= 1:
        pe.wait_ge(s.s_R, b)
    for q in range(QT):
        mm = k.nc.tensor.transpose(s.rows_bank(b)[0:HEADS, q * P:(q + 1) * P], s.nm[:, b % 2, :, q], k.idF[:, :])
    mm.then_inc(s.s_tr, 1)


def rows_scalar(k, s, act, b):
    act.wait_ge(s.s_tr, b + 1)
    k.nc.scalar.activation(s.R[b % 2][:, :], s.rows_bank(b)[0:HEADS, :], ACT.Copy).then_inc(s.s_R, 1)


def rows_out(k, m, s, sp, b):
    row = ROW_M[BRANCHES[b]]
    sp.wait_ge(s.s_R, b + 1)
    sp.dma_start(queries_of(m, b)[0][row:row + 1].bitcast(F32), s.R[b % 2][:, :].bitcast(F32))\
        .then_inc(s.s_row[b], 16)


def attention(k, m, s, following):
    nc, a = k.nc, k.a
    order = s.order
    unit_at = [(b, u) for kind, b, u in (x for x in order if x[0] == "unit")]
    index = {x: i for i, x in enumerate(unit_at)}
    info = [(b,) + attention_units(b)[u] for b, u in unit_at]
    def values(b, h, kb):
        g = h // REP
        if b == 0:
            return m.vch[0:NC_BLOCKS, g, 0:DH + 1], m.vcl[0:NC_BLOCKS, g, 0:DH + 1]
        return m.vh[:, b - 1, g, kb, 0:DH + 1], m.vl[:, b - 1, g, kb, 0:DH + 1]

    def head_no(i):
        return info[i][0] * HEADS + info[i][1]

    with nc.Block() as block:
        @block.sync
        def _(sp):
            sp.dma_start(s.sinks[:, :], a.sinks.unsqueeze(0).to_broadcast([P, HEADS])).then_inc(s.s_setup, 16)
            sp.dma_start(s.sk[:, :, :].rearrange("p h q -> p (h q)"), a.slope_cols).then_inc(s.s_setup, 16)
            sp.dma_start(s.sinkc[:, :], a.sinks.rearrange("(h o) -> h o", o=1)).then_inc(s.s_setup, 16)
            sp.dma_start(s.se[:, :], a.slope_rows).then_inc(s.s_setup, 16)
            for b, rows in enumerate((0, 2, 1)):
                sp.dma_start(s.gsp[:, b], m.gs[rows * HEADS:(rows + 1) * HEADS, :]).then_inc(s.s_gsp, 16)
            sp.dma_start(m.qs[DH:96].bitcast(F32), m.qn[DH:96].bitcast(F32)).then_inc(s.s_qrows, 16)

            def denominator_out(i):
                if i >= 0 and info[i][6]:
                    c, h = head_no(i), info[i][1]
                    sp.wait_ge(s.s_dr, c + 1)
                    sp.dma_start(s.den[h * 16:(h + 1) * 16, info[i][0]], s.dr[c % 2][DH:DH + 1, :])\
                        .then_inc(s.s_drd[c % 2], 16)
            for x in order:
                if x[0] == "rows":
                    rows_out(k, m, s, sp, x[1])
                    if x[1] == 3:
                        sp.wait_ge(s.s_seex, 1)
                        sp.dma_start(s.sden[:, :], s.se[:, :]).then_inc(s.s_sed, 16)
                elif x[0] == "unit":
                    denominator_out(index[x[1:]] - LAG)
                elif x[0] == "div":
                    factors_out(k, s, sp, x[1])
                elif x[0] == "merge":
                    sp.wait_ge(s.s_pv, index[(2, 31)] + 1)
                    for i in range(2):
                        merge_load(following, sp, i)
            for i in range(len(info) - LAG, len(info)):
                denominator_out(i)

        @block.gpsimd
        def _(pool):
            for i, (b, h, kb, q0, n, first, last) in enumerate(info):
                rows = NC_BLOCKS if b == 0 else P
                pool.wait_ge(s.s_ph, i + 1)
                nc.gpsimd.tensor_tensor(s.pl[0:rows, i % RING, 0:n], s.p32[0:rows, i % RING, 0:n],
                                        s.ph[0:rows, i % RING, 0:n].bitcast(F32), ALU.subtract).then_inc(s.s_pl, 1)

        @block.scalar
        def _(act):
            A = nc.scalar

            def exps(i):
                b, h, kb, q0, n, first, last = info[i]
                rows = NC_BLOCKS if b == 0 else P
                act.wait_ge(s.s_st, i + 1)
                if i >= RING:
                    act.wait_ge(s.s_pv, i - RING + 1)
                src = k.bank[2 + i % 3][0:rows, 0:n]
                A.activation(s.p32[0:rows, i % RING, 0:n], src, ACT.Exp)
                A.activation(s.ph[0:rows, i % RING, 0:n], src, ACT.Exp).then_inc(s.s_ph, 1)

            def numerator(i):
                b, h, kb, q0, n, first, last = info[i]
                if last:
                    c = b * HEADS + h
                    act.wait_ge(s.s_pv, i + 1)
                    if b >= 2 and h == 0:
                        act.wait_ge(s.s_d2, 4 * (b - 1))
                    half = slice((h % 2) * DH, (h % 2 + 1) * DH)
                    A.activation(s.num[b % 2][half, h // 2], k.bank[5 + c % 2][0:DH, :], ACT.Copy).then_inc(s.s_num, 1)
            for x in order:
                if x[0] == "unit":
                    i = index[x[1:]]
                    exps(i)
                    if i >= LAG:
                        numerator(i - LAG)
                elif x[0] == "rows":
                    rows_scalar(k, s, act, x[1])
                    if x[1] == 3:
                        act.wait_ge(s.s_sead, 1)
                        A.activation(s.se[:, :], s.se[:, :], ACT.Exp, bias=s.sinkc[:, :]).then_inc(s.s_seex, 1)
                elif x[0] == "swaq":
                    h = x[1]
                    src = m.qsf[(h % 2) * DH:(h % 2 + 1) * DH, h // 2]
                    A.activation(m.qs[0:DH, h], src, ACT.Copy)
                    A.activation(m.qs2[DH:P, h], src, ACT.Copy).then_inc(s.s_qsh, 1)
                elif x[0] == "yhi":
                    p = x[1]
                    act.wait_ge(s.s_d2, 8 + p + 1)
                    A.activation(s.yah[:, p], s.ya[:, p], ACT.Copy).then_inc(s.s_yh, 1)
                    if p >= 2:
                        merge_w_hi(k, following, act, p - 2)
            for i in range(len(info) - LAG, len(info)):
                numerator(i)

        @block.vector
        def _(dve):
            V = nc.vector

            def denominator(i):
                b, h, kb, q0, n, first, last = info[i]
                if last:
                    c = b * HEADS + h
                    if c == 0:
                        dve.wait_ge(s.s_gsp, 48)
                    dve.wait_ge(s.s_pv, i + 1)
                    if c >= 2:
                        dve.wait_ge(s.s_drd[c % 2], 16 * (c // 2))
                    V.tensor_copy(s.dr[c % 2][DH:DH + 1, :], k.bank[5 + c % 2][DH:DH + 1, :]).then_inc(s.s_dr, 1)
            for x in order:
                if x[0] == "max":
                    max_vector(k, s, dve, *x[1:])
                elif x[0] == "rows" and x[1] == 3:
                    dve.wait_ge(s.s_R, 4)
                    V.tensor_tensor(s.se[:, :], s.se[:, :], s.R[1][:, :].bitcast(F32), ALU.add).then_inc(s.s_sead, 1)
                elif x[0] == "unit":
                    i = index[x[1:]]
                    if i >= LAG:
                        denominator(i - LAG)
                elif x[0] == "swaq":
                    h = x[1]
                    dve.wait_ge(s.s_qsh, h + 1)
                    hi = m.qs2[DH:P, h] if h % 2 else m.qs[0:DH, h]
                    V.tensor_tensor(m.qs2[0:DH, h], m.qsf[(h % 2) * DH:(h % 2 + 1) * DH, h // 2], hi.bitcast(F32),
                                    ALU.subtract).then_inc(s.s_qsl, 1)
                elif x[0] == "yhi":
                    p = x[1]
                    dve.wait_ge(s.s_yh, p + 1)
                    V.tensor_tensor(s.yal[:, p], s.ya[:, p], s.yah[:, p].bitcast(F32), ALU.subtract).then_inc(s.s_yl, 1)
                    if p >= 2:
                        merge_w_lo(k, following, dve, p - 2)
                elif x[0] == "sinks":
                    dve.wait_ge(s.s_setup, 64)
                    V.tensor_tensor(s.sk[:, :, :], s.sk[:, :, :], s.sinks[:, :].unsqueeze(2).to_broadcast([P, HEADS, QT]),
                                    ALU.add).then_inc(s.s_sets, 1)
                    dve.wait_ge(s.s_sets, 1)
                    V.tensor_scalar(s.sk[:, :, :], s.sk[:, :, :], -1.0, None, ALU.mult).then_inc(s.s_sets, 1)
                elif x[0] == "div":
                    factors(k, s, dve, x[1])
                elif x[0] == "mul":
                    weigh(k, s, dve, x[1], x[2])
            for i in range(len(info) - LAG, len(info)):
                denominator(i)

        @block.tensor
        def _(pe):
            def scores(i):
                b, h, kb, q0, n, first, last = info[i]
                rows, last_row = (NC_BLOCKS if b == 0 else P), ROW_M[BRANCHES[b]] + 1
                kr, kp = keys_of(m, b, h)
                ks = slice(kb * P, kb * P + rows)
                q1, q2 = queries_of(m, b)
                out = k.bank[2 + i % 3][0:rows, 0:n]
                if h == 0 and first:
                    pe.wait_ge(s.s_row[b], 16)
                    if b == 3:
                        pe.wait_ge(s.s_qsl, HEADS)
                if i >= 3:
                    pe.wait_ge(s.s_ph, i - 2)
                mm = nc.tensor.matmul
                width = T if b == 0 else P if b < 3 or n == P else 2 * P
                mask = k.mcc[0:rows, :] if b == 0 else \
                    k.msk[:, M_L:M_L + width // P].rearrange("p m c -> p (m c)")
                mm(out[:, 0:width], k.idR[0:rows, 0:rows], mask, start=True, stop=False, skip_group_check=True)
                mm(out, kr[0:last_row, ks], q1[0:last_row, h, q0:q0 + n], start=False, stop=False,
                   skip_group_check=True)
                mm(out, kp[:, ks], q2[:, h, q0:q0 + n], start=False, stop=True, skip_group_check=True)\
                    .then_inc(s.s_st, 1)

            def product(i):
                b, h, kb, q0, n, first, last = info[i]
                c = b * HEADS + h
                rows = NC_BLOCKS if b == 0 else P
                vh, vl = values(b, h, kb)
                out = k.bank[5 + c % 2][0:DH + 1, q0:q0 + n]
                pe.wait_ge(s.s_pl, i + 1)
                if first and c >= 2:
                    pe.wait_ge(s.s_num, c - 1)
                    pe.wait_ge(s.s_dr, c - 1)
                ph, pl = s.ph[0:rows, i % RING, 0:n], s.pl[0:rows, i % RING, 0:n]
                for j, (x, y) in enumerate(((vh, ph), (vh, pl), (vl, ph))):
                    mm = nc.tensor.matmul(out, x, y, start=(first and j == 0), stop=(last and j == 2),
                                          skip_group_check=True)
                mm.then_inc(s.s_pv, 1)

            for x in order:
                if x[0] == "max":
                    max_tensor(k, m, s, pe, *x[1:])
                elif x[0] == "rows":
                    rows_tensor(k, s, pe, x[1])
                elif x[0] == "unit":
                    i = index[x[1:]]
                    scores(i)
                    if i >= LAG:
                        product(i - LAG)
            for i in range(len(info) - LAG, len(info)):
                product(i)


def factors(k, s, dve, b):
    V = k.nc.vector
    den, fac = s.den[:, b], s.fac[:, b % 2]
    n = counter()
    n(3 * b)

    def then(ins):
        ins.then_inc(s.s_d1, 1)
        return n()
    for j in range(2):
        dve.wait_ge(s.s_drd[j], 16 * 4 * (b + 1))
    if b == 0:
        dve.wait_ge(s.s_gsp, 48)
    if b == 3:
        dve.wait_ge(s.s_sed, 16)
        dve.wait_ge(s.s_d1, then(V.tensor_tensor(den, den, s.sden[:, :], ALU.add)))
    else:
        dve.wait_ge(s.s_d1, then(V.tensor_scalar(den, den, 1e-30, None, ALU.max)))
    dve.wait_ge(s.s_d1, then(V.reciprocal(fac, den)))
    if b < 3:
        V.tensor_tensor(fac, fac, s.gsp[:, b], ALU.mult).then_inc(s.s_d1, 1)


def factors_out(k, s, sp, b, between=None):
    sp.wait_ge(s.s_d1, 3 * b + (3 if b < 3 else 2))
    sp.dma_start(k.fac[b].rearrange("(p c) -> p c", c=32), s.fac[:, b % 2]).then_inc(s.s_fout[b], 16)
    if between is not None:
        between()
    sp.wait_ge(s.s_fout[b], 16)
    if b == 0:
        sp.wait_ge(s.s_qsl, HEADS)
    else:
        sp.wait_ge(s.s_d2, 4 * b)
    rows = k.fac[b].rearrange("(h r t) -> r h t", r=2, t=T)
    for r in range(2):
        sp.dma_start(s.fb[r * DH:(r + 1) * DH, :, :], rows[r].unsqueeze(0).to_broadcast([DH, HEADS // 2, T])).then_inc(s.s_fin[b], 16)


def weigh(k, s, dve, b, p):
    V = k.nc.vector
    num = s.num[b % 2][:, p]
    if p == 0:
        dve.wait_ge(s.s_fin[b], 32)
    dve.wait_ge(s.s_num, b * HEADS + 2 * p + 2)
    if b == 0:
        V.tensor_tensor(s.ya[:, p], num, s.fb[:, p], ALU.mult).then_inc(s.s_d2, 1)
    elif b == 3:
        V.tensor_tensor(num, num, s.fb[:, p], ALU.mult).then_inc(s.s_d2, 1)
    else:
        V.tensor_tensor(num, num, s.fb[:, p], ALU.mult).then_inc(s.s_mul, 1)
        dve.wait_ge(s.s_mul, (b - 1) * 4 + p + 1)
        V.tensor_tensor(s.ya[:, p], s.ya[:, p], num, ALU.add).then_inc(s.s_d2, 1)


def merge_buffers(k):
    g, at, X, K = Record(), k.at, k.X, 1024
    g.raw = at("merge_raw", [P, 3, D], F32, X + 64 * K)
    g.wh = [at(f"merge_w_hi{j}", [P, D], F32R, X + o) for j, o in enumerate((76 * K, 88 * K, 114 * K, 122 * K))]
    g.wl = [at(f"merge_w_lo{j}", [P, D], F32R, X + o)
            for j, o in enumerate((80 * K, 88 * K + 6400, 118 * K, 126 * K))]
    g.ta = at("gated_a", [P, 6, T], F32, X + 130 * K)
    g.tb = at("gated_b", [P, 2, T], F32, X + 142 * K)
    g.sum = at("merged_f32", [P, 2, T], F32, X + 84 * K)
    g.s_raw = [k.sem(f"mg_raw{j}") for j in range(3)]
    g.s_hi, g.s_lo, g.s_item = k.sem("mg_w_hi"), k.sem("mg_w_lo"), k.sem("mg_item")
    lead = 5
    g.items = [("a", n) for n in range(lead)]
    for n in range(DT):
        g.items.append(("b", n))
        if n + lead < DT:
            g.items.append(("a", n + lead))
    g.items += [("o", n) for n in range(DT)]
    g.width = [D if x[0] == "o" else D // 2 for x in g.items]
    g.source = [k.a.wout[n].rearrange("p k c -> p (k c)") if kind == "o" else
                k.a.wup[n, :, "ab".index(kind)].rearrange("p k c -> p (k c)") for kind, n in g.items]
    return g


def merge_load(g, sp, i):
    sp.dma_start(g.raw[:, i % 3, 0:g.width[i]], g.source[i]).then_inc(g.s_raw[i % 3], 16)


def merge_w_hi(k, g, act, i):
    act.wait_ge(g.s_raw[i % 3], 16 * (i // 3 + 1))
    if i >= 4:
        act.wait_ge(g.s_item, i - 3)
    w = g.width[i]
    k.nc.scalar.activation(g.wh[i % 4][:, 0:w], g.raw[:, i % 3, 0:w], ACT.Copy).then_inc(g.s_hi, 1)


def merge_w_lo(k, g, dve, i):
    dve.wait_ge(g.s_hi, i + 1)
    w = g.width[i]
    k.nc.vector.tensor_tensor(g.wl[i % 4][:, 0:w], g.raw[:, i % 3, 0:w], g.wh[i % 4][:, 0:w].bitcast(F32),
                              ALU.subtract).then_inc(g.s_lo, 1)


def merge(k, m, g, s, f, n3):
    nc = k.nc
    S = k.sem
    ta, tb, mg = g.ta, g.tb, g.sum
    mh, ml = k.uh, k.ul
    items, width, s_item, s_lo = g.items, g.width, g.s_item, g.s_lo
    s_h, s_ta, s_tb, s_mg = S("mg_h"), S("mg_ta"), S("mg_tb"), S("mg_sum")
    s_mh, s_ml, s_add = S("mg_hi"), S("mg_lo"), S("mg_add")
    N = len(items)
    with nc.Block() as block:
        @block.sync
        def _(sp):
            def load(i):
                if i >= 3:
                    sp.wait_ge(s_lo, i - 2)
                merge_load(g, sp, i)

            def next_loads():
                load(4)
                load(5)
            load(2)
            load(3)
            factors_out(k, s, sp, 3, between=next_loads)
            for i in range(6, N):
                if i == items.index(("b", 4)):
                    sp.wait_ge(s.s_yl, 8)
                    sp.dma_start(k.hT[:, :, :], k.hT_spill.rearrange("(t p) n -> p t n", p=P)).then_inc(s_h, 16)
                load(i)
            sp.wait_ge(s_tb, DT)
            sp.wait_ge(s_ta, DT)
            for j in range(2):
                ffn_load_gu(k, f, sp, 0, j)
            for j in range(2):
                ffn_load_dn(k, f, sp, 0, j)

        @block.gpsimd
        def _(pool):
            for i in range(N - DT, N):
                pool.wait_ge(g.s_hi, i + 1)
                if i == N - DT:
                    pool.wait_ge(s_lo, i)
                nc.gpsimd.tensor_tensor(g.wl[i % 4][:, :], g.raw[:, i % 3], g.wh[i % 4][:, :].bitcast(F32),
                                        ALU.subtract).then_inc(s_lo, 1)

        @block.scalar
        def _(act):
            A = nc.scalar

            merge_w_hi(k, g, act, 2)
            for i in range(N):
                if i + 3 < N:
                    merge_w_hi(k, g, act, i + 3)
                if i == 3:
                    for p in range(4):
                        act.wait_ge(s.s_d2, 12 + p + 1)
                        A.activation(s.ybh[:, p], s.yb[:, p], ACT.Copy).then_inc(s.s_yh, 1)
                kind, n = items[i]
                if kind == "b":
                    act.wait_ge(s_mg, n + 1)
                    A.activation(mh[:, n], mg[:, n % 2], ACT.Copy).then_inc(s_mh, 1)
                elif kind == "o" and n in (3, 4):
                    ffn_scalar_gu_hi(k, f, act, 0, n - 3)
            norm_scalar_squares(k, n3, act, s_add)

        @block.vector
        def _(dve):
            V = nc.vector

            merge_w_lo(k, g, dve, 2)
            factors(k, s, dve, 3)
            for i in range(N):
                if i + 3 < N - DT:
                    merge_w_lo(k, g, dve, i + 3)
                if i == 3:
                    weigh(k, s, dve, 3, 0)
                    for p in range(4):
                        if p < 3:
                            weigh(k, s, dve, 3, p + 1)
                        dve.wait_ge(s.s_yh, 4 + p + 1)
                        V.tensor_tensor(s.ybl[:, p], s.yb[:, p], s.ybh[:, p].bitcast(F32), ALU.subtract)\
                            .then_inc(s.s_yl, 1)
                kind, n = items[i]
                if kind == "a":
                    dve.wait_ge(s_item, i + 1)
                    V.tensor_tensor(ta[:, n % 6], m.gates[:, n], k.bank[n % 4][:, :], ALU.mult).then_inc(s_ta, 1)
                elif kind == "b":
                    dve.wait_ge(s_item, i + 1)
                    V.tensor_tensor(tb[:, n % 2], m.gates[:, DT + n], k.bank[4 + n % 2][:, :], ALU.mult).then_inc(s_tb, 1)
                    dve.wait_ge(s_ta, n + 1)
                    dve.wait_ge(s_tb, n + 1)
                    V.tensor_tensor(mg[:, n % 2], ta[:, n % 6], tb[:, n % 2], ALU.add).then_inc(s_mg, 1)
                    dve.wait_ge(s_mh, n + 1)
                    V.tensor_tensor(ml[:, n], mg[:, n % 2], mh[:, n].bitcast(F32), ALU.subtract).then_inc(s_ml, 1)
                elif kind == "o":
                    if n == 0:
                        dve.wait_ge(s_h, 16)
                    dve.wait_ge(s_item, i + 1)
                    V.scalar_tensor_tensor(k.hT[:, n], k.bank[6 + n % 2][:, :], k.gate[:, 1, n:n + 1], k.hT[:, n],
                                           ALU.mult, ALU.add).then_inc(s_add, 1)
                    if n in (4, 5):
                        ffn_vector_gu_lo(k, f, dve, 0, n - 4)
                    if n >= 2:
                        norm_vector_sum(k, n3, dve, n - 1)
            norm_vector_sum(k, n3, dve, DT - 1)
            norm_vector_rstd(k, n3, dve)

        @block.tensor
        def _(pe):
            for i in range(N):
                kind, n = items[i]
                pe.wait_ge(s_lo, i + 1)
                w = [x[i % 4][:, 0:width[i]].rearrange("p (k c) -> p k c", c=P) for x in (g.wh, g.wl)]
                if kind == "o":
                    bank, xs = k.bank[6 + n % 2], (mh, ml)
                    if n >= 2:
                        pe.wait_ge(s_add, n - 1)
                elif kind == "a":
                    bank, xs = k.bank[n % 4], (s.yah, s.yal)
                    if n >= 4:
                        pe.wait_ge(s_ta, n - 3)
                else:
                    bank, xs = k.bank[4 + n % 2], (s.ybh, s.ybl)
                    if n >= 2:
                        pe.wait_ge(s_tb, n - 1)
                depth = width[i] // P
                for kt in range(depth):
                    if kind == "a" and n == 0:
                        pe.wait_ge(s.s_yl, kt + 1)
                    if kind == "b" and n == 0:
                        pe.wait_ge(s.s_yl, 4 + kt + 1)
                    if kind == "o" and n == 0:
                        pe.wait_ge(s_ml, kt + 1)
                    for j, (x, y) in enumerate(split_terms(w[0][:, kt], w[1][:, kt], xs[0][:, kt], xs[1][:, kt])):
                        mm = nc.tensor.matmul(bank[:, :], x, y, start=(kt == 0 and j == 0),
                                              stop=(kt == depth - 1 and j == 2))
                mm.then_inc(s_item, 1)
            norm_tensor_sums(k, n3, pe)
            norm_tensor_broadcast(k, n3, pe)


def ffn2_and_output(k, f, n):
    nc, a, X, K = k.nc, k.a, k.X, 1024
    e = norm_buffers(k, 4, X, X + 8 * K, X + 10 * K, banks=(0, 1))
    o = k.at("out_tiles", [P, DT, T], F32, X + 104 * K)
    s_y, s_out = k.sem("out_ready"), k.sem("out_stored")
    yT = a.out.rearrange("(t p) n -> t p n", p=P)
    last_add = 4 + 8 * (GROUPS - 1)
    with nc.Block() as block:
        @block.sync
        def _(sp):
            ffn_sync_gu(k, f, sp, 1)
            with sp.Fori(1, GROUPS - 1) as g:
                ffn_sync_gu(k, f, sp, g + 1)
                ffn_sync_dn(k, f, sp, g)
            ffn_sync_dn(k, f, sp, GROUPS - 1)
            for t in range(DT):
                sp.wait_ge(s_y, t + 1)
                sp.dma_start(yT[t], o[:, t]).then_inc(s_out, 16)
            sp.wait_ge(s_out, 16 * DT)

        @block.scalar
        def _(act):
            norm_scalar_modulate(k, n, act, k.gain[:, 2], k.mod[:, 48:56])
            load_table(k, act, ACT.Silu)
            ffn_scalar_group(k, f, act, 0, 0, first=True)
            with act.Fori(0, 4) as it:
                ffn_scalar_group(k, f, act, it * 2 + 1, 1)
                ffn_scalar_group(k, f, act, it * 2 + 2, 0)
            ffn_scalar_group(k, f, act, 9, 1)
            ffn_scalar_group(k, f, act, 10, 0, last=True)
            ffn_scalar_dn_hi(k, f, act, 10, last=True)
            norm_scalar_squares(k, e, act, f.s_bank, last_add)

        @block.vector
        def _(dve):
            norm_vector_modulate(k, n, dve)
            nc.vector.tensor_copy(k.stat[:, 0], k.stat[:, 1]).then_inc(f.s_bank, 4)
            for s in range(2):
                ffn_vector_hidden(k, f, dve, 0, 0, s, split_next=True)

            def group(g, q):
                ffn_vector_dn_lo(k, f, dve, g - 1)
                for s in range(2):
                    ffn_vector_hidden(k, f, dve, g, q, s, split_next=(s == 0))
                ffn_vector_down(k, f, dve, g - 1, k.gate[:, 2], range(4))
                ffn_vector_gu_lo(k, f, dve, g + 1, 1)
                ffn_vector_down(k, f, dve, g - 1, k.gate[:, 2], range(4, DT))
            with dve.Fori(0, 4) as it:
                group(it * 2 + 1, 1)
                group(it * 2 + 2, 0)
            group(9, 1)
            ffn_vector_dn_lo(k, f, dve, 9)
            for s in range(2):
                ffn_vector_hidden(k, f, dve, 10, 0, s, split_next=False)
            ffn_vector_down(k, f, dve, 9, k.gate[:, 2], range(4))
            ffn_vector_dn_lo(k, f, dve, 10, last=True)
            ffn_vector_down(k, f, dve, 9, k.gate[:, 2], range(4, DT))
            ffn_vector_down(k, f, dve, 10, k.gate[:, 2], norm=e)
            norm_vector_rstd(k, e, dve)
            dve.wait_ge(e.s_bc, 1)
            for t in range(DT):
                nc.vector.scalar_tensor_tensor(o[:, t], k.hT[:, t], k.vec[:, V_G + 24 + t:V_G + 25 + t], e.bc[:, :],
                                               ALU.mult, ALU.mult).then_inc(s_y, 1)

        @block.tensor
        def _(pe):
            ffn_tensor_first(k, f, pe, n.s_ul, FIRST_STEPS)

            def group(g, q):
                for s in range(2):
                    ffn_tensor_gate_up(k, f, pe, g, s)
                ffn_tensor_down(k, f, pe, g - 1, 1 - q)
            with pe.Fori(0, 4) as it:
                group(it * 2 + 1, 1)
                group(it * 2 + 2, 0)
            group(9, 1)
            group(10, 0)
            ffn_tensor_down(k, f, pe, 10, 0, last=True)
            norm_tensor_sums(k, e, pe)
            norm_tensor_broadcast(k, e, pe)


def _constants():
    const = np.zeros((P, C_END), np.float32)
    const[:, C_ID:C_ID + P] = np.eye(P, dtype=np.float32)
    i, j = np.arange(P)[:, None], np.arange(P)[None, :]
    for n, hidden in ((M_UP, j <= i), (M_U, j > i), (M_L, i > j), (M_LP, i <= j)):
        const[:, C_MSK + n * P:C_MSK + (n + 1) * P] = np.where(hidden, np.float32(MASKED), np.float32(0))
    t = np.arange(T)
    end = np.arange(NCP) * CMP_STRIDE + CMP_LEN - 1
    end[NC_BLOCKS:] = 2 * T
    hidden = (end[None, :] > t[:, None]).reshape(QT, P, NCP).transpose(1, 0, 2).reshape(P, QT * NCP)
    const[:, C_MCA:C_MCC] = np.where(hidden, np.float32(MASKED), np.float32(0))
    const[:NC_BLOCKS, C_MCC:] = np.where(end[:NC_BLOCKS, None] > t[None, :], np.float32(MASKED), np.float32(0))
    aug = np.zeros((AUG_ROWS, A_END), np.float32)
    aug[0, A_KPOS:A_KPOS + T] = t
    aug[0, A_CPOS:A_CPOS + NC_BLOCKS] = end[:NC_BLOCKS]
    for n, br in enumerate(BRANCHES):
        aug[ROW_M[br] - AUG0, A_IND + n] = 1.0
    aug[0, A_SLOPE:A_SLOPE + HEADS] = SLOPES
    rows = np.asarray(SLOPES, np.float32)[:, None] * t[None, :].astype(np.float32)
    cols = rows.reshape(HEADS, QT, P).transpose(2, 0, 1).reshape(P, HEADS * QT)
    return const, aug, rows, np.ascontiguousarray(cols)


def _tiles(w, per=P):
    kk, n = w.shape
    return np.ascontiguousarray(w.reshape(kk // P, P, n // per, per).transpose(2, 1, 0, 3))


def kernel(**inputs):
    import concourse.bacc as bacc
    from concourse.bass_utils import run_bass_kernel_spmd as run

    x = {n: np.asarray(v) for n, v in inputs.items()}
    cols = lambda v: v.reshape(-1, P).T
    w_in = x["w_in"][0]
    at = {"qn": 0, "kc": 512, "vc": 640, "ks": 768, "vs": 896, "kw": 1024, "vw": 1152, "gn": 1280, "qs": 1304,
          "kb": 1816, "vb": 1944, "gm": 2072}
    order = []
    for name in TILES_IN:
        if name == "gn":
            order.append(np.concatenate([at["gn"] + np.arange(24).reshape(HEADS, 3).T.reshape(-1),
                                         np.arange(P - 24)]))
        else:
            order.append(at[name[:2]] + P * int(name[2:] or 0) + np.arange(P))
    order += [at["gm"] + P * n + np.arange(P) for n in range(N_GATES)]
    chunk = lambda w: w[0].reshape(4, 4, 2 * DH, HID_C).transpose(0, 2, 1, 3)
    const, aug, rows, tcols = _constants()
    gu = lambda g, u: np.ascontiguousarray(np.stack([_tiles(x[g][0]), _tiles(x[u][0])], axis=2))
    arrays = dict(
        xT=x["x"][0].T,
        vec=np.concatenate([cols(x["b_ada"][0]), cols(x["g_ffn1"][0]), cols(x["g_mix"][0]), cols(x["g_ffn2"][0]),
                            cols(x["g_final"]), cols(x["c"][0])], axis=1),
        w_ada=x["w_ada"][0], gu1=gu("w1_gate", "w1_up"), dn1=x["w1_down"][0],
        gu2=gu("w2_gate", "w2_up"), dn2=x["w2_down"][0],
        win=_tiles(w_in[:, np.concatenate(order)]),
        cw1=np.concatenate([chunk(x["cmp_w1_k"]), chunk(x["cmp_w1_v"])]),
        cw2=np.stack([x[n][0].reshape(2, P, DH).transpose(1, 0, 2) for n in ("cmp_w2_k", "cmp_w2_v")], axis=1),
        cpos=np.stack([x[n][0].reshape(16, 2 * DH).T for n in ("cmp_pos_k", "cmp_pos_v")], axis=1),
        wup=np.stack([_tiles(x["w_up_a"][0]), _tiles(x["w_up_b"][0])], axis=2),
        wout=_tiles(x["w_out"][0]),
        sinks=x["sinks"].reshape(HEADS), const=const, aug=aug, slope_rows=rows, slope_cols=tcols)
    arrays = {n: np.ascontiguousarray(v) for n, v in arrays.items()}
    nc = bacc.Bacc("TRN2", target_bir_lowering=False, num_devices=1)
    a = Record()
    (a.xT, a.vec, a.w_ada, a.gu1, a.dn1, a.gu2, a.dn2, a.win, a.cw1, a.cw2, a.cpos, a.wup, a.wout, a.sinks, a.const, a.aug, a.slope_rows, a.slope_cols) = (
        nc.dram_tensor(f"in_{n}", v.shape, mybir.dt.from_np(v.dtype), kind="ExternalInput").ap()
        for n, v in arrays.items())
    a.out = nc.dram_tensor("out_T", (D, T), F32, kind="ExternalOutput").ap()
    build(nc, a)
    r = run(nc, [{f"in_{n}": v for n, v in arrays.items()}], core_ids=[0])
    return np.ascontiguousarray(r.results[0]["out_T"].T)[None]
```
